# Optimizing a Trainium2 kernel written in Bass

```python
import jax, jax.numpy as jnp
from jax import lax
import numpy as np
import math

D_MODEL = 1024
BATCH = 1
SEQ = 512
DEPTH = 1

CTX_LEN = 256
GRID_W = 64
RET_W = D_MODEL // 2
RET_HEADS = 4
RET_HEAD_DIM = RET_W // RET_HEADS
FOURIER_W = D_MODEL - RET_W
FOURIER_GROUPS = 4
FOURIER_GROUP_DIM = FOURIER_W // FOURIER_GROUPS
MIX_W = RET_W + FOURIER_W
IN_W = 4 * RET_W + FOURIER_W
D_FF = ((8 * D_MODEL // 3 + 127) // 128) * 128
CONV_WIDTH = 3
CHUNK = 128
ROPE_BASE = 10000.0
NORM_EPS = 1e-6
N_MOD = 6


def rms_norm(x, g):
    xf = x.astype(jnp.float32)
    xf = xf * lax.rsqrt(jnp.mean(xf * xf, axis=-1, keepdims=True) + NORM_EPS)
    return xf.astype(x.dtype) * g

def modulate(h, shift, scale):
    return h * (1 + scale) + shift

def adaln(cond, w, b):
    return jnp.split(jax.nn.silu(cond) @ w + b, N_MOD, axis=-1)

def split_heads(t):
    bsz, length, _ = t.shape
    return t.reshape(bsz, length, RET_HEADS, RET_HEAD_DIM).transpose(0, 2, 1, 3).astype(jnp.float32)

def axial_rope(length):
    t = jnp.arange(length)
    row = (t // GRID_W).astype(jnp.float32)
    col = (t % GRID_W).astype(jnp.float32)
    n_freq = RET_HEAD_DIM // 4
    freqs = ROPE_BASE ** (-jnp.arange(n_freq, dtype=jnp.float32) / n_freq)
    ang = jnp.concatenate([row[:, None] * freqs, col[:, None] * freqs], axis=-1)
    return jnp.cos(ang), jnp.sin(ang)

def apply_rope(t, cos, sin):
    half = RET_HEAD_DIM // 2
    t1, t2 = t[..., :half], t[..., half:]
    return jnp.concatenate([t1 * cos - t2 * sin, t1 * sin + t2 * cos], axis=-1)

def retention_scan(q, k, v, log_gamma, init_state, strict):
    bsz, heads, length, dk = q.shape
    dv = v.shape[-1]
    n_chunks = length // CHUNK
    pos = jnp.arange(CHUNK, dtype=jnp.float32)
    diff = pos[:, None] - pos[None, :]
    mask = diff > 0 if strict else diff >= 0
    dmask = jnp.where(mask[None], jnp.exp(jnp.where(mask, diff, 0.0)[None] * log_gamma[:, None, None]), 0.0)
    qc = q.reshape(bsz, heads, n_chunks, CHUNK, dk)
    kc = k.reshape(bsz, heads, n_chunks, CHUNK, dk)
    vc = v.reshape(bsz, heads, n_chunks, CHUNK, dv)
    scores = jnp.einsum('bhncd,bhnmd->bhncm', qc, kc) * dmask[:, None]
    intra = jnp.einsum('bhncm,bhnme->bhnce', scores, vc)
    zeta = jnp.exp((CHUNK - 1 - pos)[None, :] * log_gamma[:, None])
    xi = jnp.exp((pos + 1)[None, :] * log_gamma[:, None])
    kv = jnp.einsum('bhnmd,bhnme->nbhde', kc * zeta[None, :, None, :, None], vc)
    chunk_decay = jnp.exp(CHUNK * log_gamma)[None, :, None, None]

    def step(state, kv_i):
        return state * chunk_decay + kv_i, state

    _, prev = lax.scan(step, init_state, kv)
    cross = jnp.einsum('bhncd,nbhde->bhnce', qc * xi[None, :, None, :, None], prev)
    return (intra + cross).reshape(bsz, heads, length, dv)

def context_states(h_ctx, w_in, lg_f, lg_b):
    kv = h_ctx @ w_in[:, RET_W:3 * RET_W]
    k, v = jnp.split(kv, 2, axis=-1)
    k = split_heads(k) * RET_HEAD_DIM ** -0.5
    v = split_heads(v)
    length = k.shape[2]
    m = jnp.arange(length, dtype=jnp.float32)
    w_f = jnp.exp((length - 1 - m)[None, :] * lg_f[:, None])
    w_b = jnp.exp(m[None, :] * lg_b[:, None])
    s_f = jnp.einsum('bhld,hl,bhle->bhde', k, w_f, v)
    s_b = jnp.einsum('bhld,hl,bhle->bhde', k, w_b, v)
    return s_f, s_b

def fourier_mix(f):
    bsz, length, _ = f.shape
    fg = f.reshape(bsz, length, FOURIER_GROUPS, FOURIER_GROUP_DIM).astype(jnp.float32)
    out = jnp.fft.fft2(fg, axes=(1, 3), norm="ortho").real
    return out.reshape(bsz, length, FOURIER_W).astype(f.dtype)

def token_mixer(h, w_in, w_out, lg_f, lg_b, init_f, init_b, rope):
    proj = h @ w_in
    q, k, v, g, f = jnp.split(proj, [RET_W, 2 * RET_W, 3 * RET_W, 4 * RET_W], axis=-1)
    q = split_heads(q)
    k = split_heads(k) * RET_HEAD_DIM ** -0.5
    v = split_heads(v)
    if rope is not None:
        q = apply_rope(q, *rope)
        k = apply_rope(k, *rope)
    o_f = retention_scan(q, k, v, lg_f, init_f, strict=False)
    flip = lambda t: jnp.flip(t, axis=2)
    o_b = flip(retention_scan(flip(q), flip(k), flip(v), lg_b, init_b, strict=True))
    o = o_f + o_b
    o = o * lax.rsqrt(jnp.mean(o * o, axis=-1, keepdims=True) + NORM_EPS)
    bsz, length = h.shape[0], h.shape[1]
    o = o.transpose(0, 2, 1, 3).reshape(bsz, length, RET_W).astype(h.dtype)
    ret = o * jax.nn.silu(g)
    return jnp.concatenate([ret, fourier_mix(f)], axis=-1) @ w_out

def conv_ffn(h, w_up, conv_w, conv_b, w_down, rows):
    bsz, length, _ = h.shape
    u = (h @ w_up).reshape(bsz, rows, length // rows, 2 * D_FF)
    up = jnp.pad(u, ((0, 0), (0, 0), (1, 1), (0, 0)))
    u = up[:, :, :-2] * conv_w[0] + up[:, :, 1:-1] * conv_w[1] + up[:, :, 2:] * conv_w[2] + conv_b
    a, b = jnp.split(u.reshape(bsz, length, 2 * D_FF), 2, axis=-1)
    return (jax.nn.silu(a) * b) @ w_down

def first_inputs(seed: int = 0) -> dict:
    key = jax.random.key(seed)
    ks = jax.random.split(key, 20)
    nrm = lambda k, shape, s: jax.random.normal(k, shape, jnp.float32) * s
    base = 1.0 - 2.0 ** (-5.0 - jnp.arange(RET_HEADS, dtype=jnp.float32))
    logit = jnp.log(base / (1.0 - base))
    return {
        "x": nrm(ks[0], (BATCH, SEQ, D_MODEL), 1.0),
        "c": nrm(ks[1], (BATCH, D_MODEL), 1.0),
        "ctx": nrm(ks[2], (BATCH, CTX_LEN, D_MODEL), 1.0),
        "c_ctx": nrm(ks[3], (D_MODEL,), 1.0),
        "w_ada": nrm(ks[4], (DEPTH, D_MODEL, N_MOD * D_MODEL), D_MODEL ** -0.5),
        "b_ada": nrm(ks[5], (DEPTH, N_MOD * D_MODEL), 0.02),
        "g_mix_pre": 1.0 + nrm(ks[6], (DEPTH, D_MODEL), 0.05),
        "g_mix_post": 1.0 + nrm(ks[7], (DEPTH, D_MODEL), 0.05),
        "g_ffn_pre": 1.0 + nrm(ks[8], (DEPTH, D_MODEL), 0.05),
        "g_ffn_post": 1.0 + nrm(ks[9], (DEPTH, D_MODEL), 0.05),
        "w_in": nrm(ks[10], (DEPTH, D_MODEL, IN_W), D_MODEL ** -0.5),
        "ret_decay_fwd": logit[None] + nrm(ks[11], (DEPTH, RET_HEADS), 0.1),
        "ret_decay_bwd": logit[None] + nrm(ks[12], (DEPTH, RET_HEADS), 0.1),
        "w_out": nrm(ks[13], (DEPTH, MIX_W, D_MODEL), MIX_W ** -0.5),
        "w_up": nrm(ks[14], (DEPTH, D_MODEL, 2 * D_FF), D_MODEL ** -0.5),
        "conv_w": nrm(ks[15], (DEPTH, CONV_WIDTH, 2 * D_FF), CONV_WIDTH ** -0.5),
        "conv_b": nrm(ks[16], (DEPTH, 2 * D_FF), 0.02),
        "w_down": nrm(ks[17], (DEPTH, D_FF, D_MODEL), D_FF ** -0.5),
    }

def first_block(x, c, ctx, c_ctx, w_ada, b_ada, g_mix_pre, g_mix_post, g_ffn_pre, g_ffn_post,
              w_in, ret_decay_fwd, ret_decay_bwd, w_out, w_up, conv_w, conv_b, w_down):
    seq_len = x.shape[1]
    rows = seq_len // GRID_W
    rope = axial_rope(seq_len)
    ctx_s = ctx
    for layer in range(DEPTH):
        lg_f = jax.nn.log_sigmoid(ret_decay_fwd[layer].astype(jnp.float32))
        lg_b = jax.nn.log_sigmoid(ret_decay_bwd[layer].astype(jnp.float32))
        sh_a, sc_a, gt_a, sh_f, sc_f, gt_f = [m[:, None, :] for m in adaln(c, w_ada[layer], b_ada[layer])]
        csh_a, csc_a, cgt_a, csh_f, csc_f, cgt_f = adaln(c_ctx, w_ada[layer], b_ada[layer])
        h_ctx = modulate(rms_norm(ctx_s, g_mix_pre[layer]), csh_a, csc_a)
        s_f, s_b = context_states(h_ctx, w_in[layer], lg_f, lg_b)
        h_lat = modulate(rms_norm(x, g_mix_pre[layer]), sh_a, sc_a)
        mix = token_mixer(h_lat, w_in[layer], w_out[layer], lg_f, lg_b, s_f, s_b, rope)
        x = x + gt_a * rms_norm(mix, g_mix_post[layer])
        h_ffn = modulate(rms_norm(x, g_ffn_pre[layer]), sh_f, sc_f)
        ffn = conv_ffn(h_ffn, w_up[layer], conv_w[layer], conv_b[layer], w_down[layer], rows)
        x = x + gt_f * rms_norm(ffn, g_ffn_post[layer])
        if layer + 1 < DEPTH:
            zero = jnp.zeros_like(s_f)
            mix_c = token_mixer(h_ctx, w_in[layer], w_out[layer], lg_f, lg_b, zero, zero, None)
            ctx_s = ctx_s + cgt_a * rms_norm(mix_c, g_mix_post[layer])
            h_cffn = modulate(rms_norm(ctx_s, g_ffn_pre[layer]), csh_f, csc_f)
            ffn_c = conv_ffn(h_cffn, w_up[layer], conv_w[layer], conv_b[layer], w_down[layer], 1)
            ctx_s = ctx_s + cgt_f * rms_norm(ffn_c, g_ffn_post[layer])
    return x


CONV_WIDTH_2 = D_MODEL // 2
CONV_KERNEL = 31
N_HEADS = 8
HEAD_DIM = 64
ATT_WIDTH = N_HEADS * HEAD_DIM
N_BRANCH = 2
D_FF_2 = -(-8 * D_MODEL // (3 * 256)) * 256
IN_COLS = 2 * CONV_WIDTH_2 + 3 * ATT_WIDTH + N_BRANCH * D_MODEL
Q_BLOCK = 128
EPS = 1e-6


def rmsnorm(x, g):
    xf = x.astype(jnp.float32)
    y = xf * lax.rsqrt(jnp.mean(xf * xf, axis=-1, keepdims=True) + EPS)
    return (y * g.astype(jnp.float32)).astype(x.dtype)

def layernorm(x, g, b):
    xf = x.astype(jnp.float32)
    mu = jnp.mean(xf, axis=-1, keepdims=True)
    xc = xf - mu
    y = xc * lax.rsqrt(jnp.mean(xc * xc, axis=-1, keepdims=True) + EPS)
    return (y * g.astype(jnp.float32) + b.astype(jnp.float32)).astype(x.dtype)

def causal_depthwise_conv(u, w, b):
    ch = u.shape[-1]
    y = lax.conv_general_dilated(
        u, w[:, None, :].astype(u.dtype), window_strides=(1,), padding=[(CONV_KERNEL - 1, 0)],
        dimension_numbers=("NWC", "WIO", "NWC"), feature_group_count=ch)
    return y + b

def stick_breaking_attention(q, k, v):
    s_len = q.shape[1]
    scale = 1.0 / math.sqrt(q.shape[-1])
    qf = q.astype(jnp.float32) * scale
    kf = k.astype(jnp.float32)
    vf = v.astype(jnp.float32)
    outs = []
    for start in range(0, s_len, Q_BLOCK):
        end = start + Q_BLOCK
        z = jnp.einsum("bqhd,bkhd->bhqk", qf[:, start:end], kf[:, :end])
        t_idx = start + jnp.arange(Q_BLOCK)[:, None]
        s_idx = jnp.arange(end)[None, :]
        causal = s_idx < t_idx
        log_keep = jnp.where(causal, jax.nn.log_sigmoid(-z), 0.0)
        log_after = lax.cumsum(log_keep, axis=3, reverse=True) - log_keep
        a = jnp.where(causal, jnp.exp(jax.nn.log_sigmoid(z) + log_after), 0.0)
        outs.append(jnp.einsum("bhqk,bkhd->bqhd", a, vf[:, :end]))
    return jnp.concatenate(outs, axis=1).astype(q.dtype)

def hybrid_mixer(h, w_in, conv_w, conv_b, conv_ln_g, conv_ln_b, w_conv_out, w_att_out, w_o):
    b, s, _ = h.shape
    proj = h @ w_in
    glu_in, qkv, gates = jnp.split(proj, [2 * CONV_WIDTH_2, 2 * CONV_WIDTH_2 + 3 * ATT_WIDTH], axis=-1)
    u_val, u_gate = jnp.split(glu_in, 2, axis=-1)
    u = u_val * jax.nn.sigmoid(u_gate)
    u = causal_depthwise_conv(u, conv_w, conv_b)
    u = jax.nn.silu(layernorm(u, conv_ln_g, conv_ln_b))
    y_conv = u @ w_conv_out
    qkv = qkv.reshape(b, s, 3, N_HEADS, HEAD_DIM)
    o = stick_breaking_attention(qkv[:, :, 0], qkv[:, :, 1], qkv[:, :, 2])
    y_att = o.reshape(b, s, ATT_WIDTH) @ w_att_out
    g_conv, g_att = jnp.split(gates, 2, axis=-1)
    merged = jax.nn.sigmoid(g_conv) * y_conv + jax.nn.sigmoid(g_att) * y_att
    return merged @ w_o

def swiglu_ffn(h, w_ffn_in, w_ffn_out):
    gate, up = jnp.split(h @ w_ffn_in, 2, axis=-1)
    return (jax.nn.silu(gate) * up) @ w_ffn_out

def _normal(k, shape, scale):
    return jax.random.normal(k, shape, jnp.float32) * scale

def second_inputs(seed: int = 0) -> dict:
    key = jax.random.key(seed)
    ks = jax.random.split(key, 20)
    D = D_MODEL
    return {
        "x": _normal(ks[0], (BATCH, SEQ, D), 1.0),
        "c": _normal(ks[1], (BATCH, D), 1.0),
        "ada_w": _normal(ks[2], (DEPTH, D, 6 * D), D ** -0.5),
        "ada_b": _normal(ks[3], (DEPTH, 6 * D), 0.02),
        "pre_mix_g": 1.0 + _normal(ks[4], (DEPTH, D), 0.02),
        "post_mix_g": 1.0 + _normal(ks[5], (DEPTH, D), 0.02),
        "pre_ffn_g": 1.0 + _normal(ks[6], (DEPTH, D), 0.02),
        "post_ffn_g": 1.0 + _normal(ks[7], (DEPTH, D), 0.02),
        "w_in": _normal(ks[8], (DEPTH, D, IN_COLS), D ** -0.5),
        "conv_w": _normal(ks[9], (DEPTH, CONV_KERNEL, CONV_WIDTH_2), CONV_KERNEL ** -0.5),
        "conv_b": _normal(ks[10], (DEPTH, CONV_WIDTH_2), 0.02),
        "conv_ln_g": 1.0 + _normal(ks[11], (DEPTH, CONV_WIDTH_2), 0.02),
        "conv_ln_b": _normal(ks[12], (DEPTH, CONV_WIDTH_2), 0.02),
        "w_conv_out": _normal(ks[13], (DEPTH, CONV_WIDTH_2, D), CONV_WIDTH_2 ** -0.5),
        "w_att_out": _normal(ks[14], (DEPTH, ATT_WIDTH, D), ATT_WIDTH ** -0.5),
        "w_o": _normal(ks[15], (DEPTH, D, D), D ** -0.5),
        "w_ffn_in": _normal(ks[16], (DEPTH, D, 2 * D_FF_2), D ** -0.5),
        "w_ffn_out": _normal(ks[17], (DEPTH, D_FF_2, D), D_FF_2 ** -0.5),
    }

def second_block(x, c, ada_w, ada_b, pre_mix_g, post_mix_g, pre_ffn_g, post_ffn_g, w_in, conv_w, conv_b,
              conv_ln_g, conv_ln_b, w_conv_out, w_att_out, w_o, w_ffn_in, w_ffn_out):
    c_act = jax.nn.silu(c)
    for l in range(DEPTH):
        mod = c_act @ ada_w[l] + ada_b[l]
        sh1, sc1, ga1, sh2, sc2, ga2 = [m[:, None, :] for m in jnp.split(mod, 6, axis=-1)]
        h = rmsnorm(x, pre_mix_g[l]) * (1.0 + sc1) + sh1
        y = hybrid_mixer(h, w_in[l], conv_w[l], conv_b[l], conv_ln_g[l], conv_ln_b[l],
                         w_conv_out[l], w_att_out[l], w_o[l])
        x = x + ga1 * rmsnorm(y, post_mix_g[l])
        h = rmsnorm(x, pre_ffn_g[l]) * (1.0 + sc2) + sh2
        y = swiglu_ffn(h, w_ffn_in[l], w_ffn_out[l])
        x = x + ga2 * rmsnorm(y, post_ffn_g[l])
    return x


def setup_inputs(seed=0):
    out = dict(first_inputs(seed))
    for name, value in second_inputs(seed + 1).items():
        if name != "x":
            out[name + "_2"] = value
    return out


def reference(
    x, c, ctx, c_ctx, w_ada, b_ada, g_mix_pre, g_mix_post, g_ffn_pre, g_ffn_post, w_in,
    ret_decay_fwd, ret_decay_bwd, w_out, w_up, conv_w, conv_b, w_down, c_2, ada_w_2, ada_b_2,
    pre_mix_g_2, post_mix_g_2, pre_ffn_g_2, post_ffn_g_2, w_in_2, conv_w_2, conv_b_2,
    conv_ln_g_2, conv_ln_b_2, w_conv_out_2, w_att_out_2, w_o_2, w_ffn_in_2, w_ffn_out_2,
):
    x = first_block(
        x, c, ctx, c_ctx, w_ada, b_ada, g_mix_pre, g_mix_post, g_ffn_pre, g_ffn_post, w_in,
        ret_decay_fwd, ret_decay_bwd, w_out, w_up, conv_w, conv_b, w_down,
    )
    return second_block(
        x, c_2, ada_w_2, ada_b_2, pre_mix_g_2, post_mix_g_2, pre_ffn_g_2, post_ffn_g_2, w_in_2,
        conv_w_2, conv_b_2, conv_ln_g_2, conv_ln_b_2, w_conv_out_2, w_att_out_2, w_o_2,
        w_ffn_in_2, w_ffn_out_2,
    )


_drawn_inputs = setup_inputs


def setup_inputs(seed=0):
    import zlib

    import numpy as np

    out = dict(_drawn_inputs(seed))
    spreads = {}
    factors = {'conv_b': 5.012,
     'pre_mix_g_2': 5.974,
     'post_mix_g_2': 6.766,
     'pre_ffn_g_2': 16.84,
     'post_ffn_g_2': 29.122,
     'conv_b_2': 8.0,
     'conv_ln_g_2': 29.369,
     'conv_ln_b_2': 28.141}
    for name, (base, spread) in spreads.items():
        noise = np.random.default_rng([zlib.crc32(name.encode()), seed]).standard_normal(out[name].shape)
        drawn = base * np.exp(spread * noise) if base else spread * noise
        out[name] = __import__('jax').numpy.asarray(drawn.astype(out[name].dtype))
    for name, factor in factors.items():
        out[name] = (out[name] * factor).astype(out[name].dtype)
    return out
```

```python
from contextlib import ExitStack

import numpy as np
import concourse.bass as bass
from concourse import mybir

P = 128
D, L, LC = 1024, 512, 256
KT = D // P
TT, TC = L // P, LC // P
HEADS, HD = 4, 128
RET = HEADS * HD
GROUPS = 4
FF = ((8 * D // 3 + 127) // 128) * 128
FT = FF // P
ROW = 64
NH2, HD2 = 8, 64
CW = 512
CT = CW // P
TAPS = 31
EPS = 1e-6
CH = 2048
NEG = -1e30

C_KV, C_Q, C_F, C_DFT, C_G = 0, 4, 6, 8, 10
C_OUT = 12
C_UP = 16
C_DOWN = C_UP + FT
C_U = C_DOWN + 12
C_K2, C_V2, C_Q2, C_GATES = C_U + 4, C_U + 6, C_U + 8, C_U + 10
C_MERGE = C_GATES + 8
C_O = C_MERGE + 4
C_UP2 = C_O + 4
C_DOWN2 = C_UP2 + FT
N_CHUNKS = C_DOWN2 + 12
ADA_FIRST = 8
ADA_LATER = 40

VECS = [("c", KT), ("cc", KT), ("c2", KT), ("b_ada", 48), ("b_ada2", 48), ("g0", KT), ("p0", KT), ("g1", KT),
        ("p1", KT), ("g2", KT), ("p2", KT), ("g3", KT), ("p3", KT), ("cw", 3 * 2 * FT), ("cb", 2 * FT),
        ("cw2", TAPS * CT), ("cb2", CT), ("lng", CT), ("lnb", CT), ("dec", 2 * HEADS), ("mpos", 2 * TC)]
VAT = {}
_at = 0
for _n, _w in VECS:
    VAT[_n] = _at
    _at += _w
NV = _at
B_OUT, B_UP = 0, KT
B_DOWN = B_UP + 2 * FT
B_U = B_DOWN + KT
B_K2, B_V2, B_Q2, B_MERGE = B_U + 8, B_U + 12, B_U + 16, B_U + 20
B_O = B_MERGE + 16
B_UP2 = B_O + KT
B_DOWN2 = B_UP2 + 2 * FT
SP_AT = (0, P, 3 * P, 6 * P)
BAND = L + (TT - 1) * P


def build(nc, weights, ada, x_t, ctx_t, vecs, rope, band, pos, csd, masks, out):
    F, R = mybir.dt.float32, mybir.dt.float32r
    ALU, ACT = mybir.AluOpType, mybir.ActivationFunctionType
    mult, add, sub = ALU.mult, ALU.add, ALU.subtract
    stack = ExitStack()
    with stack:
        KB = 1024
        base = [(nc.sbuf_base + 31) // 32 * 32]

        def fix(name, shape, dt=F):
            size = int(np.prod(shape[1:])) * 4
            t = nc.alloc_sbuf_tensor_at(name, shape, dt, offset=base[0])
            base[0] += (size + 31) // 32 * 32
            return t

        def over(name, shape, at, dt=F):
            return nc.alloc_sbuf_tensor_at(name, shape, dt, offset=int(at))

        xT = fix("xT", [P, KT, L])
        H0 = base[0]
        hH, hL = fix("hH", [P, KT, L], R), fix("hL", [P, KT, L], R)
        raw = fix("raw", [P, 2, CH])
        WH, WL = fix("WH", [P, 2, CH], R), fix("WL", [P, 2, CH], R)
        ada_half = fix("ada_half", [P, CH // 2])
        vec = fix("vec", [P, NV])
        ones = fix("ones", [P, P])
        csil = fix("csil", [P, KT, 2])
        csil2 = fix("csil2", [P, KT])
        rstd = fix("rstd", [P, L])
        scratch = fix("scratch", [P, 2, L])
        ada_acc = fix("ada_acc", [P, 256])
        mod0 = fix("mod0", [P, 16, 2])
        mod = fix("mod", [P, 2 * ADA_LATER])
        gm = fix("gm", [P, 2, KT])
        gp = fix("gp", [P, KT])
        lg = fix("lg", [P, 3, 2 * HEADS])
        eps = fix("eps", [P, 1])
        zeta = fix("zeta", [P, 2, HEADS, TC])
        U = base[0]
        adaf = over("adaf", [P, ADA_FIRST, CH], U)
        kH, kL = over("kH", [P, HEADS, L], U, R), over("kL", [P, HEADS, L], U + 8 * KB, R)
        vH, vL = over("vH", [P, TT, RET], U + 16 * KB, R), over("vL", [P, TT, RET], U + 24 * KB, R)
        qH, qL = over("qH", [P, HEADS, L], U + 32 * KB, R), over("qL", [P, HEADS, L], U + 40 * KB, R)
        ktmp = over("ktmp", [P, 4, L], U + 32 * KB)
        kctmp = over("kctmp", [P, 2, 256], U + 40 * KB)
        sH, sL = over("sH", [P, 2, HEADS, P], U + 48 * KB, R), over("sL", [P, 2, HEADS, P], U + 52 * KB, R)
        hcH, hcL = over("hcH", [P, KT, LC], U + 56 * KB, R), over("hcL", [P, KT, LC], U + 64 * KB, R)
        qtmp = over("qtmp", [P, 4, L], U + 56 * KB)
        kcH, kcL = over("kcH", [P, TC, 2, 256], U + 72 * KB, R), over("kcL", [P, TC, 2, 256], U + 76 * KB, R)
        csd_in = over("csd_in", [P, 256], U + 72 * KB)
        ctxT = over("ctxT", [P, KT, LC], U + 76 * KB)
        vcH, vcL = over("vcH", [P, TC, 256], U + 80 * KB, R), over("vcL", [P, TC, 256], U + 82 * KB, R)
        ropeT = over("ropeT", [P, 2, L], U + 84 * KB)
        bandT = over("bandT", [P, BAND], U + 88 * KB)
        posT = over("posT", [P, L], U + 91.5 * KB)
        csdH, csdL = over("csdH", [P, 256], U + 93.5 * KB, R), over("csdL", [P, 256], U + 94.5 * KB, R)
        decay = over("decay", [P, BAND], U + 56 * KB)
        xi = over("xi", [P, 2, L], U + 59.5 * KB)
        aF = over("aF", [P, 2, L], U + 63.5 * KB)
        aH, aL = over("aH", [P, 2, L], U + 67.5 * KB, R), over("aL", [P, 2, L], U + 71.5 * KB, R)
        comb = over("comb", [P, L], U + 75.5 * KB)
        oT = over("oT", [P, HEADS, L], U + 77.5 * KB)
        fH, fL = over("fH", [P, GROUPS, L], U, R), over("fL", [P, GROUPS, L], U + 8 * KB, R)
        fcH, fcL = over("fcH", [P, 2, TT, 256], U + 16 * KB, R), over("fcL", [P, 2, TT, 256], U + 24 * KB, R)
        mixH, mixL = over("mixH", [P, KT, L], U + 32 * KB, R), over("mixL", [P, KT, L], U + 48 * KB, R)
        GH, GL = over("GH", [P, FT, L], U, R), over("GL", [P, FT, L], U + 44 * KB, R)
        tA, tB = over("tA", [P, 2, L], U + 88 * KB), over("tB", [P, 2, L], U + 92 * KB)
        yT = over("yT", [P, KT, L], H0)
        uT, cacc = over("uT", [P, CT, L], U), over("cacc", [P, CT, L], U + 8 * KB)
        q2H, q2L = over("q2H", [P, 4, L], U + 16 * KB, R), over("q2L", [P, 4, L], U + 24 * KB, R)
        k2H, k2L = over("k2H", [P, 4, L], U + 32 * KB, R), over("k2L", [P, 4, L], U + 40 * KB, R)
        v2H, v2L = over("v2H", [P, TT, CW], U + 48 * KB, R), over("v2L", [P, TT, CW], U + 56 * KB, R)
        gates = over("gates", [P, 16, L], U + 64 * KB)
        mgH, mgL = over("mgH", [P, KT, L], U + 64 * KB, R), over("mgL", [P, KT, L], U + 80 * KB, R)
        spH, spL = over("spH", [P, 1280], H0, R), over("spL", [P, 1280], H0 + 5 * KB, R)
        atH, atL = over("atH", [P, 2, L], H0 + 10 * KB, R), over("atL", [P, 2, L], H0 + 14 * KB, R)
        maskR = over("maskR", [P, 4, P], H0 + 18 * KB, R)
        sptmp = over("sptmp", [P, 2, L], H0 + 20 * KB)
        spF = over("spF", [P, 2, L], H0 + 24 * KB)
        atF = over("atF", [P, 2, L], H0 + 28 * KB)
        mask_in = over("mask_in", [P, 4, P], H0 + 28 * KB)
        cH, cL = over("cH", [P, CT, L], H0, R), over("cL", [P, CT, L], H0 + 8 * KB, R)
        assert U + 96 * KB <= nc.sbuf_usable_end, (U, nc.sbuf_usable_end)

        bank = [stack.enter_context(nc.psum_tensor(f"bank{i}", [P, 512], F)) for i in range(8)]
        sems = {}

        class Sems:
            def __getattr__(self, name):
                if name not in sems:
                    sems[name] = stack.enter_context(nc.semaphore(name))
                return sems[name]

        s = Sems()

        def v(name, i, n=1):
            return vec[:, VAT[name] + i:VAT[name] + i + n]

        def step(n, of):
            return 1 if n < of - 1 else 17 - of

        def done(c, n, of):
            return 16 * c + (n + 1 if n < of - 1 else 16)

        def dft_done(g):
            return 16 * C_DFT + g + 1 if g < GROUPS - 1 else 16 * (C_DFT + 2)

        block = stack.enter_context(nc.Block())

        class Chain:
            def __init__(self, eng, sem):
                self.eng, self.sem, self.n, self.extra = eng, sem, 0, None

            def link(self, ins):
                self.n += 1
                ins.then_inc(self.sem, 1)
                self.eng.wait_ge(self.sem, self.n if self.extra is None else self.extra + self.n)

            def enter(self, i, per):
                self.extra, self.start, self.per = i * per, self.n, per

            def leave(self, passes):
                assert self.n - self.start == self.per, self.n - self.start
                self.n, self.extra = self.start + passes * self.per, None

        @block.sync
        def _(sp):
            sp.dma_start(vec[:, :], vecs).then_inc(s.vec_in, 16)
            sp.dma_start(ctxT[:, :, :], ctx_t).then_inc(s.ctx_in, 16)
            for i in range(ADA_FIRST):
                sp.dma_start(adaf[:, i, :], ada[i]).then_inc(s.adaf_in, 16)
                if i == 1:
                    for j in range(2):
                        half = slice(j * KT // 2, (j + 1) * KT // 2)
                        sp.dma_start(xT[:, half, :], x_t[:, half, :]).then_inc(s.x_in, 16)
            sp.dma_start(csd_in[:, :], csd).then_inc(s.csd_in, 16)
            for j in range(2):
                sp.dma_start(raw[:, j, :], weights[j]).then_inc([s.raw0_in, s.raw1_in][j], 16)
            sp.dma_start(ropeT[:, :, :], rope).then_inc(s.rope_in, 16)
            sp.dma_start(bandT[:, :], band).then_inc(s.band_in, 16)
            sp.dma_start(posT[:, :], pos).then_inc(s.pos_in, 16)

            def load_pair(i):
                for j in range(2):
                    sp.wait_ge(s.lo_done, 2 * i + j - 1)
                    sp.dma_start(raw[:, j, :], weights[2 * i + j]).then_inc([s.raw0_in, s.raw1_in][j], 16)

            with sp.Fori(1, N_CHUNKS // 2) as i:
                load_pair(i)
            sp.wait_ge(s.out_done, 16 * KT)

        @block.gpsimd
        def _(pool):
            nc.gpsimd.memset(eps[:, :], EPS).then_inc(s.eps_ready, 1)
            nc.gpsimd.memset(ones[:, :], 1.0).then_inc(s.ones_ready, 1)
            pool.wait_ge(s.adaf_in, 16 * ADA_FIRST)
            pool.dma_start(ada_half[:, :], ada[ADA_FIRST, :, 0:CH // 2]).then_inc(s.ada_in, 16)
            pool.wait_ge(s.ada_read, 1)
            pool.dma_start(ada_half[:, :], ada[ADA_FIRST, :, CH // 2:CH]).then_inc(s.ada_in, 16)
            with pool.Fori(1, ADA_LATER) as i:
                for j in range(2):
                    pool.wait_ge(s.ada_read, 2 * i + j)
                    pool.dma_start(ada_half[:, :], ada[i + ADA_FIRST, :, j * (CH // 2):(j + 1) * (CH // 2)])\
                        .then_inc(s.ada_in, 16)
            pool.wait_ge(s.mm_done, 16 * C_MERGE)
            pool.dma_start(mask_in[:, :, :], masks).then_inc(s.mask_in, 16)
            for k in range(KT):
                pool.wait_ge(s.x_new, 3 * KT + k + 1)
                pool.dma_start(out[:, k, :], xT[:, k, :]).then_inc(s.out_done, 16)
            pool.wait_ge(s.out_done, 16 * KT)

        @block.scalar
        def _(act):
            A = nc.scalar.activation
            own = Chain(act, s.act_own)

            def split_hi(c, slot, first=False):
                act.wait_ge([s.raw0_in, s.raw1_in][slot], c * 8 + 16 - 8 * slot)
                if not first:
                    act.wait_ge(s.mm_done, 16 * c - 16)
                A(WH[:, slot, :], raw[:, slot, :], ACT.Copy).then_inc(s.hi_done, 1)

            def norm_hi(m, src, hi, n, width, ready, done, shift, gain):
                for k in range(n):
                    t = src[:, k % 2, 0:width]
                    act.wait_ge(ready, m * n + k + 1)
                    own.link(A(t, t, ACT.Identity, bias=shift(k), scale=gain(k)))
                    A(hi[:, k, :], t, ACT.Copy).then_inc(done, 1)

            act.wait_ge(s.vec_in, 16)
            A(csil[:, :, 0], v("c", 0, KT), ACT.Silu).then_inc(s.csil_ready, 1)
            A(csil[:, :, 1], v("cc", 0, KT), ACT.Silu).then_inc(s.csil_ready, 1)
            A(csil2[:, :], v("c2", 0, KT), ACT.Silu).then_inc(s.csil_ready, 1)
            act.wait_ge(s.ctx_in, 16)
            for k in range(KT):
                if k >= 2:
                    act.wait_ge(s.csq_used, k - 1)
                A(scratch[:, k % 2, 0:LC], ctxT[:, k, :], ACT.Square).then_inc(s.csq_ready, 1)

            def squares_of_x(m):
                for k in range(KT):
                    if m == 0:
                        act.wait_ge(s.x_in, 32)
                        if k < 2:
                            act.wait_ge(s.csq_used, KT)
                    else:
                        act.wait_ge(s.x_new, (m - 1) * KT + k + 1)
                        if k < 2:
                            act.wait_ge(s.ysq_used, m * KT)
                    if k >= 2:
                        act.wait_ge(s.xsq_used, m * KT + k - 1)
                    A(scratch[:, k % 2, :], xT[:, k, :], ACT.Square).then_inc(s.xsq_ready, 1)

            squares_of_x(0)
            act.wait_ge(s.csq_used, KT)
            act.wait_ge(s.eps_ready, 1)
            A(rstd[:, 0:LC], bank[6][:, 0:LC], ACT.Sqrt, bias=eps[:, :], scale=1.0 / D).then_inc(s.croot_ready, 1)
            act.wait_ge(s.lg_abs, 1)
            own.link(A(lg[:, 1, :], lg[:, 1, :], ACT.Exp))
            A(lg[:, 1, :], lg[:, 1, :], ACT.Ln, bias=1.0).then_inc(s.lg_ln, 1)
            act.wait_ge(s.lg_ready, 1)
            for d in range(2):
                for h in range(HEADS):
                    A(zeta[:, d, h, :], v("mpos", d * TC, TC), ACT.Exp,
                      scale=lg[:, 0, d * HEADS + h:d * HEADS + h + 1]).then_inc(s.zeta_exp, 1)
            act.wait_ge(s.csd_in, 16)
            A(csdH[:, :], csd_in[:, :], ACT.Copy).then_inc(s.csd_hi, 1)
            split_hi(0, 0, True)
            act.wait_ge(s.mod0_ready, 2)
            norm_hi(0, scratch, hcH, KT, LC, s.cnorm_mul, s.hc_hi, lambda k: mod0[:, k, 1:2], lambda k: gm[:, 1, k:k + 1])
            act.wait_ge(s.cnorm_mul, KT)
            act.wait_ge(s.xsq_used, KT)
            A(rstd[:, :], bank[5][:, :], ACT.Sqrt, bias=eps[:, :], scale=1.0 / D).then_inc(s.xroot_ready, 1)
            norm_hi(0, scratch, hH, KT, L, s.norm_mul, s.h_hi, lambda k: mod0[:, k, 0:1], lambda k: gm[:, 0, k:k + 1])

            def rope_tile(i, tmp, pb, dst, head, done, swapped, summed, hi):
                act.wait_ge(s.mm_done, done)
                if i >= 2:
                    act.wait_ge(summed, i - 1)
                A(tmp[0:64, i % 2, :], pb[64:128, :], ACT.Copy)
                A(tmp[64:128, i % 2, :], pb[0:64, :], ACT.Copy).then_inc(swapped, 1)
                act.wait_ge(summed, i + 1)
                A(dst[:, head, :], tmp[:, 2 + i % 2, :], ACT.Copy).then_inc(hi, 1)

            def states_hi(p):
                act.wait_ge(s.state_done, p + 1)
                A(sH[:, :, 2 * p:2 * p + 2, :],
                  bank[3][:, :].rearrange("p (d h e) -> p d h e", d=2, h=2), ACT.Copy).then_inc(s.state_hi, 1)

            for p in range(2):
                split_hi(2 * p + 1, 1, p == 0)
                for n in range(2):
                    rope_tile(2 * p + n, ktmp, bank[n], kH, 2 * p + n, done(2 * p, n, 4), s.k_swap, s.k_sum, s.k_hi)
                if p:
                    states_hi(p - 1)
                for tt in range(TC):
                    act.wait_ge(s.kc_scaled, 2 * p + tt + 1)
                    if p:
                        act.wait_ge(s.state_done, p)
                    A(kcH[:, tt, :, :], kctmp[:, :, :], ACT.Copy).then_inc(s.kc_hi, 1)
                split_hi(2 * p + 2, 0)
                for n in range(2):
                    act.wait_ge(s.mm_done, done(2 * p + 1, n, 3))
                    A(vH[:, 2 * n:2 * n + 2, 256 * p:256 * p + 256],
                      bank[n][:, :].rearrange("p (t e) -> p t e", t=2), ACT.Copy).then_inc(s.v_hi, 1)
                act.wait_ge(s.mm_done, done(2 * p + 1, 2, 3))
                A(vcH[:, :, :], bank[2][:, :].rearrange("p (t e) -> p t e", t=2), ACT.Copy).then_inc(s.vc_hi, 1)
            for p in range(2):
                split_hi(C_Q + p + 1, 1 - p)
                for n in range(2):
                    rope_tile(2 * p + n, qtmp, bank[n], qH, 2 * p + n, done(C_Q + p, n, 2), s.q_swap, s.q_sum, s.q_hi)
                if p == 0:
                    states_hi(1)
            for h in range(HEADS):
                act.wait_ge(s.decay_arg, h + 1)
                A(decay[:, :], decay[:, :], ACT.Exp).then_inc(s.decay_ready, 1)
                if h:
                    act.wait_ge(s.cross_read, h)
                A(xi[:, 0, :], posT[:, :], ACT.Exp, scale=lg[:, 0, h:h + 1]).then_inc(s.xi_ready, 1)
                A(xi[:, 1, :], posT[:, :], ACT.Exp, scale=lg[:, 1, HEADS + h:HEADS + h + 1],
                  bias=lg[:, 2, HEADS + h:HEADS + h + 1]).then_inc(s.xi_ready, 1)
                for j in range(TT):
                    i = TT * h + j
                    act.wait_ge(s.a_mul, i + 1)
                    if i >= 2:
                        act.wait_ge(s.pv_done, i - 1)
                    A(aH[:, i % 2, :], aF[:, i % 2, :], ACT.Copy).then_inc(s.a_hi, 1)
                act.wait_ge(s.o_sum, h + 1)
                A(scratch[:, 1, :], oT[:, h, :], ACT.Square).then_inc(s.osq_ready, 1)
                act.wait_ge(s.ostat_done, h + 1)
                A(scratch[:, 0, :], bank[1][:, :], ACT.Sqrt, bias=eps[:, :], scale=1.0 / HD).then_inc(s.oroot_ready, 1)
            for p in range(2):
                split_hi(C_F + p + 1, 1 - p)
                for n in range(2):
                    i = 2 * p + n
                    act.wait_ge(s.mm_done, done(C_F + p, n, 2))
                    A(fH[:, i, :], bank[n][:, :], ACT.Copy).then_inc(s.f_hi, 1)
            split_hi(C_DFT + 1, 1)
            for g in range(GROUPS + 1):
                for n in range(2):
                    i = 2 * g + n
                    if g == GROUPS:
                        break
                    act.wait_ge(s.fc_done, i + 1)
                    if g >= 2:
                        act.wait_ge(s.mm_done, dft_done(g - 2))
                    A(fcH[:, g % 2, 2 * n:2 * n + 2, :], bank[n][:, :].rearrange("p (t e) -> p t e", t=2),
                      ACT.Copy).then_inc(s.fc_hi, 1)
                if g:
                    act.wait_ge(s.mm_done, dft_done(g - 1))
                    A(mixH[:, 3 + g, :], bank[4 + (g - 1) % 2][:, :], ACT.Copy).then_inc(s.mix_hi, 1)
            split_hi(C_G, 0)
            for p in range(2):
                split_hi(C_G + p + 1, 1 - p)
                for n in range(2):
                    i = 2 * p + n
                    act.wait_ge(s.mm_done, done(C_G + p, n, 2))
                    if i >= 2:
                        act.wait_ge(s.mix_lo, GROUPS + i - 1)
                    A(scratch[:, i % 2, :], bank[n][:, :], ACT.Silu).then_inc(s.g_silu, 1)
                    act.wait_ge(s.g_mul, i + 1)
                    A(mixH[:, i, :], scratch[:, i % 2, :], ACT.Copy).then_inc(s.mix_hi, 1)

            def out_squares(m, n, done_at):
                act.wait_ge(s.mm_done, done_at)
                if n >= 2:
                    act.wait_ge(s.ysq_used, m * KT + n - 1)
                elif m == 0:
                    act.wait_ge(s.mix_lo, KT)
                elif m == 2:
                    act.wait_ge(s.mg_lo, KT)
                A(scratch[:, n % 2, :], bank[n % 4][:, :], ACT.Square).then_inc(s.ysq_ready, 1)

            def out_root(m):
                act.wait_ge(s.ysq_used, (m + 1) * KT)
                A(rstd[:, :], bank[4][:, :], ACT.Sqrt, bias=eps[:, :], scale=1.0 / D).then_inc(s.root_ready, 1)

            def out_norm_square(m, c0):
                for p in range(4):
                    split_hi(c0 + p + 1, (p + 1) % 2)
                    for n in range(2):
                        out_squares(m, 2 * p + n, done(c0 + p, n, 2))
                out_root(m)

            def down_square(m, c0, last):
                for p in range(4):
                    for j in range(3):
                        if not (last and p == 3 and j == 2):
                            split_hi(c0 + 3 * p + j + 1, (3 * p + j + 1) % 2)
                    for n in range(2):
                        out_squares(m, 2 * p + n, done(c0 + 3 * p + 2, n, 2))
                out_root(m)

            def shift_gain(m):
                at = {1: 8, 2: 32, 3: 56}[m]
                return lambda k: mod[:, at + k:at + k + 1], lambda k: gm[:, 0, k:k + 1]

            def x_root(m):
                act.wait_ge(s.xsq_used, (m + 1) * KT)
                if m:
                    act.wait_ge(s.x_new, m * KT)
                A(rstd[:, :], bank[5][:, :], ACT.Sqrt, bias=eps[:, :], scale=1.0 / D).then_inc(s.xroot_ready, 1)

            def next_norm(m):
                squares_of_x(m)
                x_root(m)
                act.wait_ge(s.gm_ready, m)
                norm_hi(m, scratch, hH, KT, L, s.norm_mul, s.h_hi, *shift_gain(m))

            out_norm_square(0, C_OUT)
            next_norm(1)
            with act.Fori(0, FT // 2) as i:
                for j in range(2):
                    split_hi(2 * i + (C_UP + j + 1), 1 - j)
                    for x, tmp in enumerate((tA, tB)):
                        act.wait_ge(s.mm_done, 32 * i + done(C_UP + j, x, 2))
                        w = VAT["cw"] + 2 * FT + x * FT + j
                        b = VAT["cb"] + x * FT + j
                        A(tmp[:, j, :], bank[2 * j + x][:, :], ACT.Identity, bias=vec[:, bass.ds(2 * i + b, 1)],
                          scale=vec[:, bass.ds(2 * i + w, 1)]).then_inc(s.conv_mid, 1)
                    act.wait_ge(s.bank_free, 4 * i + (B_UP + 2 * j + 1))
                    A(tA[:, j, :], tA[:, j, :], ACT.Silu).then_inc(s.ffn_silu, 1)
                    act.wait_ge(s.ffn_mul, 2 * i + j + 1)
                    A(GH[:, bass.ds(2 * i + j, 1), :], tB[:, j:j + 1, :], ACT.Copy).then_inc(s.ffn_hi, 1)
            down_square(1, C_DOWN, False)
            next_norm(2)
            for i in range(4):
                split_hi(C_U + i + 1, (i + 1) % 2)
                act.wait_ge(s.mm_done, done(C_U + i, 1, 2))
                if i >= 2:
                    act.wait_ge(s.bank_free, B_U + 2 * (i - 1))
                else:
                    act.wait_ge(s.h_lo, 3 * KT)
                A(scratch[:, i % 2, :], bank[2 * (i % 2) + 1][:, :], ACT.Sigmoid).then_inc(s.u_sig, 1)
            for c0, ready in ((C_K2, s.k2_hi), (C_V2, s.v2_hi), (C_Q2, s.q2_hi)):
                for i in range(4):
                    c, n = c0 + i // 2, i % 2
                    if n == 0:
                        split_hi(c + 1, (c + 1) % 2)
                    act.wait_ge(s.mm_done, done(c, n, 2))
                    if c0 == C_K2:
                        A(k2H[:, i, :], bank[i][:, :], ACT.Copy).then_inc(ready, 1)
                    elif c0 == C_V2:
                        A(v2H[:, 2 * n:2 * n + 2, 256 * (i // 2):256 * (i // 2) + 256],
                          bank[i][:, :].rearrange("p (t e) -> p t e", t=2), ACT.Copy).then_inc(ready, 1)
                    else:
                        A(q2H[:, i, :], bank[i][:, :], ACT.Copy, scale=HD2 ** -0.5).then_inc(ready, 1)
            for p in range(8):
                split_hi(C_GATES + p + 1, (p + 1) % 2)
                for n in range(2):
                    i = 2 * p + n
                    act.wait_ge(s.mm_done, done(C_GATES + p, n, 2))
                    A(gates[:, i, :], bank[i % 4][:, :], ACT.Sigmoid).then_inc(s.gate_sig, 1)
            act.wait_ge(s.mask_in, 16)
            A(maskR[:, :, :], mask_in[:, :, :], ACT.Copy).then_inc(s.mask_ready, 1)

            def attn_exp(i):
                w = P * (i % 4 + 1)
                act.wait_ge(s.arg_done, i + 1)
                if i == 0:
                    act.wait_ge(s.mask_ready, 1)
                if i >= 2:
                    act.wait_ge(s.at_lo, i - 1)
                A(atF[:, i % 2, 0:w], bank[i % 4][:, 0:w], ACT.Exp).then_inc(s.at_exp, 1)
                act.wait_ge(s.at_exp, i + 1)
                if i >= 2:
                    act.wait_ge(s.pv2_done, i - 1)
                A(atH[:, i % 2, 0:w], atF[:, i % 2, 0:w], ACT.Copy).then_inc(s.at_hi, 1)

            for i in range(4 * NH2 + 5):
                if i < 4 * NH2:
                    w = P * (i % 4 + 1)
                    act.wait_ge(s.z_done, i + 1)
                    if i >= 2:
                        act.wait_ge(s.sp_sum, i - 1)
                    own.link(A(sptmp[:, i % 2, 0:w], bank[i % 4][:, 0:w], ACT.Abs))
                    own.link(A(sptmp[:, i % 2, 0:w], sptmp[:, i % 2, 0:w], ACT.Exp, scale=-1.0))
                    A(sptmp[:, i % 2, 0:w], sptmp[:, i % 2, 0:w], ACT.Ln, bias=1.0).then_inc(s.sp_ln, 1)
                if 0 <= i - 3 < 4 * NH2:
                    attn_exp(i - 3)
                if i >= 8 and i % 4 == 0:
                    h = (i - 8) // 4
                    r = 64 * (h % 2)
                    act.wait_ge(s.pv2_done, 4 * h + 4)
                    A(q2H[r:r + 64, h // 2, :], bank[4 + h % 2][r:r + 64, :], ACT.Copy).then_inc(s.o2_hi, 1)
            for k in range(CT):
                act.wait_ge(s.ln_center, k + 1)
                if k >= 2:
                    act.wait_ge(s.lnsq_used, k - 1)
                A(scratch[:, k % 2, :], cacc[:, k, :], ACT.Square).then_inc(s.lnsq_ready, 1)
            act.wait_ge(s.lnvar_done, 1)
            A(rstd[:, :], bank[5][:, :], ACT.Sqrt, bias=eps[:, :], scale=1.0 / CW).then_inc(s.lnroot_ready, 1)
            for k in range(CT):
                act.wait_ge(s.ln_mul, k + 1)
                own.link(A(cacc[:, k, :], cacc[:, k, :], ACT.Silu, scale=v("lng", k), bias=v("lnb", k)))
                A(cH[:, k, :], cacc[:, k, :], ACT.Copy).then_inc(s.c_hi, 1)
            for p in range(4):
                split_hi(C_MERGE + p + 1, (p + 1) % 2)
                for n in (2 * p, 2 * p + 1):
                    act.wait_ge(s.mg_sum, n + 1)
                    A(mgH[:, n, :], scratch[:, 0, :], ACT.Copy).then_inc(s.mg_hi, 1)
            out_norm_square(2, C_O)
            next_norm(3)
            with act.Fori(0, FT // 2) as i:
                for j in range(2):
                    split_hi(2 * i + (C_UP2 + j + 1), 1 - j)
                    act.wait_ge(s.mm_done, 32 * i + done(C_UP2 + j, 0, 2))
                    A(tA[:, j, :], bank[2 * j][:, :], ACT.Silu).then_inc(s.ffn2_silu, 1)
                    act.wait_ge(s.bank_free, 4 * i + (B_UP2 + 2 * j + 2))
                    A(GH[:, bass.ds(2 * i + j, 1), :], tB[:, j:j + 1, :], ACT.Copy).then_inc(s.ffn2_hi, 1)
            down_square(3, C_DOWN2, True)

        @block.vector
        def _(dve):
            V = nc.vector
            TT_, TS, STT = V.tensor_tensor, V.tensor_scalar, V.scalar_tensor_tensor
            own = Chain(dve, s.dve_own)

            def split_lo(c, slot):
                dve.wait_ge(s.hi_done, c + 1)
                TT_(WL[:, slot, :], raw[:, slot, :], WH[:, slot, :], sub).then_inc(s.lo_done, 1)

            def ada_job(a, c_col, first=False):
                if not first:
                    dve.wait_ge(s.ada_summed, a)
                for half in range(2):
                    dve.wait_ge(s.ada_in, 32 * a + 16 * (half + 1))
                    for k in range(4):
                        w = ada_half[:, 256 * k:256 * k + 256]
                        if half == k == 0:
                            ins = TS(ada_acc[:, :], w, c_col(0), None, mult)
                        else:
                            ins = STT(ada_acc[:, :], w, c_col(4 * half + k), ada_acc[:, :], mult, add)
                        if k < 3:
                            own.link(ins)
                        else:
                            ins.then_inc(s.ada_read, 1)
                            dve.wait_ge(s.ada_read, 2 * a + (half + 1))

            ada_next = [0]

            def ada_now():
                a = ada_next[0]
                ada_next[0] += 1
                ada_job(a, (lambda k: csil[:, k, 0:1]) if a < 16 else (lambda k: csil2[:, k:k + 1]), a == 0)

            def norm_lo(m, src, width, hi, lo, mul_s, hi_s, lo_s):
                for k in range(KT + 1):
                    if k < KT:
                        if k >= 2:
                            dve.wait_ge(lo_s, m * KT + k - 1)
                        TT_(scratch[:, k % 2, 0:width], src[:, k, :], rstd[:, 0:width], mult).then_inc(mul_s, 1)
                    if k:
                        dve.wait_ge(hi_s, m * KT + k)
                        TT_(lo[:, k - 1, :], scratch[:, (k - 1) % 2, 0:width], hi[:, k - 1, :], sub).then_inc(lo_s, 1)

            dve.wait_ge(s.vec_in, 16)
            dec = v("dec", 0, 2 * HEADS)
            STT(lg[:, 1, :], dec, -1.0, dec, mult, ALU.min).then_inc(s.lg_abs, 1)
            own.link(TS(lg[:, 0, :], dec, 0.0, None, ALU.min))
            dve.wait_ge(s.lg_ln, 1)
            own.link(TT_(lg[:, 0, :], lg[:, 0, :], lg[:, 1, :], sub))
            TS(lg[:, 1, :], lg[:, 0, :], -1.0, None, mult)
            TS(lg[:, 2, :], lg[:, 0, :], float(L + 1), None, mult).then_inc(s.lg_ready, 1)
            dve.wait_ge(s.zeta_exp, 2 * HEADS)
            own.link(TS(zeta[:, :, :, :], zeta[:, :, :, :], HD ** -0.5, None, mult))
            dve.wait_ge(s.csd_hi, 1)
            TT_(csdL[:, :], csd_in[:, :], csdH[:, :], sub).then_inc(s.csd_lo, 1)
            split_lo(0, 0)
            dve.wait_ge(s.mod0_done, 1)
            for j in range(2):
                b3 = bank[3][:, 0:32].rearrange("p (n j) -> p n j", j=2)
                own.link(TT_(mod0[:, :, j], b3[:, :, j], v("b_ada", 0, 16), add))
                STT(gm[:, j, :], mod0[:, 8:16, j], 1.0, v("g0", 0, KT), add, mult).then_inc(s.mod0_ready, 1)
            dve.wait_ge(s.croot_ready, 1)
            own.link(V.reciprocal(rstd[:, 0:LC], rstd[:, 0:LC]))
            dve.wait_ge(s.xsq_used, KT)
            norm_lo(0, ctxT, LC, hcH, hcL, s.cnorm_mul, s.hc_hi, s.hc_lo)
            dve.wait_ge(s.xroot_ready, 1)
            own.link(V.reciprocal(rstd[:, :], rstd[:, :]))
            norm_lo(0, xT, L, hH, hL, s.norm_mul, s.h_hi, s.h_lo)

            def rope_tile(i, tmp, pb, hi, lo, head, done_at, swapped, summed, hi_s, lo_s):
                dve.wait_ge(s.mm_done, done_at)
                if i == 0:
                    dve.wait_ge(s.rope_in, 16)
                dve.wait_ge(swapped, i + 1)
                TT_(tmp[:, 2 + i % 2, :], pb[:, :], ropeT[:, 0, :], mult)
                own.link(TT_(tmp[:, i % 2, :], tmp[:, i % 2, :], ropeT[:, 1, :], mult))
                TT_(tmp[:, 2 + i % 2, :], tmp[:, 2 + i % 2, :], tmp[:, i % 2, :], add).then_inc(summed, 1)
                dve.wait_ge(hi_s, i + 1)
                TT_(lo[:, head, :], tmp[:, 2 + i % 2, :], hi[:, head, :], sub).then_inc(lo_s, 1)

            def states_lo(p):
                dve.wait_ge(s.state_hi, p + 1)
                TT_(sL[:, :, 2 * p:2 * p + 2, :], bank[3][:, :].rearrange("p (d h e) -> p d h e", d=2, h=2),
                    sH[:, :, 2 * p:2 * p + 2, :], sub).then_inc(s.state_lo, 1)

            for p in range(2):
                split_lo(2 * p + 1, 1)
                for n in range(2):
                    rope_tile(2 * p + n, ktmp, bank[n], kH, kL, 2 * p + n, done(2 * p, n, 4), s.k_swap, s.k_sum,
                              s.k_hi, s.k_lo)
                if p:
                    states_lo(p - 1)
                for tt in range(TC):
                    dve.wait_ge(s.mm_done, done(2 * p, 2 + tt, 4))
                    if 2 * p + tt:
                        dve.wait_ge(s.kc_lo, 2 * p + tt)
                    for d in range(2):
                        for h in range(2):
                            ins = TS(kctmp[:, d, P * h:P * h + P], bank[2 + tt][:, P * h:P * h + P],
                                     zeta[:, d, 2 * p + h, tt:tt + 1], None, mult)
                    ins.then_inc(s.kc_scaled, 1)
                    dve.wait_ge(s.kc_hi, 2 * p + tt + 1)
                    TT_(kcL[:, tt, :, :], kctmp[:, :, :], kcH[:, tt, :, :], sub).then_inc(s.kc_lo, 1)
                ada_now()
                split_lo(2 * p + 2, 0)
                for n in range(2):
                    dve.wait_ge(s.v_hi, 2 * p + n + 1)
                    TT_(vL[:, 2 * n:2 * n + 2, 256 * p:256 * p + 256],
                        bank[n][:, :].rearrange("p (t e) -> p t e", t=2),
                        vH[:, 2 * n:2 * n + 2, 256 * p:256 * p + 256], sub).then_inc(s.v_lo, 1)
                dve.wait_ge(s.vc_hi, p + 1)
                TT_(vcL[:, :, :], bank[2][:, :].rearrange("p (t e) -> p t e", t=2), vcH[:, :, :], sub)\
                    .then_inc(s.vc_lo, 1)
                ada_now()
            for p in range(2):
                split_lo(C_Q + p + 1, 1 - p)
                for n in range(2):
                    rope_tile(2 * p + n, qtmp, bank[n], qH, qL, 2 * p + n, done(C_Q + p, n, 2), s.q_swap, s.q_sum,
                              s.q_hi, s.q_lo)
                if p == 0:
                    states_lo(1)
                ada_now()
            dve.wait_ge(s.band_in, 16)
            for h in range(HEADS):
                own.link(TS(decay[:, :], bandT[:, :], lg[:, 1, HEADS + h:HEADS + h + 1], None, mult))
                STT(decay[:, :], bandT[:, :], lg[:, 0, h:h + 1], decay[:, :], mult, ALU.min).then_inc(s.decay_arg, 1)
                dve.wait_ge(s.decay_ready, h + 1)
                for j in range(TT + 1):
                    i = TT * h + j
                    if j < TT:
                        dve.wait_ge(s.s_done, i + 1)
                        if i >= 2:
                            dve.wait_ge(s.a_lo, i - 1)
                        at = (TT - 1 - j) * P
                        STT(aF[:, i % 2, :], bank[4 + i % 2][:, :], HD ** -0.5, decay[:, at:at + L], mult, mult)\
                            .then_inc(s.a_mul, 1)
                    if j:
                        dve.wait_ge(s.a_hi, i)
                        TT_(aL[:, (i - 1) % 2, :], aF[:, (i - 1) % 2, :], aH[:, (i - 1) % 2, :], sub)\
                            .then_inc(s.a_lo, 1)
                dve.wait_ge(s.cross_done, h + 1)
                dve.wait_ge(s.xi_ready, 2 * h + 2)
                TT_(comb[:, :], bank[2][:, :], xi[:, 0, :], mult)
                TT_(scratch[:, 0, :], bank[3][:, :], xi[:, 1, :], mult).then_inc(s.cross_read, 1)
                dve.wait_ge(s.cross_read, h + 1)
                own.link(TT_(comb[:, :], comb[:, :], scratch[:, 0, :], add))
                dve.wait_ge(s.pv_done, TT * h + TT)
                TT_(oT[:, h, :], bank[6 if h % 2 == 0 else 0][:, :], comb[:, :], add).then_inc(s.o_sum, 1)
                dve.wait_ge(s.oroot_ready, h + 1)
                own.link(V.reciprocal(scratch[:, 0, :], scratch[:, 0, :]))
                TT_(oT[:, h, :], oT[:, h, :], scratch[:, 0, :], mult).then_inc(s.o_norm, 1)
                ada_now()
            for p in range(2):
                split_lo(C_F + p + 1, 1 - p)
                for n in range(2):
                    i = 2 * p + n
                    dve.wait_ge(s.f_hi, i + 1)
                    TT_(fL[:, i, :], bank[n][:, :], fH[:, i, :], sub).then_inc(s.f_lo, 1)
                ada_now()
            split_lo(C_DFT + 1, 1)
            for g in range(GROUPS + 1):
                for n in range(2):
                    i = 2 * g + n
                    if g == GROUPS:
                        break
                    dve.wait_ge(s.fc_hi, i + 1)
                    TT_(fcL[:, g % 2, 2 * n:2 * n + 2, :], bank[n][:, :].rearrange("p (t e) -> p t e", t=2),
                        fcH[:, g % 2, 2 * n:2 * n + 2, :], sub).then_inc(s.fc_lo, 1)
                if g:
                    dve.wait_ge(s.mix_hi, g)
                    TT_(mixL[:, 3 + g, :], bank[4 + (g - 1) % 2][:, :], mixH[:, 3 + g, :], sub).then_inc(s.mix_lo, 1)
            split_lo(C_G, 0)
            for p in range(2):
                split_lo(C_G + p + 1, 1 - p)
                for n in range(2):
                    i = 2 * p + n
                    dve.wait_ge(s.g_silu, i + 1)
                    TT_(scratch[:, i % 2, :], oT[:, i, :], scratch[:, i % 2, :], mult).then_inc(s.g_mul, 1)
                    dve.wait_ge(s.mix_hi, GROUPS + i + 1)
                    TT_(mixL[:, i, :], scratch[:, i % 2, :], mixH[:, i, :], sub).then_inc(s.mix_lo, 1)
                ada_now()

            SCALE_AT, GATE_AT = {1: 16, 2: 40, 3: 64}, {0: 0, 1: 24, 2: 48, 3: 72}

            def post_gain(m):
                at = GATE_AT[m]
                own.link(TT_(gp[:, :], mod[:, at:at + KT], v(f"p{m}", 0, KT), mult))

            def out_tile(m, n):
                dve.wait_ge(s.ysq_ready, m * KT + n + 1)
                TS(yT[:, n, :], bank[n % 4][:, :], gp[:, n:n + 1], None, mult).then_inc(s.bank_free, 1)

            def add_and_norm(m, free0):
                dve.wait_ge(s.root_ready, m + 1)
                own.link(V.reciprocal(rstd[:, :], rstd[:, :]))
                dve.wait_ge(s.bank_free, free0 + KT)
                for k in range(KT):
                    own.link(TT_(yT[:, k, :], yT[:, k, :], rstd[:, :], mult))
                    TT_(xT[:, k, :], xT[:, k, :], yT[:, k, :], add).then_inc(s.x_new, 1)
                if m == 3:
                    return
                at = SCALE_AT[m + 1]
                STT(gm[:, 0, :], mod[:, at:at + KT], 1.0, v(f"g{m + 1}", 0, KT), add, mult).then_inc(s.gm_ready, 1)
                dve.wait_ge(s.xroot_ready, m + 2)
                own.link(V.reciprocal(rstd[:, :], rstd[:, :]))
                norm_lo(m + 1, xT, L, hH, hL, s.norm_mul, s.h_hi, s.h_lo)

            def out_phase(m, c0, free0, jobs=0):
                post_gain(m)
                for p in range(4):
                    split_lo(c0 + p + 1, (p + 1) % 2)
                    for _ in range(jobs):
                        ada_now()
                    out_tile(m, 2 * p)
                    out_tile(m, 2 * p + 1)
                add_and_norm(m, free0)

            def down_phase(m, c0, free0, last):
                post_gain(m)
                for p in range(4):
                    for j in range(3):
                        if not (last and p == 3 and j == 2):
                            split_lo(c0 + 3 * p + j + 1, (3 * p + j + 1) % 2)
                    out_tile(m, 2 * p)
                    out_tile(m, 2 * p + 1)
                add_and_norm(m, free0)

            dve.wait_ge(s.ada_summed, 14)
            own.link(TT_(mod[:, 0:24], bank[7][:, 0:24], v("b_ada", 16, 24), add))
            out_phase(0, C_OUT, B_OUT, 1)
            assert ada_next[0] == 18, ada_next
            with dve.Fori(0, FT // 2) as i:
                own.enter(i, 2 * (4 - 2 + 6) + 2 * 0)
                for j in range(2):
                    split_lo(2 * i + (C_UP + j + 1), 1 - j)
                    views = []
                    for x, tmp in enumerate((tA, tB)):
                        views.append((tmp[:, j, :].rearrange("p (r c) -> p r c", c=ROW),
                                      bank[2 * j + x][:, :].rearrange("p (r c) -> p r c", c=ROW),
                                      VAT["cw"] + x * FT + j))
                    for x, (t, b, w) in enumerate(views):
                        dve.wait_ge(s.conv_mid, 4 * i + (2 * j + x + 1))
                        own.link(STT(t[:, :, 1:ROW], b[:, :, 0:ROW - 1], vec[:, bass.ds(2 * i + w, 1)],
                                     t[:, :, 1:ROW], mult, add))
                    for x, (t, b, w) in enumerate(views):
                        STT(t[:, :, 0:ROW - 1], b[:, :, 1:ROW], vec[:, bass.ds(2 * i + w + 4 * FT, 1)],
                            t[:, :, 0:ROW - 1], mult, add).then_inc(s.bank_free, 1)
                    ada_job(2 * i + (18 + j), lambda k: csil2[:, k:k + 1])
                    dve.wait_ge(s.bank_free, 4 * i + (B_UP + 2 * j + 2))
                    dve.wait_ge(s.ffn_silu, 2 * i + (j + 1))
                    TT_(tB[:, j, :], tA[:, j, :], tB[:, j, :], mult).then_inc(s.ffn_mul, 1)
                    dve.wait_ge(s.ffn_hi, 2 * i + (j + 1))
                    TT_(GL[:, bass.ds(2 * i + j, 1), :], tB[:, j:j + 1, :], GH[:, bass.ds(2 * i + j, 1), :], sub)\
                        .then_inc(s.ffn_lo, 1)
            own.leave(FT // 2)
            dve.wait_ge(s.ada_summed, ADA_LATER)
            TT_(mod[:, 24:32], bank[7][:, 24:32], v("b_ada", 40, 8), add)
            own.link(TT_(mod[:, 32:80], bank[7][:, 32:80], v("b_ada2", 0, 48), add))
            down_phase(1, C_DOWN, B_DOWN, False)

            for i in range(4):
                split_lo(C_U + i + 1, (i + 1) % 2)
                dve.wait_ge(s.u_sig, i + 1)
                TT_(uT[:, i, :], bank[2 * (i % 2)][:, :], scratch[:, i % 2, :], mult).then_inc(s.bank_free, 2)

            conv_n = [0]

            def conv_taps(count):
                for _ in range(count):
                    o = conv_n[0]
                    if o == TAPS * CT:
                        return
                    conv_n[0] += 1
                    shift, k = divmod(o, CT)
                    w = v("cw2", (TAPS - 1 - shift) * CT + k)
                    if shift == 0:
                        dve.wait_ge(s.bank_free, B_K2)
                        TS(cacc[:, k, :], uT[:, k, :], w, v("cb2", k), mult, add).then_inc(s.conv_tap, 1)
                    else:
                        dve.wait_ge(s.conv_tap, o - 3)
                        STT(cacc[:, k, shift:L], uT[:, k, 0:L - shift], w, cacc[:, k, shift:L], mult, add)\
                            .then_inc(s.conv_tap, 1)

            for c0, ready in ((C_K2, s.k2_hi), (C_V2, s.v2_hi), (C_Q2, s.q2_hi)):
                for i in range(4):
                    c, n = c0 + i // 2, i % 2
                    if n == 0:
                        split_lo(c + 1, (c + 1) % 2)
                        conv_taps(9)
                    dve.wait_ge(ready, i + 1)
                    if c0 == C_K2:
                        ins = TT_(k2L[:, i, :], bank[i][:, :], k2H[:, i, :], sub)
                    elif c0 == C_V2:
                        at = slice(256 * (i // 2), 256 * (i // 2) + 256)
                        ins = TT_(v2L[:, 2 * n:2 * n + 2, at], bank[i][:, :].rearrange("p (t e) -> p t e", t=2),
                                  v2H[:, 2 * n:2 * n + 2, at], sub)
                    else:
                        ins = STT(q2L[:, i, :], bank[i][:, :], HD2 ** -0.5, q2H[:, i, :], mult, sub)
                    ins.then_inc(s.bank_free, 1)
            for p in range(8):
                split_lo(C_GATES + p + 1, (p + 1) % 2)
                conv_taps(9)
            for i in range(4 * NH2 + 5):
                if 0 <= i - 1 < 4 * NH2:
                    k = i - 1
                    w = P * (k % 4 + 1)
                    dve.wait_ge(s.sp_ln, k + 1)
                    if k >= 2:
                        dve.wait_ge(s.sp_lo, k - 1)
                    STT(spF[:, k % 2, 0:w], bank[k % 4][:, 0:w], 0.0, sptmp[:, k % 2, 0:w], ALU.max, add)\
                        .then_inc(s.sp_sum, 1)
                    at = SP_AT[k % 4]
                    dve.wait_ge(s.sp_sum, k + 1)
                    if k >= 4:
                        dve.wait_ge(s.arg_done, k - k % 4)
                    V.tensor_copy(spH[:, at:at + w], spF[:, k % 2, 0:w]).then_inc(s.sp_hi, 1)
                    dve.wait_ge(s.sp_hi, k + 1)
                    TT_(spL[:, at:at + w], spF[:, k % 2, 0:w], spH[:, at:at + w], sub).then_inc(s.sp_lo, 1)
                if 0 <= i - 4 < 4 * NH2:
                    k = i - 4
                    w = P * (k % 4 + 1)
                    dve.wait_ge(s.at_hi, k + 1)
                    TT_(atL[:, k % 2, 0:w], atF[:, k % 2, 0:w], atH[:, k % 2, 0:w], sub).then_inc(s.at_lo, 1)
                if i >= 8 and i % 4 == 0:
                    h = (i - 8) // 4
                    r = 64 * (h % 2)
                    dve.wait_ge(s.o2_hi, h + 1)
                    TT_(q2L[r:r + 64, h // 2, :], bank[4 + h % 2][r:r + 64, :], q2H[r:r + 64, h // 2, :], sub)\
                        .then_inc(s.o2_lo, 1)
            dve.wait_ge(s.lnsum_done, 1)
            own.link(TS(rstd[:, :], bank[6][:, :], 1.0 / CW, None, mult))
            for k in range(CT):
                TT_(cacc[:, k, :], cacc[:, k, :], rstd[:, :], sub).then_inc(s.ln_center, 1)
            dve.wait_ge(s.lnroot_ready, 1)
            own.link(V.reciprocal(rstd[:, :], rstd[:, :]))
            for k in range(CT):
                TT_(cacc[:, k, :], cacc[:, k, :], rstd[:, :], mult).then_inc(s.ln_mul, 1)
            for k in range(CT):
                dve.wait_ge(s.c_hi, k + 1)
                TT_(cL[:, k, :], cacc[:, k, :], cH[:, k, :], sub).then_inc(s.c_lo, 1)
            for p in range(4):
                split_lo(C_MERGE + p + 1, (p + 1) % 2)
                for x in range(2):
                    n = 2 * p + x
                    dve.wait_ge(s.mm_done, done(C_MERGE + p, x, 2))
                    if n:
                        dve.wait_ge(s.mg_lo, n)
                    TT_(scratch[:, 0, :], gates[:, n, :], bank[2 * x][:, :], mult)
                    TT_(scratch[:, 1, :], gates[:, 8 + n, :], bank[2 * x + 1][:, :], mult).then_inc(s.bank_free, 2)
                    dve.wait_ge(s.bank_free, B_MERGE + 2 * (n + 1))
                    TT_(scratch[:, 0, :], scratch[:, 0, :], scratch[:, 1, :], add).then_inc(s.mg_sum, 1)
                    dve.wait_ge(s.mg_hi, n + 1)
                    TT_(mgL[:, n, :], scratch[:, 0, :], mgH[:, n, :], sub).then_inc(s.mg_lo, 1)
            out_phase(2, C_O, B_O)
            with dve.Fori(0, FT // 2) as i:
                for j in range(2):
                    split_lo(2 * i + (C_UP2 + j + 1), 1 - j)
                    dve.wait_ge(s.ffn2_silu, 2 * i + (j + 1))
                    dve.wait_ge(s.mm_done, 32 * i + done(C_UP2 + j, 1, 2))
                    TT_(tB[:, j, :], tA[:, j, :], bank[2 * j + 1][:, :], mult).then_inc(s.bank_free, 2)
                    dve.wait_ge(s.ffn2_hi, 2 * i + (j + 1))
                    TT_(GL[:, bass.ds(2 * i + j, 1), :], tB[:, j:j + 1, :], GH[:, bass.ds(2 * i + j, 1), :], sub)\
                        .then_inc(s.ffn2_lo, 1)
            down_phase(3, C_DOWN2, B_DOWN2, True)

        @block.tensor
        def _(pe):
            mm = nc.tensor.matmul

            def mm3(o, lh, ll, rh, rl, start, stop, skip=False):
                mm(o, lh, rh, start=start, stop=False, skip_group_check=skip)
                mm(o, lh, rl, start=False, stop=False, skip_group_check=skip)
                return mm(o, ll, rh, start=False, stop=stop, skip_group_check=skip)

            def have(c):
                pe.wait_ge(s.lo_done, c + 1)

            def wblock(slot, k, a, b):
                return WH[:, slot, 256 * k + a:256 * k + b], WL[:, slot, 256 * k + a:256 * k + b]

            def project(o, slot, n, src_h, src_l, ks, start=True, stop=True, ready=None):
                for x, (kb, k) in enumerate(ks):
                    if ready is not None:
                        pe.wait_ge(ready[0], ready[1] + k + 1)
                    wh, wl = wblock(slot, kb, P * n, P * n + P)
                    ins = mm3(o, wh, wl, src_h[:, k, :], src_l[:, k, :], start and x == 0, stop and x == len(ks) - 1)
                return ins

            ALL = [(k, k) for k in range(KT)]
            ada_next = [0]

            def ada_sum(a, col):
                pe.wait_ge(s.ada_read, 2 * a + 2)
                for j in range(2):
                    ins = mm(bank[7][:, col(j)], ada_acc[:, P * j:P * j + P], ones[:, 0:1], start=True, stop=True,
                             skip_group_check=True)
                ins.then_inc(s.ada_summed, 1)

            def ada_now():
                a = ada_next[0]
                ada_next[0] += 1
                ada_sum(a, lambda j: slice(2 * a + j, 2 * a + j + 1))

            def stat(b, src, width, ready, count, done_s, n, of, final):
                pe.wait_ge(ready, count)
                ins = mm(bank[b][:, 0:width], ones[:, :], src, start=(n == 0), stop=(n == of - 1))
                ins.then_inc(final if n == of - 1 and final is not None else done_s, 1)

            pe.wait_ge(s.ones_ready, 1)
            for k in range(KT):
                stat(6, scratch[:, k % 2, 0:LC], LC, s.csq_ready, k + 1, s.csq_used, k, KT, None)
            pe.wait_ge(s.csil_ready, 2)
            pe.wait_ge(s.adaf_in, 16 * ADA_FIRST)
            for c in range(ADA_FIRST):
                for j in range(2):
                    for k in range(KT):
                        ins = mm(bank[3][:, 4 * c + 2 * j:4 * c + 2 * j + 2],
                                 adaf[:, c, 256 * k + P * j:256 * k + P * j + P], csil[:, k, :],
                                 start=(k == 0), stop=(k == KT - 1), skip_group_check=True)
            ins.then_inc(s.mod0_done, 1)
            for k in range(KT):
                stat(5, scratch[:, k % 2, :], L, s.xsq_ready, k + 1, s.xsq_used, k, KT, None)

            have(0)
            for p in range(2):
                slot, c = 0, 2 * p
                have(c)
                for n in range(2):
                    if p:
                        pe.wait_ge(s.v_lo, n + 1)
                    project(bank[n][:, :], slot, n, hH, hL, ALL, ready=(s.h_lo, 0))\
                        .then_inc(s.mm_done, step(n, 4))

                def states(q):
                    pe.wait_ge(s.kc_lo, 2 * q + 2)
                    pe.wait_ge(s.vc_lo, q + 1)
                    for d in range(2):
                        for h in range(2):
                            at = slice(P * (2 * d + h), P * (2 * d + h) + P)
                            hs = slice(P * h, P * h + P)
                            for tt in range(TC):
                                ins = mm3(bank[3][:, at], kcH[:, tt, d, hs], kcL[:, tt, d, hs], vcH[:, tt, hs],
                                          vcL[:, tt, hs], tt == 0, tt == TC - 1, True)
                    ins.then_inc(s.state_done, 1)

                if p:
                    states(0)
                for tt in range(TC):
                    if p and tt == 0:
                        pe.wait_ge(s.vc_lo, 1)
                    if p and tt == 1:
                        pe.wait_ge(s.state_lo, 1)
                    if p == 0 and tt == 1:
                        pe.wait_ge(s.mod0_ready, 2)
                    for k in range(KT):
                        pe.wait_ge(s.hc_lo, k + 1)
                        wh, wl = wblock(slot, k, 0, 256)
                        ts = slice(P * tt, P * tt + P)
                        ins = mm3(bank[2 + tt][:, 0:256], hcH[:, k, ts], hcL[:, k, ts], wh, wl, k == 0, k == KT - 1)
                    ins.then_inc(s.mm_done, step(2 + tt, 4))
                ada_now()
                slot, c = 1, 2 * p + 1
                have(c)
                for b in range(3):
                    if b < 2:
                        pe.wait_ge(s.k_sum, 2 * p + b + 1)
                    else:
                        pe.wait_ge(s.kc_lo, 2 * p + 1)
                    for half in range(2):
                        hh, hl = (hH, hL) if b < 2 else (hcH, hcL)
                        tt = 2 * b + half if b < 2 else half
                        for k in range(KT):
                            wh, wl = wblock(slot, k, 0, 256)
                            ts = slice(P * tt, P * tt + P)
                            ins = mm3(bank[b][:, 256 * half:256 * half + 256], hh[:, k, ts], hl[:, k, ts], wh, wl,
                                      k == 0, k == KT - 1)
                    ins.then_inc(s.mm_done, step(b, 3))
                ada_now()
            for p in range(2):
                have(C_Q + p)
                for n in range(2):
                    if p:
                        pe.wait_ge(s.q_sum, n + 1)
                    else:
                        pe.wait_ge(s.v_lo, 3 + n)
                    project(bank[n][:, :], p, n, hH, hL, ALL).then_inc(s.mm_done, step(n, 2))
                if p == 0:
                    pe.wait_ge(s.kc_lo, 4)
                    states(1)
                ada_now()
            pe.wait_ge(s.q_lo, 4)
            pe.wait_ge(s.state_lo, 2)
            for i in range(TT * HEADS + 2):
                if i < TT * HEADS:
                    h, j = divmod(i, TT)
                    if i >= 2:
                        pe.wait_ge(s.a_mul, i - 1)
                    ks = slice(P * j, P * j + P)
                    mm3(bank[4 + i % 2][:, :], kH[:, h, ks], kL[:, h, ks], qH[:, h, :], qL[:, h, :], True, True)\
                        .then_inc(s.s_done, 1)
                if i >= 2:
                    h, j = divmod(i - 2, TT)
                    pe.wait_ge(s.a_lo, i - 1)
                    if j == 0 and h >= 2:
                        pe.wait_ge(s.o_sum, h - 1)
                    hs = slice(P * h, P * h + P)
                    mm3(bank[6 if h % 2 == 0 else 0][:, :], vH[:, j, hs], vL[:, j, hs], aH[:, (i - 2) % 2, :],
                        aL[:, (i - 2) % 2, :], j == 0, j == TT - 1).then_inc(s.pv_done, 1)
                    if j == TT - 1:
                        pe.wait_ge(s.osq_ready, h + 1)
                        mm(bank[1][:, :], ones[:, :], scratch[:, 1, :], start=True, stop=True).then_inc(s.ostat_done, 1)
                        ada_now()
                if i < TT * HEADS and i % TT == 3:
                    h = i // TT
                    if h:
                        pe.wait_ge(s.cross_read, h)
                    for d in range(2):
                        ins = mm3(bank[2 + d][:, :], sH[:, d, h, :], sL[:, d, h, :], qH[:, h, :], qL[:, h, :],
                                  True, True)
                    ins.then_inc(s.cross_done, 1)
            for p in range(2):
                have(C_F + p)
                for n in range(2):
                    if p:
                        pe.wait_ge(s.f_lo, n + 1)
                    else:
                        pe.wait_ge(s.o_norm, HEADS)
                    project(bank[n][:, :], p, n, hH, hL, ALL).then_inc(s.mm_done, step(n, 2))
                ada_now()
            have(C_DFT + 1)
            pe.wait_ge(s.csd_lo, 1)
            pe.wait_ge(s.f_lo, GROUPS)
            for g in range(GROUPS + 1):
                if g < GROUPS:
                    for n in range(2):
                        if g:
                            pe.wait_ge(s.fc_lo, 2 * (g - 1) + n + 1)
                        for half in range(2):
                            ts = slice(P * (2 * n + half), P * (2 * n + half) + P)
                            ins = mm3(bank[n][:, 256 * half:256 * half + 256], fH[:, g, ts], fL[:, g, ts],
                                      csdH[:, :], csdL[:, :], True, True)
                        ins.then_inc(s.fc_done, 1)
                if g:
                    q = g - 1
                    pe.wait_ge(s.fc_lo, 2 * g)
                    if q >= 2:
                        pe.wait_ge(s.mix_lo, q - 1)
                    for part in range(2):
                        for st in range(TT):
                            es = slice(P * part, P * part + P)
                            ss = slice(L * st, L * st + L)
                            ins = mm3(bank[4 + q % 2][:, :], fcH[:, q % 2, st, es], fcL[:, q % 2, st, es],
                                      WH[:, part, ss], WL[:, part, ss], part == st == 0,
                                      part == 1 and st == TT - 1)
                        if q == GROUPS - 1:
                            ins.then_inc(s.mm_done, 17 - GROUPS if part == 0 else 16)
                        elif part:
                            ins.then_inc(s.mm_done, 1)
            for p in range(2):
                have(C_G + p)
                for n in range(2):
                    if p:
                        pe.wait_ge(s.g_silu, n + 1)
                    else:
                        pe.wait_ge(s.fc_lo, 2 * GROUPS)
                    project(bank[n][:, :], p, n, hH, hL, ALL).then_inc(s.mm_done, step(n, 2))
                ada_now()

            def out_stat(m, n):
                pe.wait_ge(s.ysq_ready, m * KT + n + 1)
                mm(bank[4][:, :], ones[:, :], scratch[:, n % 2, :], start=(n == 0), stop=(n == KT - 1))\
                    .then_inc(s.ysq_used, 1)

            def x_stats(m):
                for k in range(KT):
                    pe.wait_ge(s.xsq_ready, m * KT + k + 1)
                    mm(bank[5][:, :], ones[:, :], scratch[:, k % 2, :], start=(k == 0), stop=(k == KT - 1))\
                        .then_inc(s.xsq_used, 1)

            def free(t):
                pe.wait_ge(s.bank_free, t - 3)

            def out_phase(m, c0, free0, src_h, src_l, ready, jobs=0):
                for p in range(4):
                    have(c0 + p)
                    for n in range(2):
                        t = 2 * p + n
                        if free0 + t >= 4:
                            free(free0 + t)
                        else:
                            pe.wait_ge(s.g_silu, 4)
                        project(bank[t % 4][:, :], p % 2, n, src_h, src_l, ALL, ready=ready)\
                            .then_inc(s.mm_done, step(n, 2))
                        if t:
                            out_stat(m, t - 1)
                    for _ in range(jobs):
                        ada_now()
                out_stat(m, KT - 1)
                if m < 3:
                    x_stats(m + 1)

            def down_phase(m, c0, free0, ready):
                for p in range(4):
                    for j in range(3):
                        c = c0 + 3 * p + j
                        have(c)
                        ks = [(k, 8 * j + k) for k in range(min(8, FT - 8 * j))]
                        for n in range(2):
                            t = 2 * p + n
                            if j == 0:
                                free(free0 + t)
                            ins = project(bank[t % 4][:, :], c % 2, n, GH, GL, ks, j == 0, j == 2,
                                          ready=(ready, 0) if p == 0 and n == 0 else None)
                            if j == 2:
                                ins.then_inc(s.mm_done, step(n, 2))
                            elif n == 1:
                                ins.then_inc(s.mm_done, 16)
                            if j == 0 and t >= 2:
                                out_stat(m, t - 2)
                out_stat(m, KT - 2)
                out_stat(m, KT - 1)
                if m < 3:
                    x_stats(m + 1)

            pe.wait_ge(s.mix_lo, KT)
            out_phase(0, C_OUT, B_OUT, mixH, mixL, None, 1)
            with pe.Fori(0, FT // 2) as i:
                for j in range(2):
                    have(2 * i + (C_UP + j))
                    for x in range(2):
                        pe.wait_ge(s.bank_free, 4 * i + (B_UP + 2 * j + x - 3))
                        if j == 0 and x == 0:
                            project(bank[0][:, :], 0, 0, hH, hL, ALL, ready=(s.h_lo, KT)).then_inc(s.mm_done, 1)
                        else:
                            project(bank[2 * j + x][:, :], j, x, hH, hL, ALL).then_inc(s.mm_done, step(x, 2))
                    ada_sum(2 * i + (18 + j), lambda jj: bass.ds(4 * i + (36 + 2 * j + jj), 1))
            down_phase(1, C_DOWN, B_DOWN, s.ffn_lo)
            for i in range(4):
                have(C_U + i)
                for x in range(2):
                    free(B_U + 2 * i + x)
                    project(bank[2 * (i % 2) + x][:, :], i % 2, x, hH, hL, ALL,
                            ready=(s.h_lo, 2 * KT) if i == x == 0 else None).then_inc(s.mm_done, step(x, 2))
            for c0, free0 in ((C_K2, B_K2), (C_V2, B_V2), (C_Q2, B_Q2)):
                for i in range(4):
                    c, n = c0 + i // 2, i % 2
                    if n == 0:
                        have(c)
                    free(free0 + i)
                    if c0 == C_V2:
                        for half in range(2):
                            for k in range(KT):
                                wh, wl = wblock(c % 2, k, 0, 256)
                                ts = slice(P * (2 * n + half), P * (2 * n + half) + P)
                                ins = mm3(bank[i][:, 256 * half:256 * half + 256], hH[:, k, ts], hL[:, k, ts], wh,
                                          wl, k == 0, k == KT - 1)
                    else:
                        ins = project(bank[i][:, :], c % 2, n, hH, hL, ALL)
                    ins.then_inc(s.mm_done, step(n, 2))
            for i in range(16):
                if i % 2 == 0:
                    have(C_GATES + i // 2)
                if i < 4:
                    free(B_MERGE + i)
                else:
                    pe.wait_ge(s.gate_sig, i - 3)
                project(bank[i % 4][:, :], (i // 2) % 2, i % 2, hH, hL, ALL).then_inc(s.mm_done, step(i % 2, 2))
            pe.wait_ge(s.mask_ready, 1)
            pe.wait_ge(s.bank_free, B_MERGE)
            for i in range(4 * NH2 + 4):
                if i < 4 * NH2:
                    h, x = divmod(i, 4)
                    j, w = 3 - x, P * (x + 1)
                    r = slice(64 * (h % 2), 64 * (h % 2) + 64)
                    if i < 4:
                        pe.wait_ge(s.gate_sig, 13 + i)
                    else:
                        pe.wait_ge(s.at_exp, i - 3)
                    z = bank[i % 4]
                    ks, qs = slice(P * j, P * j + P), slice(P * j, L)
                    mm3(z[:, 0:w], k2H[r, h // 2, ks], k2L[r, h // 2, ks], q2H[r, h // 2, qs], q2L[r, h // 2, qs],
                        True, False, True)
                    mm(z[:, 0:P], maskR[:, 0, :], maskR[:, 1, :], start=False, stop=True,
                       skip_group_check=True).then_inc(s.z_done, 1)
                if 0 <= i - 2 < 4 * NH2:
                    k = i - 2
                    x = k % 4
                    pe.wait_ge(s.sp_lo, k + 1)
                    for y in range(x + 1):
                        at, wy = SP_AT[y], P * (y + 1)
                        o = bank[k % 4][:, P * (x - y):P * (x + 1)]
                        lhs = maskR[:, 2 if y == x else 3, :]
                        mm(o, lhs, spH[:, at:at + wy], start=False, stop=False, skip_group_check=True)
                        ins = mm(o, lhs, spL[:, at:at + wy], start=False, stop=(y == x), skip_group_check=True)
                    ins.then_inc(s.arg_done, 1)
                if i >= 4:
                    k = i - 4
                    h, x = divmod(k, 4)
                    pe.wait_ge(s.at_lo, k + 1)
                    if x == 0 and h >= 2:
                        pe.wait_ge(s.o2_lo, h - 1)
                    hs = slice(P * (h // 2), P * (h // 2) + P)
                    w = P * (x + 1)
                    mm3(bank[4 + h % 2][:, L - w:L], v2H[:, 3 - x, hs], v2L[:, 3 - x, hs], atH[:, k % 2, 0:w],
                        atL[:, k % 2, 0:w], x == 0, x == 3, True).then_inc(s.pv2_done, 1)
            pe.wait_ge(s.conv_tap, TAPS * CT)
            for k in range(CT):
                ins = mm(bank[6][:, :], ones[:, :], cacc[:, k, :], start=(k == 0), stop=(k == CT - 1))
            ins.then_inc(s.lnsum_done, 1)
            for k in range(CT):
                pe.wait_ge(s.lnsq_ready, k + 1)
                if k == 0:
                    pe.wait_ge(s.o2_lo, NH2)
                mm(bank[5][:, :], ones[:, :], scratch[:, k % 2, :], start=(k == 0), stop=(k == CT - 1))\
                    .then_inc(s.lnsq_used if k < CT - 1 else s.lnvar_done, 1)
            pe.wait_ge(s.at_exp, 4 * NH2)
            pe.wait_ge(s.c_lo, CT)
            for p in range(4):
                have(C_MERGE + p)
                for x in range(2):
                    for y in range(2):
                        free(B_MERGE + 4 * p + 2 * x + y) if 4 * p + 2 * x + y >= 4 else None
                        src = (cH, cL) if y == 0 else (q2H, q2L)
                        ins = project(bank[2 * x + y][:, :], p % 2, x, *src, [(4 * y + k, k) for k in range(4)])
                    ins.then_inc(s.mm_done, step(x, 2))
            out_phase(2, C_O, B_O, mgH, mgL, (s.mg_lo, 0))
            with pe.Fori(0, FT // 2) as i:
                for j in range(2):
                    have(2 * i + (C_UP2 + j))
                    for x in range(2):
                        pe.wait_ge(s.bank_free, 4 * i + (B_UP2 + 2 * j + x - 3))
                        project(bank[2 * j + x][:, :], j, x, hH, hL, ALL,
                                ready=(s.h_lo, 3 * KT) if j == x == 0 else None).then_inc(s.mm_done, step(x, 2))
            down_phase(3, C_DOWN2, B_DOWN2, s.ffn2_lo)


def tiles(w, cols):
    k = w.shape[0] // P
    return np.concatenate([w[:, c].reshape(k, P, -1) for c in cols], axis=2).transpose(1, 0, 2)


def col(i, width=P):
    return slice(i * width, (i + 1) * width)


def weight_stream(w_in, w_out, w_up, w_down, w_in2, w_conv, w_att, w_o, w_ffn_in, w_ffn_out, dft):
    out = np.zeros((N_CHUNKS, P, CH), np.float32)

    def put(c, w, cols, at=0):
        t = tiles(w, cols)
        out[c, :, at:at + t.shape[1] * 256] = t.reshape(P, -1)

    for p in range(2):
        put(2 * p, w_in, [col(2 + p, 256)])
        put(2 * p + 1, w_in, [col(4 + p, 256)])
        put(C_Q + p, w_in, [col(p, 256)])
        put(C_F + p, w_in, [col(8 + p, 256)])
        out[C_DFT + p] = dft[p].reshape(TT, P, L).transpose(1, 0, 2).reshape(P, -1)
        put(C_G + p, w_in, [col(6 + p, 256)])
    for p in range(4):
        put(C_OUT + p, w_out, [col(p, 256)])
        put(C_MERGE + p, w_conv, [col(p, 256)])
        put(C_MERGE + p, w_att, [col(p, 256)], CH // 2)
        put(C_O + p, w_o, [col(p, 256)])
        put(C_U + p, w_in2, [col(p), col(4 + p)])
        for j in range(3):
            rows = slice(8 * j * P, min(8 * j + 8, FT) * P)
            put(C_DOWN + 3 * p + j, w_down[rows], [col(p, 256)])
            put(C_DOWN2 + 3 * p + j, w_ffn_out[rows], [col(p, 256)])
    for t in range(FT):
        put(C_UP + t, w_up, [col(t), col(FT + t)])
        put(C_UP2 + t, w_ffn_in, [col(t), col(FT + t)])
    for p in range(2):
        put(C_Q2 + p, w_in2, [col(4 + p, 256)])
        put(C_K2 + p, w_in2, [col(6 + p, 256)])
        put(C_V2 + p, w_in2, [col(8 + p, 256)])
    for p in range(8):
        put(C_GATES + p, w_in2, [col(10 + p, 256)])
    return out


def tables():
    f32 = np.float32
    n_freq = HD // 4
    freqs = (f32(10000.0) ** (-np.arange(n_freq, dtype=f32) / f32(n_freq))).astype(f32)
    t = np.arange(L)
    ang = np.concatenate([(t // ROW).astype(f32)[:, None] * freqs, (t % ROW).astype(f32)[:, None] * freqs], 1)
    cos, sin = np.cos(ang).T, np.sin(ang).T
    rope = np.stack([np.concatenate([cos, cos]), np.concatenate([-sin, sin])], 1).astype(f32)
    band = (np.arange(BAND)[None, :] - np.arange(P)[:, None] - (TT - 1) * P).astype(f32)
    pos = np.broadcast_to(np.arange(1, L + 1, dtype=f32), (P, L)).copy()
    e = np.outer(np.arange(P), np.arange(P)) % P * (2 * np.pi / P)
    csd = (np.concatenate([np.cos(e), np.sin(e)], 1) / 256.0).astype(f32)
    a = np.outer(np.arange(L), np.arange(L)) % L * (2 * np.pi / L)
    dft = np.stack([np.cos(a), -np.sin(a)]).astype(f32)
    key, query = np.arange(P)[:, None], np.arange(P)[None, :]
    masks = np.stack([np.eye(P), np.where(key >= query, NEG, 0.0), np.where(key >= query, -1.0, 0.0),
                      -np.ones((P, P))], 1).astype(f32)
    return rope, band, pos, csd, dft, masks


def kernel(x, c, ctx, c_ctx, w_ada, b_ada, g_mix_pre, g_mix_post, g_ffn_pre, g_ffn_post, w_in,
           ret_decay_fwd, ret_decay_bwd, w_out, w_up, conv_w, conv_b, w_down, c_2, ada_w_2, ada_b_2,
           pre_mix_g_2, post_mix_g_2, pre_ffn_g_2, post_ffn_g_2, w_in_2, conv_w_2, conv_b_2,
           conv_ln_g_2, conv_ln_b_2, w_conv_out_2, w_att_out_2, w_o_2, w_ffn_in_2, w_ffn_out_2):
    import concourse.bacc as bacc
    from concourse.bass_utils import run_bass_kernel_spmd

    def vt(a):
        return np.asarray(a).reshape(-1, P).T

    def feature_major(a, n):
        return np.ascontiguousarray(np.asarray(a).reshape(n, KT, P).transpose(2, 1, 0))

    rope, band, pos, csd, dft, masks = tables()
    decays = np.concatenate([np.asarray(ret_decay_fwd)[0], np.asarray(ret_decay_bwd)[0]])
    m = np.arange(LC, dtype=np.float32).reshape(TC, P).T
    vecs = np.concatenate(
        [vt(c), vt(c_ctx), vt(c_2), vt(b_ada), vt(ada_b_2), vt(g_mix_pre), vt(g_mix_post), vt(g_ffn_pre),
         vt(g_ffn_post), vt(pre_mix_g_2), vt(post_mix_g_2), vt(pre_ffn_g_2), vt(post_ffn_g_2), vt(conv_w),
         vt(conv_b), vt(conv_w_2), vt(conv_b_2), vt(conv_ln_g_2), vt(conv_ln_b_2),
         np.broadcast_to(decays, (P, 2 * HEADS)), LC - 1 - m, m], axis=1)
    stream = weight_stream(*(np.asarray(w)[0] for w in (w_in, w_out, w_up, w_down, w_in_2, w_conv_out_2,
                                                        w_att_out_2, w_o_2, w_ffn_in_2, w_ffn_out_2)), dft)
    ada = np.stack([tiles(np.asarray(w)[0], [col(i, 256)]).reshape(P, CH) for w in (w_ada, ada_w_2)
                    for i in range(24)])
    arrays = {"weights": stream, "ada": ada, "x_t": feature_major(x, L), "ctx_t": feature_major(ctx, LC),
              "vecs": vecs, "rope": rope, "band": band, "pos": pos, "csd": csd, "masks": masks}
    arrays = {k: np.ascontiguousarray(a) for k, a in arrays.items()}
    nc = bacc.Bacc("TRN2", target_bir_lowering=False, num_devices=1)
    args = {k: nc.dram_tensor(k, a.shape, mybir.dt.float32, kind="ExternalInput").ap() for k, a in arrays.items()}
    out = nc.dram_tensor("out_t", (P, KT, L), mybir.dt.float32, kind="ExternalOutput").ap()
    build(nc, out=out, **args)
    r = run_bass_kernel_spmd(nc, [arrays], core_ids=[0])
    return r.results[0]["out_t"].transpose(2, 1, 0).reshape(1, L, D)
```

```python
from contextlib import ExitStack

import numpy as np
import concourse.bass as bass
from concourse import mybir

P = 128
D, L, LC = 1024, 512, 256
KT = D // P
TT, TC = L // P, LC // P
HEADS, HD = 4, 128
RET = HEADS * HD
GROUPS = 4
FF = ((8 * D // 3 + 127) // 128) * 128
FT = FF // P
ROW = 64
NH2, HD2 = 8, 64
CW = 512
CT = CW // P
TAPS = 31
EPS = 1e-6
CH = 2048
NEG = -1e30

C_KV, C_Q, C_F, C_DFT, C_G = 0, 4, 6, 8, 10
C_OUT = 12
C_UP = 16
C_DOWN = C_UP + FT
C_U = C_DOWN + 12
C_K2, C_V2, C_Q2, C_GATES = C_U + 4, C_U + 6, C_U + 8, C_U + 10
C_MERGE = C_GATES + 8
C_O = C_MERGE + 4
C_UP2 = C_O + 4
C_DOWN2 = C_UP2 + FT
N_CHUNKS = C_DOWN2 + 12
ADA_FIRST = 8
ADA_LATER = 40
JOBS_UP = 14
JOBS_DOWN = JOBS_UP + FT // 2

VECS = [("c", KT), ("cc", KT), ("c2", KT), ("b_ada", 48), ("b_ada2", 48), ("g0", KT), ("p0", KT), ("g1", KT),
        ("p1", KT), ("g2", KT), ("p2", KT), ("g3", KT), ("p3", KT), ("cw", 3 * 2 * FT), ("cb", 2 * FT),
        ("cw2", TAPS * CT), ("cb2", CT), ("lng", CT), ("lnb", CT), ("dec", 2 * HEADS), ("mpos", 2 * TC)]
VAT = {}
_at = 0
for _n, _w in VECS:
    VAT[_n] = _at
    _at += _w
NV = _at
B_OUT, B_UP = 0, KT
B_DOWN = B_UP + 2 * FT
B_U = B_DOWN + KT
B_K2, B_V2, B_Q2, B_MERGE = B_U + 8, B_U + 12, B_U + 16, B_U + 20
B_O = B_MERGE + 16
B_UP2 = B_O + KT
B_DOWN2 = B_UP2 + 2 * FT
SHIFT_AT, SCALE_AT, GATE_AT = {1: 8, 2: 32, 3: 56}, {1: 16, 2: 40, 3: 64}, {0: 0, 1: 24, 2: 48, 3: 72}
SP_AT = (0, P, 3 * P, 6 * P)
BAND = L + (TT - 1) * P


def build(nc, weights, ada, x_t, ctx_t, vecs, rope, band, pos, csd, masks, out):
    F, R = mybir.dt.float32, mybir.dt.float32r
    ALU, ACT = mybir.AluOpType, mybir.ActivationFunctionType
    mult, add, sub = ALU.mult, ALU.add, ALU.subtract
    stack = ExitStack()
    with stack:
        KB = 1024
        base = [(nc.sbuf_base + 31) // 32 * 32]

        def fix(name, shape, dt=F):
            size = int(np.prod(shape[1:])) * 4
            t = nc.alloc_sbuf_tensor_at(name, shape, dt, offset=base[0])
            base[0] += (size + 31) // 32 * 32
            return t

        def over(name, shape, at, dt=F):
            return nc.alloc_sbuf_tensor_at(name, shape, dt, offset=int(at))

        xT = fix("xT", [P, KT, L])
        H0 = base[0]
        hH, hL = fix("hH", [P, KT, L], R), fix("hL", [P, KT, L], R)
        raw = fix("raw", [P, 2, CH])
        WH, WL = fix("WH", [P, 2, CH], R), fix("WL", [P, 2, CH], R)
        ada_half = fix("ada_half", [P, 2, CH // 2])
        vec = fix("vec", [P, NV])
        ones = fix("ones", [P, P])
        csil = fix("csil", [P, KT, 2])
        csil2 = fix("csil2", [P, KT])
        csil_up = fix("csil_up", [P, FT // 2, KT])
        rstd = fix("rstd", [P, L])
        scratch = fix("scratch", [P, 2, L])
        ada_acc = fix("ada_acc", [P, 2, 256])
        mod0 = fix("mod0", [P, 16, 2])
        mod = fix("mod", [P, 2 * ADA_LATER])
        gm = fix("gm", [P, 2, KT])
        gp = fix("gp", [P, KT])
        lg = fix("lg", [P, 3, 2 * HEADS])
        eps = fix("eps", [P, 1])
        ident2 = fix("ident2", [2, 2])
        zeta = fix("zeta", [P, 2, HEADS, TC])
        U = base[0]
        adaf = over("adaf", [P, ADA_FIRST, CH], U)
        kH, kL = over("kH", [P, HEADS, L], U, R), over("kL", [P, HEADS, L], U + 8 * KB, R)
        vH, vL = over("vH", [P, TT, RET], U + 16 * KB, R), over("vL", [P, TT, RET], U + 24 * KB, R)
        qH, qL = over("qH", [P, HEADS, L], U + 32 * KB, R), over("qL", [P, HEADS, L], U + 40 * KB, R)
        ktmp = over("ktmp", [P, 4, L], U + 32 * KB)
        tmp0 = over("tmp0", [P, 4, L], U + 32 * KB)
        kctmp = over("kctmp", [P, 2, 256], U + 40 * KB)
        sH, sL = over("sH", [P, 2, HEADS, P], U + 48 * KB, R), over("sL", [P, 2, HEADS, P], U + 52 * KB, R)
        hcH, hcL = over("hcH", [P, KT, LC], U + 56 * KB, R), over("hcL", [P, KT, LC], U + 64 * KB, R)
        qtmp = over("qtmp", [P, 4, L], U + 56 * KB)
        kcH, kcL = over("kcH", [P, TC, 2, 256], U + 72 * KB, R), over("kcL", [P, TC, 2, 256], U + 76 * KB, R)
        m0row = over("m0row", [2, 16 * P], U + 64 * KB)
        csd_in = over("csd_in", [P, 256], U + 72 * KB)
        ctxT = over("ctxT", [P, KT, LC], U + 76 * KB)
        vcH, vcL = over("vcH", [P, TC, 256], U + 80 * KB, R), over("vcL", [P, TC, 256], U + 82 * KB, R)
        ropeT = over("ropeT", [P, 2, L], U + 84 * KB)
        bandT = over("bandT", [P, BAND], U + 88 * KB)
        posT = over("posT", [P, L], U + 91.5 * KB)
        csdH, csdL = over("csdH", [P, 256], U + 93.5 * KB, R), over("csdL", [P, 256], U + 94.5 * KB, R)
        decay = (over("decay0", [P, BAND], U + 56 * KB), over("decay1", [P, BAND], U + 96 * KB))
        sqacc = over("sqacc", [P, L], U + 99.5 * KB)
        xi = over("xi", [P, 2, L], U + 59.5 * KB)
        aF = over("aF", [P, 2, L], U + 63.5 * KB)
        aH, aL = over("aH", [P, 2, L], U + 67.5 * KB, R), over("aL", [P, 2, L], U + 71.5 * KB, R)
        comb = over("comb", [P, L], U + 75.5 * KB)
        oT = over("oT", [P, HEADS, L], U + 77.5 * KB)
        fH, fL = over("fH", [P, GROUPS, L], U, R), over("fL", [P, GROUPS, L], U + 8 * KB, R)
        fcH, fcL = over("fcH", [P, 2, TT, 256], U + 16 * KB, R), over("fcL", [P, 2, TT, 256], U + 24 * KB, R)
        mixH, mixL = over("mixH", [P, KT, L], U + 32 * KB, R), over("mixL", [P, KT, L], U + 48 * KB, R)
        GH, GL = over("GH", [P, FT, L], U, R), over("GL", [P, FT, L], U + 44 * KB, R)
        tmp1 = over("tmp1", [P, 4, L], U)
        tA, tB = over("tA", [P, 2, L], U + 88 * KB), over("tB", [P, 2, L], U + 92 * KB)
        yT = over("yT", [P, KT, L], H0)
        uT, cacc = over("uT", [P, CT, L], U), over("cacc", [P, CT, L], U + 8 * KB)
        q2H, q2L = over("q2H", [P, 4, L], U + 16 * KB, R), over("q2L", [P, 4, L], U + 24 * KB, R)
        k2H, k2L = over("k2H", [P, 4, L], U + 32 * KB, R), over("k2L", [P, 4, L], U + 40 * KB, R)
        v2H, v2L = over("v2H", [P, TT, CW], U + 48 * KB, R), over("v2L", [P, TT, CW], U + 56 * KB, R)
        gates = over("gates", [P, 16, L], U + 64 * KB)
        mgH, mgL = over("mgH", [P, KT, L], U + 64 * KB, R), over("mgL", [P, KT, L], U + 80 * KB, R)
        spH, spL = over("spH", [P, 1280], H0, R), over("spL", [P, 1280], H0 + 5 * KB, R)
        atH, atL = over("atH", [P, 2, L], H0 + 10 * KB, R), over("atL", [P, 2, L], H0 + 14 * KB, R)
        maskR = over("maskR", [P, 4, P], H0 + 18 * KB, R)
        sptmp = over("sptmp", [P, 2, L], H0 + 20 * KB)
        spF = over("spF", [P, 2, L], H0 + 24 * KB)
        atF = over("atF", [P, 2, L], H0 + 28 * KB)
        mask_in = over("mask_in", [P, 4, P], H0 + 28 * KB)
        cH, cL = over("cH", [P, CT, L], H0, R), over("cL", [P, CT, L], H0 + 8 * KB, R)
        assert U + 101.5 * KB <= nc.sbuf_usable_end, (U, nc.sbuf_usable_end)

        bank = [stack.enter_context(nc.psum_tensor(f"bank{i}", [P, 512], F)) for i in range(8)]
        sems = {}

        class Sems:
            def __getattr__(self, name):
                if name not in sems:
                    sems[name] = stack.enter_context(nc.semaphore(name))
                return sems[name]

        s = Sems()

        adaf_in = [stack.enter_context(nc.semaphore(f"adaf{i}_in")) for i in range(ADA_FIRST)]
        raw_in = [stack.enter_context(nc.semaphore(f"raw{i}_in")) for i in range(2)]
        ada_in = [stack.enter_context(nc.semaphore(f"ada_half{i}_in")) for i in range(2)]

        def v(name, i, n=1):
            return vec[:, VAT[name] + i:VAT[name] + i + n]

        def step(n, of):
            return 1 if n < of - 1 else 17 - of

        def done(c, n, of):
            return 16 * c + (n + 1 if n < of - 1 else 16)

        def dft_done(g):
            return 16 * C_DFT + g + 1 if g < GROUPS - 1 else 16 * (C_DFT + 2)

        block = stack.enter_context(nc.Block())

        class Chain:
            def __init__(self, eng, sem):
                self.eng, self.sem, self.n, self.extra = eng, sem, 0, None

            def link(self, ins):
                self.n += 1
                ins.then_inc(self.sem, 1)
                self.eng.wait_ge(self.sem, self.n if self.extra is None else self.extra + self.n)

            def enter(self, i, per):
                self.extra, self.start, self.per = i * per, self.n, per

            def leave(self, passes):
                assert self.n - self.start == self.per, self.n - self.start
                self.n, self.extra = self.start + passes * self.per, None

        @block.sync
        def _(sp):
            sp.dma_start(vec[:, :], vecs).then_inc(s.vec_in, 16)
            sp.dma_start(ctxT[:, :, :], ctx_t).then_inc(s.ctx_in, 16)
            sp.dma_start(ident2[:, :], masks[0:2, 0, 0:2]).then_inc(s.ident2_in, 16)
            for i in range(ADA_FIRST):
                sp.dma_start(adaf[:, i, :], ada[i]).then_inc(adaf_in[i], 16)
                if i == 1:
                    for j in range(2):
                        half = slice(j * KT // 2, (j + 1) * KT // 2)
                        sp.dma_start(xT[:, half, :], x_t[:, half, :]).then_inc(s.x_in, 16)
            sp.dma_start(csd_in[:, :], csd).then_inc(s.csd_in, 16)
            for j in range(2):
                sp.dma_start(raw[:, j, :], weights[j]).then_inc(raw_in[j], 16)
            for j in range(2):
                sp.dma_start(ada_half[:, j, :], ada[ADA_FIRST, :, j * (CH // 2):(j + 1) * (CH // 2)])\
                    .then_inc(ada_in[j], 16)
            sp.dma_start(ropeT[:, :, :], rope).then_inc(s.rope_in, 16)
            sp.dma_start(bandT[:, :], band).then_inc(s.band_in, 16)
            sp.dma_start(posT[:, :], pos).then_inc(s.pos_in, 16)

            def load_chunk(c, slot):
                sp.wait_ge(s.lo_done, c - 1)
                sp.dma_start(raw[:, slot, :], weights[c]).then_inc(raw_in[slot], 16)

            def load_half_job(a, j):
                sp.wait_ge(s.ada_read, 2 * a + (j - 1))
                sp.dma_start(ada_half[:, j, :], ada[a + ADA_FIRST, :, j * (CH // 2):(j + 1) * (CH // 2)])\
                    .then_inc(ada_in[j], 16)

            def load_job(a):
                for j in range(2):
                    load_half_job(a, j)

            job = 1
            for c in range(2, C_UP + 3):
                load_chunk(c, c % 2)
                if c == 2 or c - 2 in (C_DFT + 1, C_G):
                    continue
                load_job(job)
                job += 1
            assert job == JOBS_UP + 1, job
            load_chunk(C_UP + 3, 1)
            with sp.Fori(0, FT // 2) as i:
                for j in range(2):
                    load_chunk(2 * i + (C_UP + 4 + j), j)
                    load_half_job(i + JOBS_UP + 1, j)
            load_job(JOBS_DOWN + 1)
            with sp.Fori(0, 6) as i:
                for j in range(2):
                    load_chunk(2 * i + (C_DOWN + 4 + j), j)
                    load_job(2 * i + (JOBS_DOWN + 2 + j))
            load_chunk(C_DOWN + 16, 0)
            load_job(ADA_LATER - 1)
            load_chunk(C_DOWN + 17, 1)
            with sp.Fori((C_DOWN + 18) // 2, (C_MERGE + 2) // 2) as i:
                for j in range(2):
                    load_chunk(2 * i + j, j)
            sp.wait_ge(s.mm_done, 16 * C_MERGE)
            sp.dma_start(mask_in[:, :, :], masks).then_inc(s.mask_in, 16)
            with sp.Fori((C_MERGE + 2) // 2, N_CHUNKS // 2) as i:
                for j in range(2):
                    load_chunk(2 * i + j, j)
            for k in range(KT):
                sp.wait_ge(s.x_new, 3 * KT + k + 1)
                sp.dma_start(out[:, k, :], xT[:, k, :]).then_inc(s.out_done, 16)
            sp.wait_ge(s.out_done, 16 * KT)

        @block.gpsimd
        def _(pool):
            nc.gpsimd.memset(eps[:, :], EPS).then_inc(s.eps_ready, 1)
            nc.gpsimd.memset(ones[:, :], 1.0).then_inc(s.ones_ready, 1)

        @block.scalar
        def _(act):
            A = nc.scalar.activation
            own = Chain(act, s.act_own)

            def split_hi(c, slot, first=False):
                act.wait_ge(raw_in[slot], c * 8 + 16 - 8 * slot)
                if not first:
                    act.wait_ge(s.mm_done, 16 * c - 16)
                A(WH[:, slot, :], raw[:, slot, :], ACT.Copy).then_inc(s.hi_done, 1)

            def norm_hi(m, tmp, hi, width, mul_s, done_s, shift):
                for k in range(KT):
                    act.wait_ge(mul_s, m * KT + k + 1)
                    A(hi[:, k, :], tmp[:, k % 4, 0:width], ACT.Identity, bias=shift(k)).then_inc(done_s, 1)

            def inverse_root(to, mean_of, scale, ready):
                own.link(A(to, mean_of, ACT.Ln, bias=eps[:, :], scale=scale))
                A(to, to, ACT.Exp, scale=-0.5).then_inc(ready, 1)

            def pin_ln_exp():
                act.preload_act_table_set("natural_log_exp_and_others")

            act.wait_ge(s.vec_in, 16)
            A(csil[:, :, 0], v("c", 0, KT), ACT.Silu).then_inc(s.csil_ready, 1)
            A(csil[:, :, 1], v("cc", 0, KT), ACT.Silu).then_inc(s.csil_ready, 1)
            A(csil2[:, :], v("c2", 0, KT), ACT.Silu).then_inc(s.csil_ready, 1)
            pin_ln_exp()
            act.wait_ge(s.ctx_in, 16)
            for k in range(KT):
                if k >= 2:
                    act.wait_ge(s.csq_used, k - 1)
                A(scratch[:, k % 2, 0:LC], ctxT[:, k, :], ACT.Square).then_inc(s.csq_ready, 1)

            def squares_of_x(m):
                for k in range(KT):
                    if m == 0:
                        act.wait_ge(s.x_in, 32)
                        if k < 2:
                            act.wait_ge(s.csq_used, KT)
                    else:
                        act.wait_ge(s.x_new, (m - 1) * KT + k + 1)
                        if k < 2:
                            act.wait_ge(s.ystat_done, m)
                    if k >= 2:
                        act.wait_ge(s.xsq_used, m * KT + k - 1)
                    A(scratch[:, k % 2, :], xT[:, k, :], ACT.Square).then_inc(s.xsq_ready, 1)

            squares_of_x(0)
            act.wait_ge(s.csq_used, KT)
            act.wait_ge(s.eps_ready, 1)
            inverse_root(rstd[:, 0:LC], bank[6][:, 0:LC], 1.0 / D, s.croot_ready)
            act.wait_ge(s.lg_abs, 1)
            own.link(A(lg[:, 1, :], lg[:, 1, :], ACT.Exp))
            A(lg[:, 1, :], lg[:, 1, :], ACT.Ln, bias=1.0).then_inc(s.lg_ln, 1)
            act.wait_ge(s.lg_ready, 1)
            for d in range(2):
                for h in range(HEADS):
                    A(zeta[:, d, h, :], v("mpos", d * TC, TC), ACT.Exp,
                      scale=lg[:, 0, d * HEADS + h:d * HEADS + h + 1]).then_inc(s.zeta_exp, 1)
            act.wait_ge(s.csd_in, 16)
            A(csdH[:, :], csd_in[:, :], ACT.Copy).then_inc(s.csd_hi, 1)
            split_hi(0, 0, True)
            for q in range(4):
                act.wait_ge(s.mod0_sum, 2 * q + 2)
                A(m0row[:, 4 * P * q:4 * P * (q + 1)], bank[q][0:2, :], ACT.Copy).then_inc(s.mod0_row, 1)
            act.wait_ge(s.mod0_ready, 2)
            norm_hi(0, tmp0, hcH, LC, s.cnorm_mul, s.hc_hi, lambda k: mod0[:, k, 1:2])
            act.wait_ge(s.cnorm_mul, KT)
            act.wait_ge(s.xsq_used, KT)
            inverse_root(rstd[:, :], bank[5][:, :], 1.0 / D, s.xroot_ready)
            norm_hi(0, tmp0, hH, L, s.norm_mul, s.h_hi, lambda k: mod0[:, k, 0:1])

            def rope_tile(i, tmp, pb, dst, head, done, swapped, summed, hi):
                act.wait_ge(s.mm_done, done)
                if i >= 2:
                    act.wait_ge(summed, i - 1)
                A(tmp[0:64, i % 2, :], pb[64:128, :], ACT.Copy)
                A(tmp[64:128, i % 2, :], pb[0:64, :], ACT.Copy).then_inc(swapped, 1)
                act.wait_ge(summed, i + 1)
                A(dst[:, head, :], tmp[:, 2 + i % 2, :], ACT.Copy).then_inc(hi, 1)

            def states_hi(p):
                act.wait_ge(s.state_done, p + 1)
                A(sH[:, :, 2 * p:2 * p + 2, :],
                  bank[3][:, :].rearrange("p (d h e) -> p d h e", d=2, h=2), ACT.Copy).then_inc(s.state_hi, 1)

            for p in range(2):
                split_hi(2 * p + 1, 1, p == 0)
                for n in range(2):
                    rope_tile(2 * p + n, ktmp, bank[n], kH, 2 * p + n, done(2 * p, n, 4), s.k_swap, s.k_sum, s.k_hi)
                if p:
                    states_hi(p - 1)
                for tt in range(TC):
                    act.wait_ge(s.kc_scaled, 2 * p + tt + 1)
                    if p:
                        act.wait_ge(s.state_done, p)
                    A(kcH[:, tt, :, :], kctmp[:, :, :], ACT.Copy).then_inc(s.kc_hi, 1)
                split_hi(2 * p + 2, 0)
                for n in range(2):
                    act.wait_ge(s.mm_done, done(2 * p + 1, n, 3))
                    A(vH[:, 2 * n:2 * n + 2, 256 * p:256 * p + 256],
                      bank[n][:, :].rearrange("p (t e) -> p t e", t=2), ACT.Copy).then_inc(s.v_hi, 1)
                act.wait_ge(s.mm_done, done(2 * p + 1, 2, 3))
                A(vcH[:, :, :], bank[2][:, :].rearrange("p (t e) -> p t e", t=2), ACT.Copy).then_inc(s.vc_hi, 1)
            for p in range(2):
                split_hi(C_Q + p + 1, 1 - p)
                for n in range(2):
                    rope_tile(2 * p + n, qtmp, bank[n], qH, 2 * p + n, done(C_Q + p, n, 2), s.q_swap, s.q_sum, s.q_hi)
                if p == 0:
                    states_hi(1)
            pin_ln_exp()

            def decays(h):
                act.wait_ge(s.decay_arg, h + 1)
                A(decay[h % 2][:, :], decay[h % 2][:, :], ACT.Exp).then_inc(s.decay_ready, 1)

            def token_decays(h):
                if h:
                    act.wait_ge(s.cross_read, h)
                A(xi[:, 0, :], posT[:, :], ACT.Exp, scale=lg[:, 0, h:h + 1]).then_inc(s.xi_ready, 1)
                A(xi[:, 1, :], posT[:, :], ACT.Exp, scale=lg[:, 1, HEADS + h:HEADS + h + 1],
                  bias=lg[:, 2, HEADS + h:HEADS + h + 1]).then_inc(s.xi_ready, 1)

            def o_square(h):
                act.wait_ge(s.o_sum, h + 1)
                A(scratch[:, 1, :], oT[:, h, :], ACT.Square).then_inc(s.osq_ready, 1)

            def o_root(h):
                act.wait_ge(s.ostat_done, h + 1)
                if h:
                    act.wait_ge(s.o_norm, h)
                inverse_root(rstd[:, :], bank[1][:, :], 1.0 / HD, s.oroot_ready)

            decays(0)
            token_decays(0)
            for i in range(TT * HEADS):
                h, j = divmod(i, TT)
                act.wait_ge(s.a_mul, i + 1)
                if i >= 2:
                    act.wait_ge(s.pv_done, i - 1)
                A(aH[:, i % 2, :], aF[:, i % 2, :], ACT.Copy).then_inc(s.a_hi, 1)
                if j == 1 and h < HEADS - 1:
                    decays(h + 1)
                if j == 1 and h:
                    o_square(h - 1)
                if j == 3 and h < HEADS - 1:
                    token_decays(h + 1)
                if j == 3 and h:
                    o_root(h - 1)
            o_square(HEADS - 1)
            for p in range(2):
                split_hi(C_F + p + 1, 1 - p)
                for n in range(2):
                    i = 2 * p + n
                    act.wait_ge(s.mm_done, done(C_F + p, n, 2))
                    A(fH[:, i, :], bank[2 + n][:, :], ACT.Copy).then_inc(s.f_hi, 1)
                    if i == 0:
                        o_root(HEADS - 1)
            split_hi(C_DFT + 1, 1)
            for g in range(GROUPS + 1):
                for n in range(2):
                    i = 2 * g + n
                    if g == GROUPS:
                        break
                    act.wait_ge(s.fc_done, i + 1)
                    if g >= 2:
                        act.wait_ge(s.mm_done, dft_done(g - 2))
                    A(fcH[:, g % 2, 2 * n:2 * n + 2, :], bank[n][:, :].rearrange("p (t e) -> p t e", t=2),
                      ACT.Copy).then_inc(s.fc_hi, 1)
                if g:
                    act.wait_ge(s.mm_done, dft_done(g - 1))
                    A(mixH[:, 3 + g, :], bank[4 + (g - 1) % 2][:, :], ACT.Copy).then_inc(s.mix_hi, 1)
            split_hi(C_G, 0)
            for p in range(2):
                split_hi(C_G + p + 1, 1 - p)
                for n in range(2):
                    i = 2 * p + n
                    act.wait_ge(s.mm_done, done(C_G + p, n, 2))
                    if i >= 2:
                        act.wait_ge(s.mix_lo, GROUPS + i - 1)
                    A(scratch[:, i % 2, :], bank[n][:, :], ACT.Silu).then_inc(s.g_silu, 1)
                    act.wait_ge(s.g_mul, i + 1)
                    A(mixH[:, i, :], scratch[:, i % 2, :], ACT.Copy).then_inc(s.mix_hi, 1)

            def out_squares(m, n, done_at):
                act.wait_ge(s.mm_done, done_at)
                if n >= 3:
                    act.wait_ge(s.ysq_used, 6 * m + n - 2)
                elif m == 0:
                    act.wait_ge(s.mix_lo, KT)
                elif m == 2:
                    act.wait_ge(s.mg_lo, KT)
                to = sqacc[:, :] if n == 0 else scratch[:, n % 2, :]
                A(to, bank[n % 4][:, :], ACT.Square).then_inc(s.ysq_ready, 1)

            def out_root(m):
                act.wait_ge(s.ystat_done, m + 1)
                inverse_root(rstd[:, :], bank[4][:, :], 1.0 / D, s.root_ready)

            def out_norm_square(m, c0):
                pin_ln_exp()
                for p in range(4):
                    split_hi(c0 + p + 1, (p + 1) % 2)
                    for n in range(2):
                        out_squares(m, 2 * p + n, done(c0 + p, n, 2))
                out_root(m)

            def down_square(m, c0, skip):
                pin_ln_exp()
                for p in range(4):
                    for j in range(3):
                        if 3 * p + j != skip:
                            split_hi(c0 + 3 * p + j + 1, (3 * p + j + 1) % 2)
                    for n in range(2):
                        out_squares(m, 2 * p + n, done(c0 + 3 * p + 2, n, 2))
                out_root(m)

            def x_root(m):
                act.wait_ge(s.xsq_used, (m + 1) * KT)
                if m:
                    act.wait_ge(s.x_new, m * KT)
                inverse_root(rstd[:, :], bank[5][:, :], 1.0 / D, s.xroot_ready)

            def next_norm(m):
                squares_of_x(m)
                x_root(m)
                act.wait_ge(s.gm_ready, m)
                at = SHIFT_AT[m]
                norm_hi(m, tmp1, hH, L, s.norm_mul, s.h_hi, lambda k: mod[:, at + k:at + k + 1])

            out_norm_square(0, C_OUT)
            next_norm(1)
            act.preload_act_table(ACT.Silu)
            split_hi(C_UP + 1, 1)
            with act.Fori(0, FT // 2) as i:
                for j in range(2):
                    for x, tmp in enumerate((tA, tB)):
                        act.wait_ge(s.mm_done, 32 * i + done(C_UP + j, x, 2))
                        w = VAT["cw"] + 2 * FT + x * FT + j
                        b = VAT["cb"] + x * FT + j
                        A(tmp[:, j, :], bank[2 * j + x][:, :], ACT.Identity, bias=vec[:, bass.ds(2 * i + b, 1)],
                          scale=vec[:, bass.ds(2 * i + w, 1)]).then_inc(s.conv_mid, 1)
                    split_hi(2 * i + (C_UP + j + 2), j)
                    act.wait_ge(s.bank_free, 4 * i + (B_UP + 2 * j + 1))
                    A(tA[:, j, :], tA[:, j, :], ACT.Silu).then_inc(s.ffn_silu, 1)
                    act.wait_ge(s.ffn_mul, 2 * i + j + 1)
                    A(GH[:, bass.ds(2 * i + j, 1), :], tB[:, j:j + 1, :], ACT.Copy).then_inc(s.ffn_hi, 1)
            down_square(1, C_DOWN, 0)
            next_norm(2)
            for i in range(4):
                split_hi(C_U + i + 1, (i + 1) % 2)
                act.wait_ge(s.mm_done, done(C_U + i, 1, 2))
                if i >= 2:
                    act.wait_ge(s.bank_free, B_U + 2 * (i - 1))
                else:
                    act.wait_ge(s.h_lo, 3 * KT)
                A(scratch[:, i % 2, :], bank[2 * (i % 2) + 1][:, :], ACT.Sigmoid).then_inc(s.u_sig, 1)
            for c0, ready in ((C_K2, s.k2_hi), (C_V2, s.v2_hi), (C_Q2, s.q2_hi)):
                for i in range(4):
                    c, n = c0 + i // 2, i % 2
                    if n == 0:
                        split_hi(c + 1, (c + 1) % 2)
                    act.wait_ge(s.mm_done, done(c, n, 2))
                    if c0 == C_K2:
                        A(k2H[:, i, :], bank[i][:, :], ACT.Copy).then_inc(ready, 1)
                    elif c0 == C_V2:
                        A(v2H[:, 2 * n:2 * n + 2, 256 * (i // 2):256 * (i // 2) + 256],
                          bank[i][:, :].rearrange("p (t e) -> p t e", t=2), ACT.Copy).then_inc(ready, 1)
                    else:
                        A(q2H[:, i, :], bank[i][:, :], ACT.Copy, scale=HD2 ** -0.5).then_inc(ready, 1)
            for p in range(8):
                split_hi(C_GATES + p + 1, (p + 1) % 2)
                for n in range(2):
                    i = 2 * p + n
                    act.wait_ge(s.mm_done, done(C_GATES + p, n, 2))
                    A(gates[:, i, :], bank[i % 4][:, :], ACT.Sigmoid).then_inc(s.gate_sig, 1)
            pin_ln_exp()
            act.wait_ge(s.mask_in, 16)
            A(maskR[:, :, :], mask_in[:, :, :], ACT.Copy).then_inc(s.mask_ready, 1)

            def attn_exp(i):
                w = P * (i % 4 + 1)
                act.wait_ge(s.arg_done, i + 1)
                if i == 0:
                    act.wait_ge(s.mask_ready, 1)
                if i >= 2:
                    act.wait_ge(s.at_lo, i - 1)
                A(atF[:, i % 2, 0:w], bank[i % 4][:, 0:w], ACT.Exp).then_inc(s.at_exp, 1)
                act.wait_ge(s.at_exp, i + 1)
                if i >= 2:
                    act.wait_ge(s.pv2_done, i - 1)
                A(atH[:, i % 2, 0:w], atF[:, i % 2, 0:w], ACT.Copy).then_inc(s.at_hi, 1)

            for i in range(4 * NH2 + 5):
                if i < 4 * NH2:
                    w = P * (i % 4 + 1)
                    act.wait_ge(s.z_done, i + 1)
                    if i >= 2:
                        act.wait_ge(s.sp_sum, i - 1)
                    own.link(A(sptmp[:, i % 2, 0:w], bank[i % 4][:, 0:w], ACT.Abs))
                    own.link(A(sptmp[:, i % 2, 0:w], sptmp[:, i % 2, 0:w], ACT.Exp, scale=-1.0))
                    A(sptmp[:, i % 2, 0:w], sptmp[:, i % 2, 0:w], ACT.Ln, bias=1.0).then_inc(s.sp_ln, 1)
                if 0 <= i - 3 < 4 * NH2:
                    attn_exp(i - 3)
                if i >= 8 and i % 4 == 0:
                    h = (i - 8) // 4
                    r = 64 * (h % 2)
                    act.wait_ge(s.pv2_done, 4 * h + 4)
                    A(q2H[r:r + 64, h // 2, :], bank[4 + h % 2][r:r + 64, :], ACT.Copy).then_inc(s.o2_hi, 1)
            for k in range(CT):
                act.wait_ge(s.ln_center, k + 1)
                if k >= 2:
                    act.wait_ge(s.lnsq_used, k - 1)
                A(scratch[:, k % 2, :], cacc[:, k, :], ACT.Square).then_inc(s.lnsq_ready, 1)
            act.wait_ge(s.lnvar_done, 1)
            inverse_root(rstd[:, :], bank[5][:, :], 1.0 / CW, s.lnroot_ready)
            for k in range(CT):
                act.wait_ge(s.ln_mul, k + 1)
                own.link(A(cacc[:, k, :], cacc[:, k, :], ACT.Silu, scale=v("lng", k), bias=v("lnb", k)))
                A(cH[:, k, :], cacc[:, k, :], ACT.Copy).then_inc(s.c_hi, 1)
            for p in range(4):
                split_hi(C_MERGE + p + 1, (p + 1) % 2)
                for n in (2 * p, 2 * p + 1):
                    act.wait_ge(s.mg_sum, n + 1)
                    A(mgH[:, n, :], scratch[:, 0, :], ACT.Copy).then_inc(s.mg_hi, 1)
            out_norm_square(2, C_O)
            next_norm(3)
            act.preload_act_table(ACT.Silu)
            with act.Fori(0, FT // 2) as i:
                for j in range(2):
                    split_hi(2 * i + (C_UP2 + j + 1), 1 - j)
                    act.wait_ge(s.mm_done, 32 * i + done(C_UP2 + j, 0, 2))
                    A(tA[:, j, :], bank[2 * j][:, :], ACT.Silu).then_inc(s.ffn2_silu, 1)
                    act.wait_ge(s.bank_free, 4 * i + (B_UP2 + 2 * j + 2))
                    A(GH[:, bass.ds(2 * i + j, 1), :], tB[:, j:j + 1, :], ACT.Copy).then_inc(s.ffn2_hi, 1)
            down_square(3, C_DOWN2, 11)

        @block.vector
        def _(dve):
            V = nc.vector
            TT_, TS, STT = V.tensor_tensor, V.tensor_scalar, V.scalar_tensor_tensor
            own = Chain(dve, s.dve_own)

            def split_lo(c, slot):
                dve.wait_ge(s.hi_done, c + 1)
                TT_(WL[:, slot, :], raw[:, slot, :], WH[:, slot, :], sub).then_inc(s.lo_done, 1)

            def ada_half_job(a, slot, half, c_col):
                dve.wait_ge(ada_in[half], 16 * a + 16)
                for k in range(4):
                    w = ada_half[:, half, 256 * k:256 * k + 256]
                    if half == k == 0:
                        ins = TS(ada_acc[:, slot, :], w, c_col(0), None, mult)
                    else:
                        ins = STT(ada_acc[:, slot, :], w, c_col(4 * half + k), ada_acc[:, slot, :], mult, add)
                    if k < 3:
                        own.link(ins)
                    else:
                        ins.then_inc(s.ada_read, 1)
                        dve.wait_ge(s.ada_read, 2 * a + (half + 1))

            def ada_job(a, slot, c_col, first=False):
                if not first:
                    dve.wait_ge(s.ada_summed, a - 1)
                for half in range(2):
                    ada_half_job(a, slot, half, c_col)

            ada_next = [0]

            def ada_now():
                a = ada_next[0]
                ada_next[0] += 1
                ada_job(a, a % 2, (lambda k: csil[:, k, 0:1]) if a < 16 else (lambda k: csil2[:, k:k + 1]), a < 2)

            def norm_lo(m, tmp, src, width, hi, lo, shift, gain, mul_s, hi_s, lo_s):
                for k in range(KT + 2):
                    if k < KT:
                        if k >= 4:
                            dve.wait_ge(lo_s, m * KT + k - 3)
                        STT(tmp[:, k % 4, 0:width], src[:, k, :], gain(k), rstd[:, 0:width], mult, mult)\
                            .then_inc(mul_s, 1)
                    if k >= 2:
                        q = k - 2
                        dve.wait_ge(hi_s, m * KT + q + 1)
                        STT(lo[:, q, :], tmp[:, q % 4, 0:width], shift(q), hi[:, q, :], add, sub).then_inc(lo_s, 1)

            dve.wait_ge(s.vec_in, 16)
            dec = v("dec", 0, 2 * HEADS)
            STT(lg[:, 1, :], dec, -1.0, dec, mult, ALU.min).then_inc(s.lg_abs, 1)
            own.link(TS(lg[:, 0, :], dec, 0.0, None, ALU.min))
            dve.wait_ge(s.lg_ln, 1)
            own.link(TT_(lg[:, 0, :], lg[:, 0, :], lg[:, 1, :], sub))
            TS(lg[:, 1, :], lg[:, 0, :], -1.0, None, mult)
            TS(lg[:, 2, :], lg[:, 0, :], float(L + 1), None, mult).then_inc(s.lg_ready, 1)
            dve.wait_ge(s.csil_ready, 3)
            for i in range(FT // 2):
                own.link(V.tensor_copy(csil_up[:, i, :], csil[:, :, 0] if JOBS_UP + i < 16 else csil2[:, :]))
            dve.wait_ge(s.zeta_exp, 2 * HEADS)
            own.link(TS(zeta[:, :, :, :], zeta[:, :, :, :], HD ** -0.5, None, mult))
            dve.wait_ge(s.csd_hi, 1)
            TT_(csdL[:, :], csd_in[:, :], csdH[:, :], sub).then_inc(s.csd_lo, 1)
            split_lo(0, 0)
            dve.wait_ge(s.mod0_done, 4)
            for j in range(2):
                b3 = bank[4][:, 0:32].rearrange("p (n j) -> p n j", j=2)
                own.link(TT_(mod0[:, :, j], b3[:, :, j], v("b_ada", 0, 16), add))
                STT(gm[:, j, :], mod0[:, 8:16, j], 1.0, v("g0", 0, KT), add, mult).then_inc(s.mod0_ready, 1)
            dve.wait_ge(s.mod0_ready, 2)
            dve.wait_ge(s.croot_ready, 1)
            dve.wait_ge(s.xsq_used, KT)
            norm_lo(0, tmp0, ctxT, LC, hcH, hcL, lambda k: mod0[:, k, 1:2], lambda k: gm[:, 1, k:k + 1],
                    s.cnorm_mul, s.hc_hi, s.hc_lo)
            dve.wait_ge(s.hc_lo, KT)
            dve.wait_ge(s.xroot_ready, 1)
            norm_lo(0, tmp0, xT, L, hH, hL, lambda k: mod0[:, k, 0:1], lambda k: gm[:, 0, k:k + 1],
                    s.norm_mul, s.h_hi, s.h_lo)

            def rope_tile(i, tmp, pb, hi, lo, head, done_at, swapped, summed, hi_s, lo_s):
                dve.wait_ge(s.mm_done, done_at)
                if i == 0:
                    dve.wait_ge(s.rope_in, 16)
                dve.wait_ge(swapped, i + 1)
                TT_(tmp[:, 2 + i % 2, :], pb[:, :], ropeT[:, 0, :], mult)
                own.link(TT_(tmp[:, i % 2, :], tmp[:, i % 2, :], ropeT[:, 1, :], mult))
                TT_(tmp[:, 2 + i % 2, :], tmp[:, 2 + i % 2, :], tmp[:, i % 2, :], add).then_inc(summed, 1)
                dve.wait_ge(hi_s, i + 1)
                TT_(lo[:, head, :], tmp[:, 2 + i % 2, :], hi[:, head, :], sub).then_inc(lo_s, 1)

            def states_lo(p):
                dve.wait_ge(s.state_hi, p + 1)
                TT_(sL[:, :, 2 * p:2 * p + 2, :], bank[3][:, :].rearrange("p (d h e) -> p d h e", d=2, h=2),
                    sH[:, :, 2 * p:2 * p + 2, :], sub).then_inc(s.state_lo, 1)

            for p in range(2):
                split_lo(2 * p + 1, 1)
                for n in range(2):
                    rope_tile(2 * p + n, ktmp, bank[n], kH, kL, 2 * p + n, done(2 * p, n, 4), s.k_swap, s.k_sum,
                              s.k_hi, s.k_lo)
                if p:
                    states_lo(p - 1)
                for tt in range(TC):
                    dve.wait_ge(s.mm_done, done(2 * p, 2 + tt, 4))
                    if 2 * p + tt:
                        dve.wait_ge(s.kc_lo, 2 * p + tt)
                    for d in range(2):
                        for h in range(2):
                            ins = TS(kctmp[:, d, P * h:P * h + P], bank[2 + tt][:, P * h:P * h + P],
                                     zeta[:, d, 2 * p + h, tt:tt + 1], None, mult)
                    ins.then_inc(s.kc_scaled, 1)
                    dve.wait_ge(s.kc_hi, 2 * p + tt + 1)
                    TT_(kcL[:, tt, :, :], kctmp[:, :, :], kcH[:, tt, :, :], sub).then_inc(s.kc_lo, 1)
                ada_now()
                split_lo(2 * p + 2, 0)
                for n in range(2):
                    dve.wait_ge(s.v_hi, 2 * p + n + 1)
                    TT_(vL[:, 2 * n:2 * n + 2, 256 * p:256 * p + 256],
                        bank[n][:, :].rearrange("p (t e) -> p t e", t=2),
                        vH[:, 2 * n:2 * n + 2, 256 * p:256 * p + 256], sub).then_inc(s.v_lo, 1)
                dve.wait_ge(s.vc_hi, p + 1)
                TT_(vcL[:, :, :], bank[2][:, :].rearrange("p (t e) -> p t e", t=2), vcH[:, :, :], sub)\
                    .then_inc(s.vc_lo, 1)
                ada_now()
            for p in range(2):
                split_lo(C_Q + p + 1, 1 - p)
                for n in range(2):
                    rope_tile(2 * p + n, qtmp, bank[n], qH, qL, 2 * p + n, done(C_Q + p, n, 2), s.q_swap, s.q_sum,
                              s.q_hi, s.q_lo)
                if p == 0:
                    states_lo(1)
                ada_now()
            dve.wait_ge(s.band_in, 16)

            def decay_args(h):
                if h >= 2:
                    dve.wait_ge(s.a_mul, TT * (h - 1))
                own.link(TS(decay[h % 2][:, :], bandT[:, :], lg[:, 1, HEADS + h:HEADS + h + 1], None, mult))
                STT(decay[h % 2][:, :], bandT[:, :], lg[:, 0, h:h + 1], decay[h % 2][:, :], mult, ALU.min)\
                    .then_inc(s.decay_arg, 1)

            def cross(h):
                dve.wait_ge(s.cross_done, h + 1)
                dve.wait_ge(s.xi_ready, 2 * h + 2)
                if h:
                    dve.wait_ge(s.o_sum, h)
                TT_(comb[:, :], bank[2][:, :], xi[:, 0, :], mult)
                TT_(scratch[:, 0, :], bank[3][:, :], xi[:, 1, :], mult).then_inc(s.cross_read, 1)

            def cross_sum(h):
                dve.wait_ge(s.cross_read, h + 1)
                own.link(TT_(comb[:, :], comb[:, :], scratch[:, 0, :], add))

            def o_add(h):
                dve.wait_ge(s.pv_done, TT * h + TT)
                TT_(oT[:, h, :], bank[6 if h % 2 == 0 else 0][:, :], comb[:, :], add).then_inc(s.o_sum, 1)

            def o_scale(h):
                dve.wait_ge(s.oroot_ready, h + 1)
                TT_(oT[:, h, :], oT[:, h, :], rstd[:, :], mult).then_inc(s.o_norm, 1)

            decay_args(0)
            for i in range(TT * HEADS + 1):
                h, j = divmod(i, TT)
                if i < TT * HEADS:
                    if j == 0:
                        dve.wait_ge(s.decay_ready, h + 1)
                    dve.wait_ge(s.s_done, i + 1)
                    if i >= 2:
                        dve.wait_ge(s.a_lo, i - 1)
                    at = (TT - 1 - j) * P
                    STT(aF[:, i % 2, :], bank[4 + i % 2][:, :], HD ** -0.5, decay[h % 2][:, at:at + L], mult, mult)\
                        .then_inc(s.a_mul, 1)
                if i:
                    dve.wait_ge(s.a_hi, i)
                    TT_(aL[:, (i - 1) % 2, :], aF[:, (i - 1) % 2, :], aH[:, (i - 1) % 2, :], sub)\
                        .then_inc(s.a_lo, 1)
                if j == 0 and h < HEADS - 1:
                    decay_args(h + 1)
                if j == 0 and h >= 2:
                    o_scale(h - 2)
                if j == 1 and h:
                    o_add(h - 1)
                if j == 2:
                    cross(h)
                if j == 3:
                    cross_sum(h)
            o_add(HEADS - 1)
            for p in range(2):
                split_lo(C_F + p + 1, 1 - p)
                for n in range(2):
                    i = 2 * p + n
                    dve.wait_ge(s.f_hi, i + 1)
                    TT_(fL[:, i, :], bank[2 + n][:, :], fH[:, i, :], sub).then_inc(s.f_lo, 1)
                    if i == 0:
                        o_scale(HEADS - 1)
                ada_now()
            split_lo(C_DFT + 1, 1)
            for g in range(GROUPS + 1):
                for n in range(2):
                    i = 2 * g + n
                    if g == GROUPS:
                        break
                    dve.wait_ge(s.fc_hi, i + 1)
                    TT_(fcL[:, g % 2, 2 * n:2 * n + 2, :], bank[n][:, :].rearrange("p (t e) -> p t e", t=2),
                        fcH[:, g % 2, 2 * n:2 * n + 2, :], sub).then_inc(s.fc_lo, 1)
                if g:
                    dve.wait_ge(s.mix_hi, g)
                    TT_(mixL[:, 3 + g, :], bank[4 + (g - 1) % 2][:, :], mixH[:, 3 + g, :], sub).then_inc(s.mix_lo, 1)
            split_lo(C_G, 0)
            for p in range(2):
                split_lo(C_G + p + 1, 1 - p)
                for n in range(2):
                    i = 2 * p + n
                    dve.wait_ge(s.g_silu, i + 1)
                    TT_(scratch[:, i % 2, :], oT[:, i, :], scratch[:, i % 2, :], mult).then_inc(s.g_mul, 1)
                    dve.wait_ge(s.mix_hi, GROUPS + i + 1)
                    TT_(mixL[:, i, :], scratch[:, i % 2, :], mixH[:, i, :], sub).then_inc(s.mix_lo, 1)
                ada_now()

            def post_gain(m):
                at = GATE_AT[m]
                own.link(TT_(gp[:, :], mod[:, at:at + KT], v(f"p{m}", 0, KT), mult))

            def out_tile(m, n):
                dve.wait_ge(s.ysq_ready, m * KT + n + 1)
                TS(yT[:, n, :], bank[n % 4][:, :], gp[:, n:n + 1], None, mult).then_inc(s.bank_free, 1)
                if 1 <= n < KT - 1:
                    if n > 1:
                        dve.wait_ge(s.ysq_used, 6 * m + n - 1)
                    TT_(sqacc[:, :], sqacc[:, :], scratch[:, n % 2, :], add).then_inc(s.ysq_used, 1)

            def add_and_norm(m, free0):
                dve.wait_ge(s.root_ready, m + 1)
                dve.wait_ge(s.bank_free, free0 + KT)
                if m == 0:
                    modulation(13, 8, 24, 2)
                for k in range(KT):
                    own.link(TT_(yT[:, k, :], yT[:, k, :], rstd[:, :], mult))
                    TT_(xT[:, k, :], xT[:, k, :], yT[:, k, :], add).then_inc(s.x_new, 1)
                if m == 3:
                    return
                at = SCALE_AT[m + 1]
                STT(gm[:, 0, :], mod[:, at:at + KT], 1.0, v(f"g{m + 1}", 0, KT), add, mult).then_inc(s.gm_ready, 1)
                dve.wait_ge(s.gm_ready, m + 1)
                dve.wait_ge(s.xroot_ready, m + 2)
                norm_lo(m + 1, tmp1, xT, L, hH, hL, lambda k: mod[:, SHIFT_AT[m + 1] + k:SHIFT_AT[m + 1] + k + 1],
                        lambda k: gm[:, 0, k:k + 1], s.norm_mul, s.h_hi, s.h_lo)

            def out_phase(m, c0, free0, jobs=0):
                post_gain(m)
                for p in range(4):
                    split_lo(c0 + p + 1, (p + 1) % 2)
                    for _ in range(jobs):
                        ada_now()
                    out_tile(m, 2 * p)
                    out_tile(m, 2 * p + 1)
                add_and_norm(m, free0)

            def down_phase(m, c0, free0, skip):
                post_gain(m)
                for p in range(4):
                    for j in range(3):
                        if 3 * p + j != skip:
                            split_lo(c0 + 3 * p + j + 1, (3 * p + j + 1) % 2)
                        a = JOBS_DOWN + 3 * p + j
                        if m == 1:
                            ada_job(a, (a + 1) % 2, lambda k: csil2[:, k:k + 1])
                    out_tile(m, 2 * p)
                    out_tile(m, 2 * p + 1)
                add_and_norm(m, free0)

            def modulation(summed, a, b, read):
                dve.wait_ge(s.ada_summed, summed)
                bias = v("b_ada", 16 + a, b - a) if b <= 32 else v("b_ada2", a - 32, b - a)
                TT_(mod[:, a:b], bank[7][:, a:b], bias, add).then_inc(s.mod_read, 1)
                dve.wait_ge(s.mod_read, read)

            modulation(9, 0, 8, 1)
            out_phase(0, C_OUT, B_OUT, 1)
            assert ada_next[0] == JOBS_UP, ada_next
            split_lo(C_UP + 1, 1)
            with dve.Fori(0, FT // 2) as i:
                own.enter(i, 2 * (2 + 3))
                for j in range(2):
                    views = []
                    for x, tmp in enumerate((tA, tB)):
                        views.append((tmp[:, j, :].rearrange("p (r c) -> p r c", c=ROW),
                                      bank[2 * j + x][:, :].rearrange("p (r c) -> p r c", c=ROW),
                                      VAT["cw"] + x * FT + j))
                    for x, (t, b, w) in enumerate(views):
                        dve.wait_ge(s.conv_mid, 4 * i + (2 * j + x + 1))
                        own.link(STT(t[:, :, 1:ROW], b[:, :, 0:ROW - 1], vec[:, bass.ds(2 * i + w, 1)],
                                     t[:, :, 1:ROW], mult, add))
                    for x, (t, b, w) in enumerate(views):
                        STT(t[:, :, 0:ROW - 1], b[:, :, 1:ROW], vec[:, bass.ds(2 * i + w + 4 * FT, 1)],
                            t[:, :, 0:ROW - 1], mult, add).then_inc(s.bank_free, 1)
                    split_lo(2 * i + (C_UP + j + 2), j)
                    dve.wait_ge(s.bank_free, 4 * i + (B_UP + 2 * j + 2))
                    dve.wait_ge(s.ffn_silu, 2 * i + (j + 1))
                    TT_(tB[:, j, :], tA[:, j, :], tB[:, j, :], mult).then_inc(s.ffn_mul, 1)
                    if j == 0:
                        dve.wait_ge(s.ada_summed, i + JOBS_UP)
                    ada_half_job(i + JOBS_UP, 1, j, lambda k: csil_up[:, bass.ds(i, 1), k])
                    dve.wait_ge(s.ffn_hi, 2 * i + (j + 1))
                    TT_(GL[:, bass.ds(2 * i + j, 1), :], tB[:, j:j + 1, :], GH[:, bass.ds(2 * i + j, 1), :], sub)\
                        .then_inc(s.ffn_lo, 1)
            own.leave(FT // 2)
            modulation(JOBS_DOWN - 1, 24, 32, 3)
            modulation(JOBS_DOWN - 1, 32, 48, 4)
            down_phase(1, C_DOWN, B_DOWN, 0)

            for i in range(4):
                split_lo(C_U + i + 1, (i + 1) % 2)
                dve.wait_ge(s.u_sig, i + 1)
                TT_(uT[:, i, :], bank[2 * (i % 2)][:, :], scratch[:, i % 2, :], mult).then_inc(s.bank_free, 2)
                a = JOBS_DOWN + 12 + i
                if a < ADA_LATER:
                    ada_job(a, (a + 1) % 2, lambda k: csil2[:, k:k + 1])
            modulation(ADA_LATER, 48, 80, 5)

            conv_n = [0]

            def conv_taps(count):
                for _ in range(count):
                    o = conv_n[0]
                    if o == TAPS * CT:
                        return
                    conv_n[0] += 1
                    shift, k = divmod(o, CT)
                    w = v("cw2", (TAPS - 1 - shift) * CT + k)
                    if shift == 0:
                        dve.wait_ge(s.bank_free, B_K2)
                        TS(cacc[:, k, :], uT[:, k, :], w, v("cb2", k), mult, add).then_inc(s.conv_tap, 1)
                    else:
                        dve.wait_ge(s.conv_tap, o - 3)
                        STT(cacc[:, k, shift:L], uT[:, k, 0:L - shift], w, cacc[:, k, shift:L], mult, add)\
                            .then_inc(s.conv_tap, 1)

            for c0, ready in ((C_K2, s.k2_hi), (C_V2, s.v2_hi), (C_Q2, s.q2_hi)):
                for i in range(4):
                    c, n = c0 + i // 2, i % 2
                    if n == 0:
                        split_lo(c + 1, (c + 1) % 2)
                        conv_taps(9)
                    dve.wait_ge(ready, i + 1)
                    if c0 == C_K2:
                        ins = TT_(k2L[:, i, :], bank[i][:, :], k2H[:, i, :], sub)
                    elif c0 == C_V2:
                        at = slice(256 * (i // 2), 256 * (i // 2) + 256)
                        ins = TT_(v2L[:, 2 * n:2 * n + 2, at], bank[i][:, :].rearrange("p (t e) -> p t e", t=2),
                                  v2H[:, 2 * n:2 * n + 2, at], sub)
                    else:
                        ins = STT(q2L[:, i, :], bank[i][:, :], HD2 ** -0.5, q2H[:, i, :], mult, sub)
                    ins.then_inc(s.bank_free, 1)
            for p in range(8):
                split_lo(C_GATES + p + 1, (p + 1) % 2)
                conv_taps(9)
            for i in range(4 * NH2 + 5):
                if 0 <= i - 1 < 4 * NH2:
                    k = i - 1
                    w = P * (k % 4 + 1)
                    dve.wait_ge(s.sp_ln, k + 1)
                    if k >= 2:
                        dve.wait_ge(s.sp_lo, k - 1)
                    STT(spF[:, k % 2, 0:w], bank[k % 4][:, 0:w], 0.0, sptmp[:, k % 2, 0:w], ALU.max, add)\
                        .then_inc(s.sp_sum, 1)
                    at = SP_AT[k % 4]
                    dve.wait_ge(s.sp_sum, k + 1)
                    if k >= 4:
                        dve.wait_ge(s.arg_done, k - k % 4)
                    V.tensor_copy(spH[:, at:at + w], spF[:, k % 2, 0:w]).then_inc(s.sp_hi, 1)
                    dve.wait_ge(s.sp_hi, k + 1)
                    TT_(spL[:, at:at + w], spF[:, k % 2, 0:w], spH[:, at:at + w], sub).then_inc(s.sp_lo, 1)
                if 0 <= i - 4 < 4 * NH2:
                    k = i - 4
                    w = P * (k % 4 + 1)
                    dve.wait_ge(s.at_hi, k + 1)
                    TT_(atL[:, k % 2, 0:w], atF[:, k % 2, 0:w], atH[:, k % 2, 0:w], sub).then_inc(s.at_lo, 1)
                if i >= 8 and i % 4 == 0:
                    h = (i - 8) // 4
                    r = 64 * (h % 2)
                    dve.wait_ge(s.o2_hi, h + 1)
                    TT_(q2L[r:r + 64, h // 2, :], bank[4 + h % 2][r:r + 64, :], q2H[r:r + 64, h // 2, :], sub)\
                        .then_inc(s.o2_lo, 1)
            dve.wait_ge(s.lnsum_done, 1)
            own.link(TS(rstd[:, :], bank[6][:, :], 1.0 / CW, None, mult))
            for k in range(CT):
                TT_(cacc[:, k, :], cacc[:, k, :], rstd[:, :], sub).then_inc(s.ln_center, 1)
            dve.wait_ge(s.lnroot_ready, 1)
            for k in range(CT):
                TT_(cacc[:, k, :], cacc[:, k, :], rstd[:, :], mult).then_inc(s.ln_mul, 1)
            for k in range(CT):
                dve.wait_ge(s.c_hi, k + 1)
                TT_(cL[:, k, :], cacc[:, k, :], cH[:, k, :], sub).then_inc(s.c_lo, 1)
            for p in range(4):
                split_lo(C_MERGE + p + 1, (p + 1) % 2)
                for x in range(2):
                    n = 2 * p + x
                    dve.wait_ge(s.mm_done, done(C_MERGE + p, x, 2))
                    if n:
                        dve.wait_ge(s.mg_lo, n)
                    TT_(scratch[:, 0, :], gates[:, n, :], bank[2 * x][:, :], mult)
                    TT_(scratch[:, 1, :], gates[:, 8 + n, :], bank[2 * x + 1][:, :], mult).then_inc(s.bank_free, 2)
                    dve.wait_ge(s.bank_free, B_MERGE + 2 * (n + 1))
                    TT_(scratch[:, 0, :], scratch[:, 0, :], scratch[:, 1, :], add).then_inc(s.mg_sum, 1)
                    dve.wait_ge(s.mg_hi, n + 1)
                    TT_(mgL[:, n, :], scratch[:, 0, :], mgH[:, n, :], sub).then_inc(s.mg_lo, 1)
            out_phase(2, C_O, B_O)
            with dve.Fori(0, FT // 2) as i:
                for j in range(2):
                    split_lo(2 * i + (C_UP2 + j + 1), 1 - j)
                    dve.wait_ge(s.ffn2_silu, 2 * i + (j + 1))
                    dve.wait_ge(s.mm_done, 32 * i + done(C_UP2 + j, 1, 2))
                    TT_(tB[:, j, :], tA[:, j, :], bank[2 * j + 1][:, :], mult).then_inc(s.bank_free, 2)
                    dve.wait_ge(s.ffn2_hi, 2 * i + (j + 1))
                    TT_(GL[:, bass.ds(2 * i + j, 1), :], tB[:, j:j + 1, :], GH[:, bass.ds(2 * i + j, 1), :], sub)\
                        .then_inc(s.ffn2_lo, 1)
            down_phase(3, C_DOWN2, B_DOWN2, 11)

        @block.tensor
        def _(pe):
            mm = nc.tensor.matmul

            def mm3(o, lh, ll, rh, rl, start, stop, skip=False):
                mm(o, lh, rh, start=start, stop=False, skip_group_check=skip)
                mm(o, lh, rl, start=False, stop=False, skip_group_check=skip)
                return mm(o, ll, rh, start=False, stop=stop, skip_group_check=skip)

            def have(c):
                pe.wait_ge(s.lo_done, c + 1)

            def wblock(slot, k, a, b):
                return WH[:, slot, 256 * k + a:256 * k + b], WL[:, slot, 256 * k + a:256 * k + b]

            def project(o, slot, n, src_h, src_l, ks, start=True, stop=True, ready=None):
                for x, (kb, k) in enumerate(ks):
                    if ready is not None:
                        pe.wait_ge(ready[0], ready[1] + k + 1)
                    wh, wl = wblock(slot, kb, P * n, P * n + P)
                    ins = mm3(o, wh, wl, src_h[:, k, :], src_l[:, k, :], start and x == 0, stop and x == len(ks) - 1)
                return ins

            ALL = [(k, k) for k in range(KT)]
            ada_next = [0]

            def ada_sum(a, slot, col):
                pe.wait_ge(s.ada_read, 2 * a + 2)
                for j in range(2):
                    ins = mm(bank[7][:, col(j)], ada_acc[:, slot, P * j:P * j + P], ones[:, 0:1], start=True, stop=True,
                             skip_group_check=True)
                ins.then_inc(s.ada_summed, 1)

            def ada_now():
                a = ada_next[0] - 1
                ada_next[0] += 1
                if a < 0:
                    return
                if a == 9:
                    pe.wait_ge(s.mod_read, 1)
                ada_sum(a, a % 2, lambda j: slice(2 * a + j, 2 * a + j + 1))

            def stat(b, src, width, ready, count, done_s, n, of, final):
                pe.wait_ge(ready, count)
                ins = mm(bank[b][:, 0:width], ones[:, :], src, start=(n == 0), stop=(n == of - 1))
                ins.then_inc(final if n == of - 1 and final is not None else done_s, 1)

            pe.wait_ge(s.ones_ready, 1)
            for k in range(KT):
                stat(6, scratch[:, k % 2, 0:LC], LC, s.csq_ready, k + 1, s.csq_used, k, KT, None)
            pe.wait_ge(s.csil_ready, 2)

            def mod0_turn(q):
                pe.wait_ge(s.mod0_row, q + 1)
                if q == 0:
                    pe.wait_ge(s.ident2_in, 16)
                for j in range(4):
                    t = 4 * q + j
                    ins = mm(bank[4][:, 2 * t:2 * t + 2], m0row[:, P * t:P * t + P], ident2[:, :], start=True,
                             stop=True, skip_group_check=True)
                ins.then_inc(s.mod0_done, 1)

            for c in range(ADA_FIRST):
                pe.wait_ge(adaf_in[c], 16)
                for k in range(KT):
                    ins = mm(bank[c // 2][0:2, 256 * (c % 2):256 * (c % 2) + 256], csil[:, k, :],
                             adaf[:, c, 256 * k:256 * k + 256], start=(k == 0), stop=(k == KT - 1))
                ins.then_inc(s.mod0_sum, 1)
                if c == 3:
                    for k in range(KT):
                        stat(5, scratch[:, k % 2, :], L, s.xsq_ready, k + 1, s.xsq_used, k, KT, None)
                if c >= 3 and c % 2:
                    mod0_turn(c // 2 - 1)
            mod0_turn(3)

            have(0)
            for p in range(2):
                slot, c = 0, 2 * p
                have(c)
                for n in range(2):
                    if p:
                        pe.wait_ge(s.v_lo, n + 1)
                    project(bank[n][:, :], slot, n, hH, hL, ALL, ready=(s.h_lo, 0))\
                        .then_inc(s.mm_done, step(n, 4))

                def states(q):
                    pe.wait_ge(s.kc_lo, 2 * q + 2)
                    pe.wait_ge(s.vc_lo, q + 1)
                    for d in range(2):
                        for h in range(2):
                            at = slice(P * (2 * d + h), P * (2 * d + h) + P)
                            hs = slice(P * h, P * h + P)
                            for tt in range(TC):
                                ins = mm3(bank[3][:, at], kcH[:, tt, d, hs], kcL[:, tt, d, hs], vcH[:, tt, hs],
                                          vcL[:, tt, hs], tt == 0, tt == TC - 1, True)
                    ins.then_inc(s.state_done, 1)

                if p:
                    states(0)
                for tt in range(TC):
                    if p and tt == 0:
                        pe.wait_ge(s.vc_lo, 1)
                    if p and tt == 1:
                        pe.wait_ge(s.state_lo, 1)
                    if p == 0 and tt == 1:
                        pe.wait_ge(s.mod0_ready, 2)
                    for k in range(KT):
                        pe.wait_ge(s.hc_lo, k + 1)
                        wh, wl = wblock(slot, k, 0, 256)
                        ts = slice(P * tt, P * tt + P)
                        ins = mm3(bank[2 + tt][:, 0:256], hcH[:, k, ts], hcL[:, k, ts], wh, wl, k == 0, k == KT - 1)
                    ins.then_inc(s.mm_done, step(2 + tt, 4))
                ada_now()
                slot, c = 1, 2 * p + 1
                have(c)
                for b in range(3):
                    if b < 2:
                        pe.wait_ge(s.k_sum, 2 * p + b + 1)
                    else:
                        pe.wait_ge(s.kc_lo, 2 * p + 1)
                    for half in range(2):
                        hh, hl = (hH, hL) if b < 2 else (hcH, hcL)
                        tt = 2 * b + half if b < 2 else half
                        for k in range(KT):
                            wh, wl = wblock(slot, k, 0, 256)
                            ts = slice(P * tt, P * tt + P)
                            ins = mm3(bank[b][:, 256 * half:256 * half + 256], hh[:, k, ts], hl[:, k, ts], wh, wl,
                                      k == 0, k == KT - 1)
                    ins.then_inc(s.mm_done, step(b, 3))
                ada_now()
            for p in range(2):
                have(C_Q + p)
                for n in range(2):
                    if p:
                        pe.wait_ge(s.q_sum, n + 1)
                    else:
                        pe.wait_ge(s.v_lo, 3 + n)
                    project(bank[n][:, :], p, n, hH, hL, ALL).then_inc(s.mm_done, step(n, 2))
                if p == 0:
                    pe.wait_ge(s.kc_lo, 4)
                    states(1)
                ada_now()
            def o_stat(h):
                pe.wait_ge(s.osq_ready, h + 1)
                if h:
                    pe.wait_ge(s.oroot_ready, h)
                mm(bank[1][:, :], ones[:, :], scratch[:, 1, :], start=True, stop=True).then_inc(s.ostat_done, 1)

            pe.wait_ge(s.q_lo, 4)
            pe.wait_ge(s.state_lo, 2)
            for i in range(TT * HEADS + 2):
                if i < TT * HEADS:
                    h, j = divmod(i, TT)
                    if i >= 2:
                        pe.wait_ge(s.a_mul, i - 1)
                    ks = slice(P * j, P * j + P)
                    mm3(bank[4 + i % 2][:, :], kH[:, h, ks], kL[:, h, ks], qH[:, h, :], qL[:, h, :], True, True)\
                        .then_inc(s.s_done, 1)
                if i >= 2:
                    h, j = divmod(i - 2, TT)
                    pe.wait_ge(s.a_lo, i - 1)
                    if j == 0 and h >= 2:
                        pe.wait_ge(s.o_sum, h - 1)
                    hs = slice(P * h, P * h + P)
                    mm3(bank[6 if h % 2 == 0 else 0][:, :], vH[:, j, hs], vL[:, j, hs], aH[:, (i - 2) % 2, :],
                        aL[:, (i - 2) % 2, :], j == 0, j == TT - 1).then_inc(s.pv_done, 1)
                if i < TT * HEADS and i % TT == 0:
                    h = i // TT
                    if h:
                        pe.wait_ge(s.cross_read, h)
                    for d in range(2):
                        ins = mm3(bank[2 + d][:, :], sH[:, d, h, :], sL[:, d, h, :], qH[:, h, :], qL[:, h, :],
                                  True, True)
                    ins.then_inc(s.cross_done, 1)
                if TT <= i < TT * HEADS and i % TT == 3:
                    o_stat(i // TT - 1)
            for p in range(2):
                have(C_F + p)
                for n in range(2):
                    if p:
                        pe.wait_ge(s.f_lo, n + 1)
                    else:
                        pe.wait_ge(s.cross_read, HEADS)
                    project(bank[2 + n][:, :], p, n, hH, hL, ALL).then_inc(s.mm_done, step(n, 2))
                    if p == n == 0:
                        o_stat(HEADS - 1)
                ada_now()
            have(C_DFT + 1)
            pe.wait_ge(s.csd_lo, 1)
            pe.wait_ge(s.oroot_ready, HEADS)
            for g in range(GROUPS + 1):
                if g < GROUPS:
                    pe.wait_ge(s.f_lo, g + 1)
                    for n in range(2):
                        if g:
                            pe.wait_ge(s.fc_lo, 2 * (g - 1) + n + 1)
                        for half in range(2):
                            ts = slice(P * (2 * n + half), P * (2 * n + half) + P)
                            ins = mm3(bank[n][:, 256 * half:256 * half + 256], fH[:, g, ts], fL[:, g, ts],
                                      csdH[:, :], csdL[:, :], True, True)
                        ins.then_inc(s.fc_done, 1)
                if g:
                    q = g - 1
                    pe.wait_ge(s.fc_lo, 2 * g)
                    if q >= 2:
                        pe.wait_ge(s.mix_lo, q - 1)
                    for part in range(2):
                        for st in range(TT):
                            es = slice(P * part, P * part + P)
                            ss = slice(L * st, L * st + L)
                            ins = mm3(bank[4 + q % 2][:, :], fcH[:, q % 2, st, es], fcL[:, q % 2, st, es],
                                      WH[:, part, ss], WL[:, part, ss], part == st == 0,
                                      part == 1 and st == TT - 1)
                        if q == GROUPS - 1:
                            ins.then_inc(s.mm_done, 17 - GROUPS if part == 0 else 16)
                        elif part:
                            ins.then_inc(s.mm_done, 1)
            for p in range(2):
                have(C_G + p)
                for n in range(2):
                    if p:
                        pe.wait_ge(s.g_silu, n + 1)
                    else:
                        pe.wait_ge(s.fc_lo, 2 * GROUPS)
                    project(bank[n][:, :], p, n, hH, hL, ALL).then_inc(s.mm_done, step(n, 2))
                ada_now()

            def out_stat(m):
                pe.wait_ge(s.ysq_used, 6 * m + 6)
                mm(bank[4][:, :], ones[:, :], sqacc[:, :], start=True, stop=False)
                pe.wait_ge(s.ysq_ready, (m + 1) * KT)
                mm(bank[4][:, :], ones[:, :], scratch[:, 1, :], start=False, stop=True).then_inc(s.ystat_done, 1)

            def x_stats(m):
                for k in range(KT):
                    pe.wait_ge(s.xsq_ready, m * KT + k + 1)
                    mm(bank[5][:, :], ones[:, :], scratch[:, k % 2, :], start=(k == 0), stop=(k == KT - 1))\
                        .then_inc(s.xsq_used, 1)

            def free(t):
                pe.wait_ge(s.bank_free, t - 3)

            def out_phase(m, c0, free0, src_h, src_l, ready, jobs=0):
                for p in range(4):
                    have(c0 + p)
                    for n in range(2):
                        t = 2 * p + n
                        if free0 + t >= 4:
                            free(free0 + t)
                        else:
                            pe.wait_ge(s.g_silu, 4)
                        project(bank[t % 4][:, :], p % 2, n, src_h, src_l, ALL, ready=ready)\
                            .then_inc(s.mm_done, step(n, 2))
                    for _ in range(jobs):
                        ada_now()
                out_stat(m)
                if m < 3:
                    x_stats(m + 1)

            def down_phase(m, c0, free0, ready):
                for p in range(4):
                    for j in range(3):
                        c = c0 + 3 * p + j
                        have(c)
                        ks = [(k, 8 * j + k) for k in range(min(8, FT - 8 * j))]
                        for n in range(2):
                            t = 2 * p + n
                            if j == 0:
                                free(free0 + t)
                            ins = project(bank[t % 4][:, :], c % 2, n, GH, GL, ks, j == 0, j == 2,
                                          ready=(ready, 0) if p == 0 and n == 0 else None)
                            if j == 2:
                                ins.then_inc(s.mm_done, step(n, 2))
                            elif n == 1:
                                ins.then_inc(s.mm_done, 16)
                        if m == 1:
                            a = JOBS_DOWN - 1 + 3 * p + j
                            pe.wait_ge(s.mod_read, 4)
                            ada_sum(a, (a + 1) % 2, lambda jj: slice(2 * a + jj, 2 * a + jj + 1))
                out_stat(m)
                if m < 3:
                    x_stats(m + 1)

            pe.wait_ge(s.mix_lo, KT)
            out_phase(0, C_OUT, B_OUT, mixH, mixL, None, 1)
            with pe.Fori(0, FT // 2) as i:
                for j in range(2):
                    have(2 * i + (C_UP + j))
                    for x in range(2):
                        pe.wait_ge(s.bank_free, 4 * i + (B_UP + 2 * j + x - 3))
                        if j == 0 and x == 0:
                            project(bank[0][:, :], 0, 0, hH, hL, ALL, ready=(s.h_lo, KT)).then_inc(s.mm_done, 1)
                        else:
                            project(bank[2 * j + x][:, :], j, x, hH, hL, ALL).then_inc(s.mm_done, step(x, 2))
                    if j == 0:
                        pe.wait_ge(s.mod_read, 2)
                        ada_sum(i + (JOBS_UP - 1), 1, lambda jj: bass.ds(2 * i + (2 * JOBS_UP - 2 + jj), 1))
            down_phase(1, C_DOWN, B_DOWN, s.ffn_lo)
            for i in range(4):
                have(C_U + i)
                for x in range(2):
                    free(B_U + 2 * i + x)
                    project(bank[2 * (i % 2) + x][:, :], i % 2, x, hH, hL, ALL,
                            ready=(s.h_lo, 2 * KT) if i == x == 0 else None).then_inc(s.mm_done, step(x, 2))
                a = JOBS_DOWN + 11 + i
                ada_sum(a, (a + 1) % 2, lambda jj: slice(2 * a + jj, 2 * a + jj + 1))
            for c0, free0 in ((C_K2, B_K2), (C_V2, B_V2), (C_Q2, B_Q2)):
                for i in range(4):
                    c, n = c0 + i // 2, i % 2
                    if n == 0:
                        have(c)
                    free(free0 + i)
                    if c0 == C_V2:
                        for half in range(2):
                            for k in range(KT):
                                wh, wl = wblock(c % 2, k, 0, 256)
                                ts = slice(P * (2 * n + half), P * (2 * n + half) + P)
                                ins = mm3(bank[i][:, 256 * half:256 * half + 256], hH[:, k, ts], hL[:, k, ts], wh,
                                          wl, k == 0, k == KT - 1)
                    else:
                        ins = project(bank[i][:, :], c % 2, n, hH, hL, ALL)
                    ins.then_inc(s.mm_done, step(n, 2))
            for i in range(16):
                if i % 2 == 0:
                    have(C_GATES + i // 2)
                if i < 4:
                    free(B_MERGE + i)
                else:
                    pe.wait_ge(s.gate_sig, i - 3)
                project(bank[i % 4][:, :], (i // 2) % 2, i % 2, hH, hL, ALL).then_inc(s.mm_done, step(i % 2, 2))
            pe.wait_ge(s.mask_ready, 1)
            pe.wait_ge(s.bank_free, B_MERGE)
            for i in range(4 * NH2 + 4):
                if i < 4 * NH2:
                    h, x = divmod(i, 4)
                    j, w = 3 - x, P * (x + 1)
                    r = slice(64 * (h % 2), 64 * (h % 2) + 64)
                    if i < 4:
                        pe.wait_ge(s.gate_sig, 13 + i)
                    else:
                        pe.wait_ge(s.at_exp, i - 3)
                    z = bank[i % 4]
                    ks, qs = slice(P * j, P * j + P), slice(P * j, L)
                    mm3(z[:, 0:w], k2H[r, h // 2, ks], k2L[r, h // 2, ks], q2H[r, h // 2, qs], q2L[r, h // 2, qs],
                        True, False, True)
                    mm(z[:, 0:P], maskR[:, 0, :], maskR[:, 1, :], start=False, stop=True,
                       skip_group_check=True).then_inc(s.z_done, 1)
                if 0 <= i - 2 < 4 * NH2:
                    k = i - 2
                    x = k % 4
                    pe.wait_ge(s.sp_lo, k + 1)
                    for y in range(x + 1):
                        at, wy = SP_AT[y], P * (y + 1)
                        o = bank[k % 4][:, P * (x - y):P * (x + 1)]
                        lhs = maskR[:, 2 if y == x else 3, :]
                        mm(o, lhs, spH[:, at:at + wy], start=False, stop=False, skip_group_check=True)
                        ins = mm(o, lhs, spL[:, at:at + wy], start=False, stop=(y == x), skip_group_check=True)
                    ins.then_inc(s.arg_done, 1)
                if i >= 4:
                    k = i - 4
                    h, x = divmod(k, 4)
                    pe.wait_ge(s.at_lo, k + 1)
                    if x == 0 and h >= 2:
                        pe.wait_ge(s.o2_lo, h - 1)
                    hs = slice(P * (h // 2), P * (h // 2) + P)
                    w = P * (x + 1)
                    mm3(bank[4 + h % 2][:, L - w:L], v2H[:, 3 - x, hs], v2L[:, 3 - x, hs], atH[:, k % 2, 0:w],
                        atL[:, k % 2, 0:w], x == 0, x == 3, True).then_inc(s.pv2_done, 1)
            pe.wait_ge(s.conv_tap, TAPS * CT)
            for k in range(CT):
                ins = mm(bank[6][:, :], ones[:, :], cacc[:, k, :], start=(k == 0), stop=(k == CT - 1))
            ins.then_inc(s.lnsum_done, 1)
            for k in range(CT):
                pe.wait_ge(s.lnsq_ready, k + 1)
                if k == 0:
                    pe.wait_ge(s.o2_lo, NH2)
                mm(bank[5][:, :], ones[:, :], scratch[:, k % 2, :], start=(k == 0), stop=(k == CT - 1))\
                    .then_inc(s.lnsq_used if k < CT - 1 else s.lnvar_done, 1)
            pe.wait_ge(s.at_exp, 4 * NH2)
            pe.wait_ge(s.c_lo, CT)
            for p in range(4):
                have(C_MERGE + p)
                for x in range(2):
                    for y in range(2):
                        free(B_MERGE + 4 * p + 2 * x + y) if 4 * p + 2 * x + y >= 4 else None
                        src = (cH, cL) if y == 0 else (q2H, q2L)
                        ins = project(bank[2 * x + y][:, :], p % 2, x, *src, [(4 * y + k, k) for k in range(4)])
                    ins.then_inc(s.mm_done, step(x, 2))
            out_phase(2, C_O, B_O, mgH, mgL, (s.mg_lo, 0))
            with pe.Fori(0, FT // 2) as i:
                for j in range(2):
                    have(2 * i + (C_UP2 + j))
                    for x in range(2):
                        pe.wait_ge(s.bank_free, 4 * i + (B_UP2 + 2 * j + x - 3))
                        project(bank[2 * j + x][:, :], j, x, hH, hL, ALL,
                                ready=(s.h_lo, 3 * KT) if j == x == 0 else None).then_inc(s.mm_done, step(x, 2))
            down_phase(3, C_DOWN2, B_DOWN2, s.ffn2_lo)


def tiles(w, cols):
    k = w.shape[0] // P
    return np.concatenate([w[:, c].reshape(k, P, -1) for c in cols], axis=2).transpose(1, 0, 2)


def col(i, width=P):
    return slice(i * width, (i + 1) * width)


def weight_stream(w_in, w_out, w_up, w_down, w_in2, w_conv, w_att, w_o, w_ffn_in, w_ffn_out, dft):
    out = np.zeros((N_CHUNKS, P, CH), np.float32)

    def put(c, w, cols, at=0):
        t = tiles(w, cols)
        out[c, :, at:at + t.shape[1] * 256] = t.reshape(P, -1)

    for p in range(2):
        put(2 * p, w_in, [col(2 + p, 256)])
        put(2 * p + 1, w_in, [col(4 + p, 256)])
        put(C_Q + p, w_in, [col(p, 256)])
        put(C_F + p, w_in, [col(8 + p, 256)])
        out[C_DFT + p] = dft[p].reshape(TT, P, L).transpose(1, 0, 2).reshape(P, -1)
        put(C_G + p, w_in, [col(6 + p, 256)])
    for p in range(4):
        put(C_OUT + p, w_out, [col(p, 256)])
        put(C_MERGE + p, w_conv, [col(p, 256)])
        put(C_MERGE + p, w_att, [col(p, 256)], CH // 2)
        put(C_O + p, w_o, [col(p, 256)])
        put(C_U + p, w_in2, [col(p), col(4 + p)])
        for j in range(3):
            rows = slice(8 * j * P, min(8 * j + 8, FT) * P)
            put(C_DOWN + 3 * p + j, w_down[rows], [col(p, 256)])
            put(C_DOWN2 + 3 * p + j, w_ffn_out[rows], [col(p, 256)])
    for t in range(FT):
        put(C_UP + t, w_up, [col(t), col(FT + t)])
        put(C_UP2 + t, w_ffn_in, [col(t), col(FT + t)])
    for p in range(2):
        put(C_Q2 + p, w_in2, [col(4 + p, 256)])
        put(C_K2 + p, w_in2, [col(6 + p, 256)])
        put(C_V2 + p, w_in2, [col(8 + p, 256)])
    for p in range(8):
        put(C_GATES + p, w_in2, [col(10 + p, 256)])
    return out


def tables():
    f32 = np.float32
    n_freq = HD // 4
    freqs = (f32(10000.0) ** (-np.arange(n_freq, dtype=f32) / f32(n_freq))).astype(f32)
    t = np.arange(L)
    ang = np.concatenate([(t // ROW).astype(f32)[:, None] * freqs, (t % ROW).astype(f32)[:, None] * freqs], 1)
    cos, sin = np.cos(ang).T, np.sin(ang).T
    rope = np.stack([np.concatenate([cos, cos]), np.concatenate([-sin, sin])], 1).astype(f32)
    band = (np.arange(BAND)[None, :] - np.arange(P)[:, None] - (TT - 1) * P).astype(f32)
    pos = np.broadcast_to(np.arange(1, L + 1, dtype=f32), (P, L)).copy()
    e = np.outer(np.arange(P), np.arange(P)) % P * (2 * np.pi / P)
    csd = (np.concatenate([np.cos(e), np.sin(e)], 1) / 256.0).astype(f32)
    a = np.outer(np.arange(L), np.arange(L)) % L * (2 * np.pi / L)
    dft = np.stack([np.cos(a), -np.sin(a)]).astype(f32)
    key, query = np.arange(P)[:, None], np.arange(P)[None, :]
    masks = np.stack([np.eye(P), np.where(key >= query, NEG, 0.0), np.where(key >= query, -1.0, 0.0),
                      -np.ones((P, P))], 1).astype(f32)
    return rope, band, pos, csd, dft, masks


def kernel(x, c, ctx, c_ctx, w_ada, b_ada, g_mix_pre, g_mix_post, g_ffn_pre, g_ffn_post, w_in,
           ret_decay_fwd, ret_decay_bwd, w_out, w_up, conv_w, conv_b, w_down, c_2, ada_w_2, ada_b_2,
           pre_mix_g_2, post_mix_g_2, pre_ffn_g_2, post_ffn_g_2, w_in_2, conv_w_2, conv_b_2,
           conv_ln_g_2, conv_ln_b_2, w_conv_out_2, w_att_out_2, w_o_2, w_ffn_in_2, w_ffn_out_2):
    import concourse.bacc as bacc
    from concourse.bass_utils import run_bass_kernel_spmd

    def vt(a):
        return np.asarray(a).reshape(-1, P).T

    def feature_major(a, n):
        return np.ascontiguousarray(np.asarray(a).reshape(n, KT, P).transpose(2, 1, 0))

    rope, band, pos, csd, dft, masks = tables()
    decays = np.concatenate([np.asarray(ret_decay_fwd)[0], np.asarray(ret_decay_bwd)[0]])
    m = np.arange(LC, dtype=np.float32).reshape(TC, P).T
    vecs = np.concatenate(
        [vt(c), vt(c_ctx), vt(c_2), vt(b_ada), vt(ada_b_2), vt(g_mix_pre), vt(g_mix_post), vt(g_ffn_pre),
         vt(g_ffn_post), vt(pre_mix_g_2), vt(post_mix_g_2), vt(pre_ffn_g_2), vt(post_ffn_g_2), vt(conv_w),
         vt(conv_b), vt(conv_w_2), vt(conv_b_2), vt(conv_ln_g_2), vt(conv_ln_b_2),
         np.broadcast_to(decays, (P, 2 * HEADS)), LC - 1 - m, m], axis=1)
    stream = weight_stream(*(np.asarray(w)[0] for w in (w_in, w_out, w_up, w_down, w_in_2, w_conv_out_2,
                                                        w_att_out_2, w_o_2, w_ffn_in_2, w_ffn_out_2)), dft)
    ada = np.stack([tiles(np.asarray(w)[0], [col(i, 256)]).reshape(P, CH) for w in (w_ada, ada_w_2)
                    for i in range(24)])
    arrays = {"weights": stream, "ada": ada, "x_t": feature_major(x, L), "ctx_t": feature_major(ctx, LC),
              "vecs": vecs, "rope": rope, "band": band, "pos": pos, "csd": csd, "masks": masks}
    arrays = {k: np.ascontiguousarray(a) for k, a in arrays.items()}
    nc = bacc.Bacc("TRN2", target_bir_lowering=False, num_devices=1, dynamic_dma_scratch_size=1024)
    args = {k: nc.dram_tensor(k, a.shape, mybir.dt.float32, kind="ExternalInput").ap() for k, a in arrays.items()}
    out = nc.dram_tensor("out_t", (P, KT, L), mybir.dt.float32, kind="ExternalOutput").ap()
    build(nc, out=out, **args)
    r = run_bass_kernel_spmd(nc, [arrays], core_ids=[0])
    return r.results[0]["out_t"].transpose(2, 1, 0).reshape(1, L, D)
```

```python
from contextlib import ExitStack

import numpy as np
import concourse.bass as bass
from concourse import mybir

P = 128
D, L, LC = 1024, 512, 256
KT = D // P
TT, TC = L // P, LC // P
HEADS, HD = 4, 128
RET = HEADS * HD
GROUPS = 4
FF = ((8 * D // 3 + 127) // 128) * 128
FT = FF // P
ROW = 64
NH2, HD2 = 8, 64
CW = 512
CT = CW // P
TAPS = 31
EPS = 1e-6
CH = 2048
NEG = -1e30

C_KV, C_Q, C_F, C_DFT, C_G = 0, 4, 6, 8, 10
C_OUT = 12
C_UP = 16
C_DOWN = C_UP + FT
C_U = C_DOWN + 12
C_K2, C_V2, C_Q2, C_GATES = C_U + 4, C_U + 6, C_U + 8, C_U + 10
C_MERGE = C_GATES + 8
C_O = C_MERGE + 4
C_UP2 = C_O + 4
C_DOWN2 = C_UP2 + FT
N_CHUNKS = C_DOWN2 + 12
ADA_FIRST = 8
ADA_LATER = 40
JOBS_UP = 14
JOBS_DOWN = JOBS_UP + FT // 2

VECS = [("c", KT), ("cc", KT), ("c2", KT), ("b_ada", 48), ("b_ada2", 48), ("g0", KT), ("p0", KT), ("g1", KT),
        ("p1", KT), ("g2", KT), ("p2", KT), ("g3", KT), ("p3", KT), ("cw", 3 * 2 * FT), ("cb", 2 * FT),
        ("cw2", TAPS * CT), ("cb2", CT), ("lng", CT), ("lnb", CT), ("dec", 2 * HEADS), ("mpos", 2 * TC)]
VAT = {}
_at = 0
for _n, _w in VECS:
    VAT[_n] = _at
    _at += _w
NV = _at
B_OUT, B_UP = 0, KT
B_DOWN = B_UP + 2 * FT
B_U = B_DOWN + KT
B_K2, B_V2, B_Q2, B_MERGE = B_U + 8, B_U + 12, B_U + 16, B_U + 20
B_O = B_MERGE + 16
B_UP2 = B_O + KT
B_DOWN2 = B_UP2 + 2 * FT
SHIFT_AT, SCALE_AT, GATE_AT = {1: 8, 2: 32, 3: 56}, {1: 16, 2: 40, 3: 64}, {0: 0, 1: 24, 2: 48, 3: 72}
Z_BANKS = (0, 1, 2, 3, 6, 7)
SP_AT = (0, P, 3 * P, 6 * P)
POOL_TILES, DVE_TILES = (2, 5), (0, 1, 3, 4, 6, 7)
BAND = L + (TT - 1) * P


def build(nc, weights, ada, x_t, ctx_t, vecs, rope, band, pos, csd, masks, out):
    F, R = mybir.dt.float32, mybir.dt.float32r
    ALU, ACT = mybir.AluOpType, mybir.ActivationFunctionType
    mult, add, sub = ALU.mult, ALU.add, ALU.subtract
    stack = ExitStack()
    with stack:
        KB = 1024
        base = [(nc.sbuf_base + 31) // 32 * 32]

        def fix(name, shape, dt=F):
            size = int(np.prod(shape[1:])) * 4
            t = nc.alloc_sbuf_tensor_at(name, shape, dt, offset=base[0])
            base[0] += (size + 31) // 32 * 32
            return t

        def over(name, shape, at, dt=F):
            return nc.alloc_sbuf_tensor_at(name, shape, dt, offset=int(at))

        xT = fix("xT", [P, KT, L])
        H0 = base[0]
        hH, hL = fix("hH", [P, KT, L], R), fix("hL", [P, KT, L], R)
        raw = fix("raw", [P, 2, CH])
        WH, WL = fix("WH", [P, 2, CH], R), fix("WL", [P, 2, CH], R)
        ada_half = fix("ada_half", [P, 2, CH // 2])
        vec = fix("vec", [P, NV])
        ones = fix("ones", [P, P])
        csil = fix("csil", [P, KT, 2])
        csil2 = fix("csil2", [P, KT])
        csil_up = fix("csil_up", [P, FT // 2, KT])
        rstd = fix("rstd", [P, L])
        scratch = fix("scratch", [P, 2, L])
        ada_acc = fix("ada_acc", [P, 2, 256])
        mod0 = fix("mod0", [P, 16, 2])
        mod = fix("mod", [P, 2 * ADA_LATER])
        gm = fix("gm", [P, 2, KT])
        gp = fix("gp", [P, KT])
        lg = fix("lg", [P, 3, 2 * HEADS])
        eps = fix("eps", [P, 1])
        ident2 = fix("ident2", [2, 2])
        zeta = fix("zeta", [P, 2, HEADS, TC])
        U = base[0]
        adaf = over("adaf", [P, ADA_FIRST, CH], U)
        kH, kL = over("kH", [P, HEADS, L], U, R), over("kL", [P, HEADS, L], U + 8 * KB, R)
        vF = over("vF", [P, TT, RET], U + 16 * KB)
        qH, qL = over("qH", [P, HEADS, L], U + 32 * KB, R), over("qL", [P, HEADS, L], U + 40 * KB, R)
        ktmp = over("ktmp", [P, 4, L], U + 32 * KB)
        tmp0 = over("tmp0", [P, 4, L], U + 32 * KB)
        kctmp = over("kctmp", [P, 2, 256], U + 40 * KB)
        sH, sL = over("sH", [P, 2, HEADS, P], U + 48 * KB, R), over("sL", [P, 2, HEADS, P], U + 52 * KB, R)
        hcH, hcL = over("hcH", [P, KT, LC], U + 56 * KB, R), over("hcL", [P, KT, LC], U + 64 * KB, R)
        qtmp = over("qtmp", [P, 4, L], U + 56 * KB)
        kcH, kcL = over("kcH", [P, TC, 2, 256], U + 72 * KB, R), over("kcL", [P, TC, 2, 256], U + 76 * KB, R)
        m0row = over("m0row", [2, 16 * P], U + 64 * KB)
        csd_in = over("csd_in", [P, 256], U + 72 * KB)
        ctxT = over("ctxT", [P, KT, LC], U + 76 * KB)
        vcH, vcL = over("vcH", [P, TC, 256], U + 80 * KB, R), over("vcL", [P, TC, 256], U + 82 * KB, R)
        csqacc = over("csqacc", [P, LC], U + 96 * KB)
        crstd = over("crstd", [P, LC], U + 97 * KB)
        ropeT = over("ropeT", [P, 2, L], U + 84 * KB)
        bandT = over("bandT", [P, BAND], U + 88 * KB)
        posT = over("posT", [P, L], U + 91.5 * KB)
        csdH, csdL = over("csdH", [P, 256], U + 93.5 * KB, R), over("csdL", [P, 256], U + 94.5 * KB, R)
        decay = (over("decay0", [P, BAND], U + 96 * KB), over("decay1", [P, BAND], U + 56 * KB))
        sqacc = over("sqacc", [P, L], U + 99.5 * KB)
        sqmore = over("sqmore", [P, L], U + 101.5 * KB)
        squares = (scratch[:, 0, :], scratch[:, 1, :], sqacc[:, :], sqmore[:, :])
        xi = over("xi", [P, 2, L], U + 59.5 * KB)
        aF = over("aF", [P, 4, L], U + 63.5 * KB)
        comb = over("comb", [P, L], U + 75.5 * KB)
        oT = over("oT", [P, HEADS, L], U + 77.5 * KB)
        fH, fL = over("fH", [P, GROUPS, L], U, R), over("fL", [P, GROUPS, L], U + 8 * KB, R)
        fcH, fcL = over("fcH", [P, 2, TT, 256], U + 16 * KB, R), over("fcL", [P, 2, TT, 256], U + 24 * KB, R)
        mixH, mixL = over("mixH", [P, KT, L], U + 32 * KB, R), over("mixL", [P, KT, L], U + 48 * KB, R)
        GH, GL = over("GH", [P, FT, L], U, R), over("GL", [P, FT, L], U + 44 * KB, R)
        tmp1 = over("tmp1", [P, 4, L], U)
        tA, tB = over("tA", [P, 2, L], U + 88 * KB), over("tB", [P, 2, L], U + 92 * KB)
        yT = over("yT", [P, KT, L], H0)
        uT, cacc = over("uT", [P, CT, L], U), over("cacc", [P, CT, L], U + 8 * KB)
        q2H, q2L = over("q2H", [P, 4, L], U + 16 * KB, R), over("q2L", [P, 4, L], U + 24 * KB, R)
        k2H, k2L = over("k2H", [P, 4, L], U + 32 * KB, R), over("k2L", [P, 4, L], U + 40 * KB, R)
        v2F = over("v2F", [P, TT, CW], U + 48 * KB)
        gates = over("gates", [P, 16, L], U + 64 * KB)
        mgH, mgL = over("mgH", [P, KT, L], U + 64 * KB, R), over("mgL", [P, KT, L], U + 80 * KB, R)
        spH = (over("spH0", [P, 1280], H0, R), over("spH1", [P, 1280], U + 96 * KB, R))
        spL = (over("spL0", [P, 1280], H0 + 5 * KB, R), over("spL1", [P, 1280], U + 101 * KB, R))
        atF = over("atF", [P, 4, L], H0 + 10 * KB)
        maskR = over("maskR", [P, 4, P], U + 56 * KB, R)
        sptmp = over("sptmp", [P, 2, L], H0 + 20 * KB)
        spF = over("spF", [P, 2, L], H0 + 24 * KB)
        mask_in = over("mask_in", [P, 4, P], U + 58 * KB)
        lnsq = over("lnsq", [P, CT, L], U + 96 * KB)
        cH, cL = over("cH", [P, CT, L], U, R), over("cL", [P, CT, L], U + 8 * KB, R)
        assert U + 106 * KB <= nc.sbuf_usable_end, (U, nc.sbuf_usable_end)

        bank = [stack.enter_context(nc.psum_tensor(f"bank{i}", [P, 512], F)) for i in range(8)]
        sems = {}

        class Sems:
            def __getattr__(self, name):
                if name not in sems:
                    sems[name] = stack.enter_context(nc.semaphore(name))
                return sems[name]

        s = Sems()

        adaf_in = [stack.enter_context(nc.semaphore(f"adaf{i}_in")) for i in range(ADA_FIRST)]
        raw_in = [stack.enter_context(nc.semaphore(f"raw{i}_in")) for i in range(2)]
        ada_in = [stack.enter_context(nc.semaphore(f"ada_half{i}_in")) for i in range(2)]

        def v(name, i, n=1):
            return vec[:, VAT[name] + i:VAT[name] + i + n]

        def step(n, of):
            return 1 if n < of - 1 else 17 - of

        def done(c, n, of):
            return 16 * c + (n + 1 if n < of - 1 else 16)

        def dft_done(g):
            return (16 * C_DFT + 1, 16 * C_DFT + 2, 16 * (C_DFT + 1) + 1, 16 * (C_DFT + 2))[g]

        def x_ready(eng, m, k):
            if k in POOL_TILES:
                eng.wait_ge(s.x_new_pool, len(POOL_TILES) * m + POOL_TILES.index(k) + 1)
            else:
                eng.wait_ge(s.x_new, len(DVE_TILES) * m + DVE_TILES.index(k) + 1)

        def x_ready_all(eng, m):
            x_ready(eng, m, POOL_TILES[-1])
            x_ready(eng, m, DVE_TILES[-1])

        block = stack.enter_context(nc.Block())

        class Chain:
            def __init__(self, eng, sem):
                self.eng, self.sem, self.n, self.extra = eng, sem, 0, None

            def link(self, ins):
                self.n += 1
                ins.then_inc(self.sem, 1)
                self.eng.wait_ge(self.sem, self.n if self.extra is None else self.extra + self.n)

            def enter(self, i, per):
                self.extra, self.start, self.per = i * per, self.n, per

            def leave(self, passes):
                assert self.n - self.start == self.per, self.n - self.start
                self.n, self.extra = self.start + passes * self.per, None

        @block.sync
        def _(sp):
            sp.dma_start(vec[:, :], vecs).then_inc(s.vec_in, 16)
            sp.dma_start(ctxT[:, :, :], ctx_t).then_inc(s.ctx_in, 16)
            sp.dma_start(ident2[:, :], masks[0:2, 0, 0:2]).then_inc(s.ident2_in, 16)
            for i in range(ADA_FIRST):
                sp.dma_start(adaf[:, i, :], ada[i]).then_inc(adaf_in[i], 16)
                if i == 1:
                    for j in range(2):
                        half = slice(j * KT // 2, (j + 1) * KT // 2)
                        sp.dma_start(xT[:, half, :], x_t[:, half, :]).then_inc(s.x_in, 16)
            sp.dma_start(csd_in[:, :], csd).then_inc(s.csd_in, 16)
            for j in range(2):
                sp.dma_start(raw[:, j, :], weights[j]).then_inc(raw_in[j], 16)
            for j in range(2):
                sp.dma_start(ada_half[:, j, :], ada[ADA_FIRST, :, j * (CH // 2):(j + 1) * (CH // 2)])\
                    .then_inc(ada_in[j], 16)
            sp.dma_start(ropeT[:, :, :], rope).then_inc(s.rope_in, 16)
            sp.dma_start(bandT[:, :], band).then_inc(s.band_in, 16)
            sp.dma_start(posT[:, :], pos).then_inc(s.pos_in, 16)

            def load_chunk(c, slot):
                sp.wait_ge(s.lo_done, c - 1)
                sp.dma_start(raw[:, slot, :], weights[c]).then_inc(raw_in[slot], 16)

            def load_half_job(a, j):
                sp.wait_ge(s.ada_read, 2 * a + (j - 1))
                sp.dma_start(ada_half[:, j, :], ada[a + ADA_FIRST, :, j * (CH // 2):(j + 1) * (CH // 2)])\
                    .then_inc(ada_in[j], 16)

            def load_job(a):
                for j in range(2):
                    load_half_job(a, j)

            job = 1
            for c in range(2, C_UP + 3):
                load_chunk(c, c % 2)
                if c == 2 or c - 2 in (C_DFT + 1, C_G):
                    continue
                load_job(job)
                job += 1
            assert job == JOBS_UP + 1, job
            load_chunk(C_UP + 3, 1)
            with sp.Fori(0, FT // 2) as i:
                for j in range(2):
                    load_chunk(2 * i + (C_UP + 4 + j), j)
                    load_half_job(i + JOBS_UP + 1, j)
            load_job(JOBS_DOWN + 1)
            with sp.Fori(0, 6) as i:
                for j in range(2):
                    load_chunk(2 * i + (C_DOWN + 4 + j), j)
                    load_job(2 * i + (JOBS_DOWN + 2 + j))
            load_chunk(C_DOWN + 16, 0)
            load_job(ADA_LATER - 1)
            load_chunk(C_DOWN + 17, 1)
            sp.wait_ge(s.mm_done, 16 * C_U)
            sp.dma_start(mask_in[:, :, :], masks).then_inc(s.mask_in, 16)
            with sp.Fori((C_DOWN + 18) // 2, (C_MERGE + 2) // 2) as i:
                for j in range(2):
                    load_chunk(2 * i + j, j)
            with sp.Fori((C_MERGE + 2) // 2, N_CHUNKS // 2) as i:
                for j in range(2):
                    load_chunk(2 * i + j, j)
            for k in range(KT):
                x_ready(sp, 3, k)
                sp.dma_start(out[:, k, :], xT[:, k, :]).then_inc(s.out_done, 16)
            sp.wait_ge(s.out_done, 16 * KT)

        @block.gpsimd
        def _(pool):
            nc.gpsimd.memset(eps[:, :], EPS).then_inc(s.eps_ready, 1)
            nc.gpsimd.memset(ones[:, :], 1.0).then_inc(s.ones_ready, 1)
            for m, free0 in enumerate((B_OUT, B_DOWN, B_O, B_DOWN2)):
                pool.wait_ge(s.root_ready, m + 1)
                pool.wait_ge(s.bank_free, free0 + KT)
                for i, k in enumerate(POOL_TILES):
                    nc.gpsimd.tensor_tensor(yT[:, k, :], yT[:, k, :], rstd[:, :], mult)\
                        .then_inc(s.y_pool, 1)
                    pool.wait_ge(s.y_pool, len(POOL_TILES) * m + i + 1)
                    nc.gpsimd.tensor_tensor(xT[:, k, :], yT[:, k, :], xT[:, k, :], add)\
                        .then_inc(s.x_new_pool, 1)

        @block.scalar
        def _(act):
            A = nc.scalar.activation
            own = Chain(act, s.act_own)

            def split_hi(c, slot, first=False):
                act.wait_ge(raw_in[slot], c * 8 + 16 - 8 * slot)
                if not first:
                    act.wait_ge(s.mm_done, 16 * c - 16)
                A(WH[:, slot, :], raw[:, slot, :], ACT.Copy).then_inc(s.hi_done, 1)

            def norm_hi(m, tmp, hi, width, mul_s, done_s, shift):
                for k in range(KT):
                    act.wait_ge(mul_s, m * KT + k + 1)
                    A(hi[:, k, :], tmp[:, k % 4, 0:width], ACT.Identity, bias=shift(k)).then_inc(done_s, 1)

            def inverse_root(to, mean_of, scale, ready):
                own.link(A(to, mean_of, ACT.Ln, bias=eps[:, :], scale=scale))
                A(to, to, ACT.Exp, scale=-0.5).then_inc(ready, 1)

            def pin_ln_exp():
                act.preload_act_table_set("natural_log_exp_and_others")

            act.wait_ge(s.vec_in, 16)
            A(csil[:, :, 0], v("c", 0, KT), ACT.Silu).then_inc(s.csil_ready, 1)
            A(csil[:, :, 1], v("cc", 0, KT), ACT.Silu).then_inc(s.csil_ready, 1)
            A(csil2[:, :], v("c2", 0, KT), ACT.Silu).then_inc(s.csil_ready, 1)
            pin_ln_exp()
            act.wait_ge(s.ctx_in, 16)
            for k in range(KT):
                if k >= 3:
                    act.wait_ge(s.csq_used, k - 2)
                A(scratch[:, k % 2, 0:LC] if k else csqacc[:, :], ctxT[:, k, :], ACT.Square).then_inc(s.csq_ready, 1)
            act.wait_ge(s.x_in, 32)
            for k in range(KT):
                if k == 1:
                    act.wait_ge(s.csq_used, KT - 1)
                if k >= 3:
                    act.wait_ge(s.xsq0_used, k - 2)
                A(scratch[:, k % 2, :] if k else sqacc[:, :], xT[:, k, :], ACT.Square).then_inc(s.xsq0_ready, 1)

            def squares_of_x(m):
                for k in range(KT):
                    x_ready(act, m - 1, k)
                    if k < 4:
                        act.wait_ge(s.ystat_done, m)
                    else:
                        act.wait_ge(s.xsq_used, (m - 1) * KT + k - 3)
                    A(squares[k % 4], xT[:, k, :], ACT.Square).then_inc(s.xsq_ready, 1)

            act.wait_ge(s.cstat_done, 1)
            act.wait_ge(s.eps_ready, 1)
            inverse_root(crstd[:, :], bank[6][:, 0:LC], 1.0 / D, s.croot_ready)
            act.wait_ge(s.lg_abs, 1)
            own.link(A(lg[:, 1, :], lg[:, 1, :], ACT.Exp))
            A(lg[:, 1, :], lg[:, 1, :], ACT.Ln, bias=1.0).then_inc(s.lg_ln, 1)
            act.wait_ge(s.lg_ready, 1)
            for d in range(2):
                for h in range(HEADS):
                    A(zeta[:, d, h, :], v("mpos", d * TC, TC), ACT.Exp,
                      scale=lg[:, 0, d * HEADS + h:d * HEADS + h + 1]).then_inc(s.zeta_exp, 1)
            act.wait_ge(s.xstat_done, 1)
            inverse_root(rstd[:, :], bank[5][:, :], 1.0 / D, s.xroot_ready)
            for q in range(4):
                act.wait_ge(s.mod0_sum, 2 * q + 2)
                A(m0row[:, 4 * P * q:4 * P * (q + 1)], bank[q][0:2, :], ACT.Copy).then_inc(s.mod0_row, 1)
                if q == 2:
                    act.wait_ge(s.csd_in, 16)
                    A(csdH[:, :], csd_in[:, :], ACT.Copy).then_inc(s.csd_hi, 1)
                    split_hi(0, 0, True)
            act.wait_ge(s.mod0_ready, 2)
            norm_hi(0, tmp0, hH, L, s.norm_mul, s.h_hi, lambda k: mod0[:, k, 0:1])
            norm_hi(0, tmp0, hcH, LC, s.cnorm_mul, s.hc_hi, lambda k: mod0[:, k, 1:2])
            act.wait_ge(s.hc_lo, KT)

            def rope_tile(i, tmp, pb, dst, head, done, swapped, summed, hi):
                act.wait_ge(s.mm_done, done)
                if i >= 2:
                    act.wait_ge(summed, i - 1)
                A(tmp[0:64, i % 2, :], pb[64:128, :], ACT.Copy)
                A(tmp[64:128, i % 2, :], pb[0:64, :], ACT.Copy).then_inc(swapped, 1)
                act.wait_ge(summed, i + 1)
                A(dst[:, head, :], tmp[:, 2 + i % 2, :], ACT.Copy).then_inc(hi, 1)

            def states_hi(p):
                act.wait_ge(s.state_done, p + 1)
                A(sH[:, :, 2 * p:2 * p + 2, :],
                  bank[3][:, :].rearrange("p (d h e) -> p d h e", d=2, h=2), ACT.Copy).then_inc(s.state_hi, 1)

            for p in range(2):
                split_hi(2 * p + 1, 1, p == 0)
                for n in range(2):
                    rope_tile(2 * p + n, ktmp, bank[n], kH, 2 * p + n, done(2 * p, n, 4), s.k_swap, s.k_sum, s.k_hi)
                if p:
                    states_hi(p - 1)
                for tt in range(TC):
                    act.wait_ge(s.kc_scaled, 2 * p + tt + 1)
                    if p:
                        act.wait_ge(s.state_done, p)
                    A(kcH[:, tt, :, :], kctmp[:, :, :], ACT.Copy).then_inc(s.kc_hi, 1)
                split_hi(2 * p + 2, 0)
                act.wait_ge(s.mm_done, done(2 * p + 1, 2, 3))
                A(vcH[:, :, :], bank[2][:, :].rearrange("p (t e) -> p t e", t=2), ACT.Copy).then_inc(s.vc_hi, 1)
            def decays(h):
                act.wait_ge(s.decay_arg, h + 1)
                A(decay[h % 2][:, :], decay[h % 2][:, :], ACT.Exp).then_inc(s.decay_ready, 1)

            for p in range(2):
                split_hi(C_Q + p + 1, 1 - p)
                for n in range(2):
                    rope_tile(2 * p + n, qtmp, bank[n], qH, 2 * p + n, done(C_Q + p, n, 2), s.q_swap, s.q_sum, s.q_hi)
                if p == 0:
                    states_hi(1)
                else:
                    decays(0)
            def token_decays(h):
                if h:
                    act.wait_ge(s.cross_read, h)
                A(xi[:, 0, :], posT[:, :], ACT.Exp, scale=lg[:, 0, h:h + 1]).then_inc(s.xi_ready, 1)
                A(xi[:, 1, :], posT[:, :], ACT.Exp, scale=lg[:, 1, HEADS + h:HEADS + h + 1],
                  bias=lg[:, 2, HEADS + h:HEADS + h + 1]).then_inc(s.xi_ready, 1)

            def o_square(h):
                act.wait_ge(s.o_sum, h + 1)
                A(scratch[:, 1, :], oT[:, h, :], ACT.Square).then_inc(s.osq_ready, 1)

            def o_root(h):
                act.wait_ge(s.ostat_done, h + 1)
                if h:
                    act.wait_ge(s.o_norm, h)
                inverse_root(rstd[:, :], bank[1][:, :], 1.0 / HD, s.oroot_ready)

            for i in range(TT * HEADS):
                h, j = divmod(i, TT)
                if i == 0:
                    act.wait_ge(s.q_lo, HEADS)
                    token_decays(0)
                if j == 1 and h < HEADS - 1:
                    decays(h + 1)
                if j == 1 and h:
                    o_square(h - 1)
                if j == 3 and h < HEADS - 1:
                    token_decays(h + 1)
                if j == 3 and h:
                    o_root(h - 1)
            o_square(HEADS - 1)
            for p in range(2):
                split_hi(C_F + p + 1, 1 - p)
                for n in range(2):
                    i = 2 * p + n
                    act.wait_ge(s.mm_done, done(C_F + p, n, 2))
                    A(fH[:, i, :], bank[2 + n][:, :], ACT.Copy).then_inc(s.f_hi, 1)
                    if i == 0:
                        o_root(HEADS - 1)
            for g in range(GROUPS + 1):
                for n in range(2):
                    i = 2 * g + n
                    if g == GROUPS:
                        break
                    act.wait_ge(s.fc_done, i + 1)
                    if g >= 2:
                        act.wait_ge(s.mm_done, dft_done(g - 2))
                    A(fcH[:, g % 2, 2 * n:2 * n + 2, :], bank[n][:, :].rearrange("p (t e) -> p t e", t=2),
                      ACT.Copy).then_inc(s.fc_hi, 1)
                if g == 0:
                    split_hi(C_DFT + 1, 1)
                if g == 3:
                    split_hi(C_G, 0)
                if g:
                    act.wait_ge(s.mm_done, dft_done(g - 1))
                    A(mixH[:, 3 + g, :], bank[4 + (g - 1) % 2][:, :], ACT.Copy).then_inc(s.mix_hi, 1)
            for p in range(2):
                split_hi(C_G + p + 1, 1 - p)
                for n in range(2):
                    i = 2 * p + n
                    act.wait_ge(s.mm_done, done(C_G + p, n, 2))
                    if i >= 2:
                        act.wait_ge(s.mix_lo, GROUPS + i - 1)
                    A(scratch[:, i % 2, :], bank[n][:, :], ACT.Silu).then_inc(s.g_silu, 1)
                    act.wait_ge(s.g_mul, i + 1)
                    A(mixH[:, i, :], scratch[:, i % 2, :], ACT.Copy).then_inc(s.mix_hi, 1)

            def out_squares(m, n, done_at):
                act.wait_ge(s.mm_done, done_at)
                if n >= 3:
                    act.wait_ge(s.ysq_used, 6 * m + n - 2)
                elif m == 0:
                    act.wait_ge(s.mix_lo, KT)
                elif m == 2:
                    act.wait_ge(s.mg_lo, KT)
                to = sqacc[:, :] if n == 0 else scratch[:, n % 2, :]
                A(to, bank[n % 4][:, :], ACT.Square).then_inc(s.ysq_ready, 1)

            def out_root(m):
                act.wait_ge(s.ystat_done, m + 1)
                inverse_root(rstd[:, :], bank[4][:, :], 1.0 / D, s.root_ready)

            def out_norm_square(m, c0):
                pin_ln_exp()
                for p in range(4):
                    split_hi(c0 + p + 1, (p + 1) % 2)
                    for n in range(2):
                        out_squares(m, 2 * p + n, done(c0 + p, n, 2))
                out_root(m)

            def down_square(m, c0, skip):
                pin_ln_exp()
                for p in range(4):
                    for j in range(3):
                        if 3 * p + j != skip:
                            split_hi(c0 + 3 * p + j + 1, (3 * p + j + 1) % 2)
                    for n in range(2):
                        out_squares(m, 2 * p + n, done(c0 + 3 * p + 2, n, 2))
                out_root(m)

            def x_root(m):
                act.wait_ge(s.xsq_used, m * KT)
                x_ready_all(act, m - 1)
                inverse_root(rstd[:, :], bank[5][:, :], 1.0 / D, s.xroot_ready)

            def next_norm(m):
                squares_of_x(m)
                x_root(m)
                act.wait_ge(s.gm_ready, m)
                at = SHIFT_AT[m]
                norm_hi(m, tmp1, hH, L, s.norm_mul, s.h_hi, lambda k: mod[:, at + k:at + k + 1])

            out_norm_square(0, C_OUT)
            next_norm(1)
            act.preload_act_table(ACT.Silu)
            split_hi(C_UP + 1, 1)
            with act.Fori(0, FT // 2) as i:
                for j in range(2):
                    for x, tmp in enumerate((tA, tB)):
                        act.wait_ge(s.mm_done, 32 * i + done(C_UP + j, x, 2))
                        w = VAT["cw"] + 2 * FT + x * FT + j
                        b = VAT["cb"] + x * FT + j
                        A(tmp[:, j, :], bank[2 * j + x][:, :], ACT.Identity, bias=vec[:, bass.ds(2 * i + b, 1)],
                          scale=vec[:, bass.ds(2 * i + w, 1)]).then_inc(s.conv_mid, 1)
                    split_hi(2 * i + (C_UP + j + 2), j)
                    act.wait_ge(s.bank_free, 4 * i + (B_UP + 2 * j + 1))
                    A(tA[:, j, :], tA[:, j, :], ACT.Silu).then_inc(s.ffn_silu, 1)
                    act.wait_ge(s.ffn_mul, 2 * i + j + 1)
                    A(GH[:, bass.ds(2 * i + j, 1), :], tB[:, j:j + 1, :], ACT.Copy).then_inc(s.ffn_hi, 1)
            down_square(1, C_DOWN, 0)
            next_norm(2)
            for i in range(4):
                split_hi(C_U + i + 1, (i + 1) % 2)
                act.wait_ge(s.mm_done, done(C_U + i, 1, 2))
                if i >= 2:
                    act.wait_ge(s.bank_free, B_U + 2 * (i - 1))
                else:
                    act.wait_ge(s.h_lo, 3 * KT)
                A(scratch[:, i % 2, :], bank[2 * (i % 2) + 1][:, :], ACT.Sigmoid).then_inc(s.u_sig, 1)
            for c0, ready in ((C_K2, s.k2_hi), (C_V2, None), (C_Q2, s.q2_hi)):
                for i in range(4):
                    c, n = c0 + i // 2, i % 2
                    if n == 0:
                        split_hi(c + 1, (c + 1) % 2)
                    if c0 == C_V2:
                        continue
                    act.wait_ge(s.mm_done, done(c, n, 2))
                    if c0 == C_K2:
                        A(k2H[:, i, :], bank[i][:, :], ACT.Copy).then_inc(ready, 1)
                    else:
                        A(q2H[:, i, :], bank[i][:, :], ACT.Copy, scale=HD2 ** -0.5).then_inc(ready, 1)
            act.wait_ge(s.mask_in, 16)
            A(maskR[:, :, :], mask_in[:, :, :], ACT.Copy).then_inc(s.mask_ready, 1)
            for p in range(8):
                split_hi(C_GATES + p + 1, (p + 1) % 2)
                for n in range(2):
                    i = 2 * p + n
                    act.wait_ge(s.mm_done, done(C_GATES + p, n, 2))
                    A(gates[:, i, :], bank[i % 4][:, :], ACT.Sigmoid).then_inc(s.gate_sig, 1)
                if p == 6:
                    for k in range(CT):
                        act.wait_ge(s.ln_center, k + 1)
                        A(lnsq[:, k, :], cacc[:, k, :], ACT.Square).then_inc(s.lnsq_ready, 1)
            pin_ln_exp()

            for i in range(4 * NH2 + 4):
                k = i - 4
                z, sp_, w = bank[Z_BANKS[i % 6]], sptmp[:, i % 2, 0:P * (i % 4 + 1)], P * (i % 4 + 1)
                if i < 4 * NH2:
                    act.wait_ge(s.z_done, i + 1)
                    if i >= 2:
                        act.wait_ge(s.sp_sum, i - 1)
                    A(sp_, z[:, 0:w], ACT.Abs).then_inc(s.sp_abs, 1)
                if k >= 0:
                    act.wait_ge(s.arg_done, k + 1)
                    if k == 0:
                        act.wait_ge(s.mask_ready, 1)
                    if k >= 4:
                        act.wait_ge(s.pv2_done, k - 3)
                    A(atF[:, k % 4, 0:w], bank[Z_BANKS[k % 6]][:, 0:w], ACT.Exp).then_inc(s.at_exp, 1)
                if i < 4 * NH2:
                    act.wait_ge(s.sp_abs, i + 1)
                    A(sp_, sp_, ACT.Exp, scale=-1.0).then_inc(s.sp_exp, 1)
                if i < 4 * NH2:
                    act.wait_ge(s.sp_exp, i + 1)
                    A(sp_, sp_, ACT.Ln, bias=1.0).then_inc(s.sp_ln, 1)
                if i == 1:
                    act.wait_ge(s.lnvar_done, 1)
                    inverse_root(rstd[:, :], bank[5][:, :], 1.0 / CW, s.lnroot_ready)
            act.preload_act_table(ACT.Silu)
            act.wait_ge(s.ln_mul, CT)
            for k in range(CT):
                A(cacc[:, k, :], cacc[:, k, :], ACT.Silu, scale=v("lng", k), bias=v("lnb", k)).then_inc(s.c_silu, 1)
            for k in range(CT):
                act.wait_ge(s.c_silu, k + 1)
                A(cH[:, k, :], cacc[:, k, :], ACT.Copy).then_inc(s.c_hi, 1)
            for p in range(4):
                split_hi(C_MERGE + p + 1, (p + 1) % 2)
                for n in (2 * p, 2 * p + 1):
                    act.wait_ge(s.mg_sum, n + 1)
                    A(mgH[:, n, :], scratch[:, 0, :], ACT.Copy).then_inc(s.mg_hi, 1)
            out_norm_square(2, C_O)
            next_norm(3)
            act.preload_act_table(ACT.Silu)
            with act.Fori(0, FT // 2) as i:
                for j in range(2):
                    split_hi(2 * i + (C_UP2 + j + 1), 1 - j)
                    act.wait_ge(s.mm_done, 32 * i + done(C_UP2 + j, 0, 2))
                    A(tA[:, j, :], bank[2 * j][:, :], ACT.Silu).then_inc(s.ffn2_silu, 1)
                    act.wait_ge(s.bank_free, 4 * i + (B_UP2 + 2 * j + 2))
                    A(GH[:, bass.ds(2 * i + j, 1), :], tB[:, j:j + 1, :], ACT.Copy).then_inc(s.ffn2_hi, 1)
            down_square(3, C_DOWN2, 11)

        @block.vector
        def _(dve):
            V = nc.vector
            TT_, TS, STT = V.tensor_tensor, V.tensor_scalar, V.scalar_tensor_tensor
            own = Chain(dve, s.dve_own)

            def split_lo(c, slot):
                dve.wait_ge(s.hi_done, c + 1)
                TT_(WL[:, slot, :], raw[:, slot, :], WH[:, slot, :], sub).then_inc(s.lo_done, 1)

            def ada_half_job(a, slot, half, c_col):
                dve.wait_ge(ada_in[half], 16 * a + 16)
                for k in range(4):
                    w = ada_half[:, half, 256 * k:256 * k + 256]
                    if half == k == 0:
                        ins = TS(ada_acc[:, slot, :], w, c_col(0), None, mult)
                    else:
                        ins = STT(ada_acc[:, slot, :], w, c_col(4 * half + k), ada_acc[:, slot, :], mult, add)
                    if k < 3:
                        own.link(ins)
                    else:
                        ins.then_inc(s.ada_read, 1)
                        dve.wait_ge(s.ada_read, 2 * a + (half + 1))

            def ada_job(a, slot, c_col, first=False):
                if not first:
                    dve.wait_ge(s.ada_summed, a - 1)
                for half in range(2):
                    ada_half_job(a, slot, half, c_col)

            ada_next = [0]

            def ada_now():
                a = ada_next[0]
                ada_next[0] += 1
                ada_job(a, a % 2, (lambda k: csil[:, k, 0:1]) if a < 16 else (lambda k: csil2[:, k:k + 1]), a < 2)

            def norm_lo(m, tmp, src, width, hi, lo, shift, gain, mul_s, hi_s, lo_s, root=rstd):
                for k in range(KT + 2):
                    if k < KT:
                        if k >= 4:
                            dve.wait_ge(lo_s, m * KT + k - 3)
                        STT(tmp[:, k % 4, 0:width], src[:, k, :], gain(k), root[:, 0:width], mult, mult)\
                            .then_inc(mul_s, 1)
                    if k >= 2:
                        q = k - 2
                        dve.wait_ge(hi_s, m * KT + q + 1)
                        STT(lo[:, q, :], tmp[:, q % 4, 0:width], shift(q), hi[:, q, :], add, sub).then_inc(lo_s, 1)

            dve.wait_ge(s.vec_in, 16)
            dec = v("dec", 0, 2 * HEADS)
            STT(lg[:, 1, :], dec, -1.0, dec, mult, ALU.min).then_inc(s.lg_abs, 1)
            own.link(TS(lg[:, 0, :], dec, 0.0, None, ALU.min))
            for acc, width, ready, used in ((csqacc, LC, s.csq_ready, s.csq_used), (sqacc, L, s.xsq0_ready, s.xsq0_used)):
                for k in range(1, KT):
                    dve.wait_ge(ready, k + 1)
                    if k > 1:
                        dve.wait_ge(used, k - 1)
                    TT_(acc[:, :], acc[:, :], scratch[:, k % 2, 0:width], add).then_inc(used, 1)
            dve.wait_ge(s.lg_ln, 1)
            own.link(TT_(lg[:, 0, :], lg[:, 0, :], lg[:, 1, :], sub))
            TS(lg[:, 1, :], lg[:, 0, :], -1.0, None, mult)
            TS(lg[:, 2, :], lg[:, 0, :], float(L + 1), None, mult).then_inc(s.lg_ready, 1)
            dve.wait_ge(s.csil_ready, 3)
            for i in range(FT // 2):
                own.link(V.tensor_copy(csil_up[:, i, :], csil[:, :, 0] if JOBS_UP + i < 16 else csil2[:, :]))
            dve.wait_ge(s.zeta_exp, 2 * HEADS)
            own.link(TS(zeta[:, :, :, :], zeta[:, :, :, :], HD ** -0.5, None, mult))
            dve.wait_ge(s.csd_hi, 1)
            TT_(csdL[:, :], csd_in[:, :], csdH[:, :], sub).then_inc(s.csd_lo, 1)
            split_lo(0, 0)
            dve.wait_ge(s.mod0_done, 4)
            for j in range(2):
                b3 = bank[4][:, 0:32].rearrange("p (n j) -> p n j", j=2)
                own.link(TT_(mod0[:, :, j], b3[:, :, j], v("b_ada", 0, 16), add))
                STT(gm[:, j, :], mod0[:, 8:16, j], 1.0, v("g0", 0, KT), add, mult).then_inc(s.mod0_ready, 1)
            dve.wait_ge(s.mod0_ready, 2)
            dve.wait_ge(s.xroot_ready, 1)
            norm_lo(0, tmp0, xT, L, hH, hL, lambda k: mod0[:, k, 0:1], lambda k: gm[:, 0, k:k + 1],
                    s.norm_mul, s.h_hi, s.h_lo)
            dve.wait_ge(s.h_lo, KT)
            dve.wait_ge(s.croot_ready, 1)
            norm_lo(0, tmp0, ctxT, LC, hcH, hcL, lambda k: mod0[:, k, 1:2], lambda k: gm[:, 1, k:k + 1],
                    s.cnorm_mul, s.hc_hi, s.hc_lo, crstd)
            dve.wait_ge(s.hc_lo, KT)

            def rope_tile(i, tmp, pb, hi, lo, head, done_at, swapped, summed, hi_s, lo_s):
                dve.wait_ge(s.mm_done, done_at)
                if i == 0:
                    dve.wait_ge(s.rope_in, 16)
                dve.wait_ge(swapped, i + 1)
                TT_(tmp[:, 2 + i % 2, :], pb[:, :], ropeT[:, 0, :], mult)
                own.link(TT_(tmp[:, i % 2, :], tmp[:, i % 2, :], ropeT[:, 1, :], mult))
                TT_(tmp[:, 2 + i % 2, :], tmp[:, 2 + i % 2, :], tmp[:, i % 2, :], add).then_inc(summed, 1)
                dve.wait_ge(hi_s, i + 1)
                TT_(lo[:, head, :], tmp[:, 2 + i % 2, :], hi[:, head, :], sub).then_inc(lo_s, 1)

            def states_lo(p):
                dve.wait_ge(s.state_hi, p + 1)
                TT_(sL[:, :, 2 * p:2 * p + 2, :], bank[3][:, :].rearrange("p (d h e) -> p d h e", d=2, h=2),
                    sH[:, :, 2 * p:2 * p + 2, :], sub).then_inc(s.state_lo, 1)

            for p in range(2):
                split_lo(2 * p + 1, 1)
                for n in range(2):
                    rope_tile(2 * p + n, ktmp, bank[n], kH, kL, 2 * p + n, done(2 * p, n, 4), s.k_swap, s.k_sum,
                              s.k_hi, s.k_lo)
                if p:
                    states_lo(p - 1)
                for tt in range(TC):
                    dve.wait_ge(s.mm_done, done(2 * p, 2 + tt, 4))
                    if 2 * p + tt:
                        dve.wait_ge(s.kc_lo, 2 * p + tt)
                    for d in range(2):
                        for h in range(2):
                            ins = TS(kctmp[:, d, P * h:P * h + P], bank[2 + tt][:, P * h:P * h + P],
                                     zeta[:, d, 2 * p + h, tt:tt + 1], None, mult)
                    ins.then_inc(s.kc_scaled, 1)
                    dve.wait_ge(s.kc_hi, 2 * p + tt + 1)
                    TT_(kcL[:, tt, :, :], kctmp[:, :, :], kcH[:, tt, :, :], sub).then_inc(s.kc_lo, 1)
                ada_now()
                split_lo(2 * p + 2, 0)
                for n in range(2):
                    dve.wait_ge(s.mm_done, done(2 * p + 1, n, 3))
                    V.tensor_copy(vF[:, 2 * n:2 * n + 2, 256 * p:256 * p + 256],
                                  bank[n][:, :].rearrange("p (t e) -> p t e", t=2)).then_inc(s.v_read, 1)
                dve.wait_ge(s.vc_hi, p + 1)
                TT_(vcL[:, :, :], bank[2][:, :].rearrange("p (t e) -> p t e", t=2), vcH[:, :, :], sub)\
                    .then_inc(s.vc_lo, 1)
                ada_now()
            def decay_args(h):
                if h >= 2:
                    dve.wait_ge(s.a_mul, TT * (h - 1))
                own.link(TS(decay[h % 2][:, :], bandT[:, :], lg[:, 1, HEADS + h:HEADS + h + 1], None, mult))
                STT(decay[h % 2][:, :], bandT[:, :], lg[:, 0, h:h + 1], decay[h % 2][:, :], mult, ALU.min)\
                    .then_inc(s.decay_arg, 1)

            for p in range(2):
                split_lo(C_Q + p + 1, 1 - p)
                for n in range(2):
                    rope_tile(2 * p + n, qtmp, bank[n], qH, qL, 2 * p + n, done(C_Q + p, n, 2), s.q_swap, s.q_sum,
                              s.q_hi, s.q_lo)
                    if p and n == 0:
                        dve.wait_ge(s.band_in, 16)
                        decay_args(0)
                if p == 0:
                    states_lo(1)
                    ada_now()
            def cross(h):
                dve.wait_ge(s.cross_done, h + 1)
                dve.wait_ge(s.xi_ready, 2 * h + 2)
                if h:
                    dve.wait_ge(s.o_sum, h)
                TT_(comb[:, :], bank[2][:, :], xi[:, 0, :], mult)
                TT_(scratch[:, 0, :], bank[3][:, :], xi[:, 1, :], mult).then_inc(s.cross_read, 1)

            def cross_sum(h):
                dve.wait_ge(s.cross_read, h + 1)
                own.link(TT_(comb[:, :], comb[:, :], scratch[:, 0, :], add))

            def o_add(h):
                dve.wait_ge(s.pv_done, TT * h + TT)
                TT_(oT[:, h, :], bank[6 if h % 2 == 0 else 0][:, :], comb[:, :], add).then_inc(s.o_sum, 1)

            def o_scale(h):
                dve.wait_ge(s.oroot_ready, h + 1)
                TT_(oT[:, h, :], oT[:, h, :], rstd[:, :], mult).then_inc(s.o_norm, 1)

            dve.wait_ge(s.q_lo, HEADS)
            for i in range(TT * HEADS + 1):
                h, j = divmod(i, TT)
                if i < TT * HEADS:
                    if j == 0:
                        dve.wait_ge(s.decay_ready, h + 1)
                    dve.wait_ge(s.s_done, i + 1)
                    if i >= 4:
                        dve.wait_ge(s.pv_done, i - 3)
                    at = (TT - 1 - j) * P
                    STT(aF[:, i % 4, :], bank[4 + i % 2][:, :], HD ** -0.5, decay[h % 2][:, at:at + L], mult, mult)\
                        .then_inc(s.a_mul, 1)
                if j == 0 and h < HEADS - 1:
                    decay_args(h + 1)
                if j == 0 and h >= 2:
                    o_scale(h - 2)
                if j == 1 and h:
                    o_add(h - 1)
                if j == 2:
                    cross(h)
                if j == 3:
                    cross_sum(h)
            o_add(HEADS - 1)
            ada_now()
            for p in range(2):
                split_lo(C_F + p + 1, 1 - p)
                for n in range(2):
                    i = 2 * p + n
                    dve.wait_ge(s.f_hi, i + 1)
                    TT_(fL[:, i, :], bank[2 + n][:, :], fH[:, i, :], sub).then_inc(s.f_lo, 1)
                    if i == 0:
                        o_scale(HEADS - 1)
                if p == 0:
                    ada_now()
            for g in range(GROUPS + 1):
                for n in range(2):
                    i = 2 * g + n
                    if g == GROUPS:
                        break
                    dve.wait_ge(s.fc_hi, i + 1)
                    TT_(fcL[:, g % 2, 2 * n:2 * n + 2, :], bank[n][:, :].rearrange("p (t e) -> p t e", t=2),
                        fcH[:, g % 2, 2 * n:2 * n + 2, :], sub).then_inc(s.fc_lo, 1)
                if g == 0:
                    split_lo(C_DFT + 1, 1)
                if g in (1, 2):
                    a = ada_next[0]
                    if g == 1:
                        dve.wait_ge(s.ada_summed, a - 1)
                    ada_half_job(a, a % 2, g - 1, lambda k: csil[:, k, 0:1])
                    ada_next[0] += g - 1
                if g == 3:
                    split_lo(C_G, 0)
                if g:
                    dve.wait_ge(s.mix_hi, g)
                    TT_(mixL[:, 3 + g, :], bank[4 + (g - 1) % 2][:, :], mixH[:, 3 + g, :], sub).then_inc(s.mix_lo, 1)
            for p in range(2):
                split_lo(C_G + p + 1, 1 - p)
                for n in range(2):
                    i = 2 * p + n
                    dve.wait_ge(s.g_silu, i + 1)
                    TT_(scratch[:, i % 2, :], oT[:, i, :], scratch[:, i % 2, :], mult).then_inc(s.g_mul, 1)
                    dve.wait_ge(s.mix_hi, GROUPS + i + 1)
                    TT_(mixL[:, i, :], scratch[:, i % 2, :], mixH[:, i, :], sub).then_inc(s.mix_lo, 1)
                ada_now()

            def post_gain(m):
                at = GATE_AT[m]
                own.link(TT_(gp[:, :], mod[:, at:at + KT], v(f"p{m}", 0, KT), mult))

            def out_tile(m, n):
                dve.wait_ge(s.ysq_ready, m * KT + n + 1)
                TS(yT[:, n, :], bank[n % 4][:, :], gp[:, n:n + 1], None, mult).then_inc(s.bank_free, 1)
                if 1 <= n < KT - 1:
                    if n > 1:
                        dve.wait_ge(s.ysq_used, 6 * m + n - 1)
                    TT_(sqacc[:, :], sqacc[:, :], scratch[:, n % 2, :], add).then_inc(s.ysq_used, 1)

            def add_and_norm(m, free0):
                dve.wait_ge(s.root_ready, m + 1)
                dve.wait_ge(s.bank_free, free0 + KT)
                if m == 0:
                    modulation(13, 8, 24, 2)
                for k in DVE_TILES:
                    own.link(TT_(yT[:, k, :], yT[:, k, :], rstd[:, :], mult))
                    TT_(xT[:, k, :], xT[:, k, :], yT[:, k, :], add).then_inc(s.x_new, 1)
                if m == 3:
                    return
                at = SCALE_AT[m + 1]
                STT(gm[:, 0, :], mod[:, at:at + KT], 1.0, v(f"g{m + 1}", 0, KT), add, mult).then_inc(s.gm_ready, 1)
                dve.wait_ge(s.gm_ready, m + 1)
                x_ready(dve, m, POOL_TILES[-1])
                dve.wait_ge(s.xroot_ready, m + 2)
                norm_lo(m + 1, tmp1, xT, L, hH, hL, lambda k: mod[:, SHIFT_AT[m + 1] + k:SHIFT_AT[m + 1] + k + 1],
                        lambda k: gm[:, 0, k:k + 1], s.norm_mul, s.h_hi, s.h_lo)

            def out_phase(m, c0, free0, jobs=0):
                post_gain(m)
                for p in range(4):
                    split_lo(c0 + p + 1, (p + 1) % 2)
                    for _ in range(jobs):
                        ada_now()
                    out_tile(m, 2 * p)
                    out_tile(m, 2 * p + 1)
                add_and_norm(m, free0)

            def down_phase(m, c0, free0, skip):
                post_gain(m)
                for p in range(4):
                    for j in range(3):
                        if 3 * p + j != skip:
                            split_lo(c0 + 3 * p + j + 1, (3 * p + j + 1) % 2)
                        a = JOBS_DOWN + 3 * p + j
                        if m == 1:
                            ada_job(a, (a + 1) % 2, lambda k: csil2[:, k:k + 1])
                    out_tile(m, 2 * p)
                    out_tile(m, 2 * p + 1)
                add_and_norm(m, free0)

            def modulation(summed, a, b, read):
                dve.wait_ge(s.ada_summed, summed)
                bias = v("b_ada", 16 + a, b - a) if b <= 32 else v("b_ada2", a - 32, b - a)
                TT_(mod[:, a:b], bank[7][:, a:b], bias, add).then_inc(s.mod_read, 1)
                dve.wait_ge(s.mod_read, read)

            modulation(9, 0, 8, 1)
            out_phase(0, C_OUT, B_OUT, 1)
            assert ada_next[0] == JOBS_UP, ada_next
            split_lo(C_UP + 1, 1)
            with dve.Fori(0, FT // 2) as i:
                own.enter(i, 2 * (2 + 3))
                for j in range(2):
                    views = []
                    for x, tmp in enumerate((tA, tB)):
                        views.append((tmp[:, j, :].rearrange("p (r c) -> p r c", c=ROW),
                                      bank[2 * j + x][:, :].rearrange("p (r c) -> p r c", c=ROW),
                                      VAT["cw"] + x * FT + j))
                    for x, (t, b, w) in enumerate(views):
                        dve.wait_ge(s.conv_mid, 4 * i + (2 * j + x + 1))
                        own.link(STT(t[:, :, 1:ROW], b[:, :, 0:ROW - 1], vec[:, bass.ds(2 * i + w, 1)],
                                     t[:, :, 1:ROW], mult, add))
                    for x, (t, b, w) in enumerate(views):
                        STT(t[:, :, 0:ROW - 1], b[:, :, 1:ROW], vec[:, bass.ds(2 * i + w + 4 * FT, 1)],
                            t[:, :, 0:ROW - 1], mult, add).then_inc(s.bank_free, 1)
                    split_lo(2 * i + (C_UP + j + 2), j)
                    dve.wait_ge(s.bank_free, 4 * i + (B_UP + 2 * j + 2))
                    dve.wait_ge(s.ffn_silu, 2 * i + (j + 1))
                    TT_(tB[:, j, :], tA[:, j, :], tB[:, j, :], mult).then_inc(s.ffn_mul, 1)
                    if j == 0:
                        dve.wait_ge(s.ada_summed, i + JOBS_UP)
                    ada_half_job(i + JOBS_UP, 1, j, lambda k: csil_up[:, bass.ds(i, 1), k])
                    dve.wait_ge(s.ffn_hi, 2 * i + (j + 1))
                    TT_(GL[:, bass.ds(2 * i + j, 1), :], tB[:, j:j + 1, :], GH[:, bass.ds(2 * i + j, 1), :], sub)\
                        .then_inc(s.ffn_lo, 1)
            own.leave(FT // 2)
            modulation(JOBS_DOWN - 1, 24, 32, 3)
            modulation(JOBS_DOWN - 1, 32, 48, 4)
            down_phase(1, C_DOWN, B_DOWN, 0)

            for i in range(4):
                split_lo(C_U + i + 1, (i + 1) % 2)
                dve.wait_ge(s.u_sig, i + 1)
                TT_(uT[:, i, :], bank[2 * (i % 2)][:, :], scratch[:, i % 2, :], mult).then_inc(s.bank_free, 2)
                a = JOBS_DOWN + 12 + i
                if a < ADA_LATER:
                    ada_job(a, (a + 1) % 2, lambda k: csil2[:, k:k + 1])
            modulation(ADA_LATER, 48, 80, 5)

            conv_n = [0]

            def conv_taps(count):
                for _ in range(count):
                    o = conv_n[0]
                    if o == TAPS * CT:
                        return
                    conv_n[0] += 1
                    shift, k = divmod(o, CT)
                    w = v("cw2", (TAPS - 1 - shift) * CT + k)
                    if shift == 0:
                        dve.wait_ge(s.bank_free, B_K2)
                        TS(cacc[:, k, :], uT[:, k, :], w, v("cb2", k), mult, add).then_inc(s.conv_tap, 1)
                    else:
                        dve.wait_ge(s.conv_tap, o - 3)
                        STT(cacc[:, k, shift:L], uT[:, k, 0:L - shift], w, cacc[:, k, shift:L], mult, add)\
                            .then_inc(s.conv_tap, 1)

            for c0, ready in ((C_K2, s.k2_hi), (C_V2, s.mm_done), (C_Q2, s.q2_hi)):
                for i in range(4):
                    c, n = c0 + i // 2, i % 2
                    if n == 0:
                        split_lo(c + 1, (c + 1) % 2)
                        conv_taps(10)
                    dve.wait_ge(ready, done(c, n, 2) if c0 == C_V2 else i + 1)
                    if c0 == C_K2:
                        ins = TT_(k2L[:, i, :], bank[i][:, :], k2H[:, i, :], sub)
                    elif c0 == C_V2:
                        at = slice(256 * (i // 2), 256 * (i // 2) + 256)
                        ins = V.tensor_copy(v2F[:, 2 * n:2 * n + 2, at], bank[i][:, :].rearrange("p (t e) -> p t e", t=2))
                    else:
                        ins = STT(q2L[:, i, :], bank[i][:, :], HD2 ** -0.5, q2H[:, i, :], mult, sub)
                    ins.then_inc(s.bank_free, 1)
            for p in range(8):
                split_lo(C_GATES + p + 1, (p + 1) % 2)
                conv_taps(11)
                if p == 6:
                    assert conv_n[0] == TAPS * CT
                    dve.wait_ge(s.lnsum_done, 1)
                    own.link(TS(rstd[:, :], bank[6][:, :], 1.0 / CW, None, mult))
                    for k in range(CT):
                        TT_(cacc[:, k, :], cacc[:, k, :], rstd[:, :], sub).then_inc(s.ln_center, 1)
            for i in range(4 * NH2 + 6):
                if i == 4:
                    dve.wait_ge(s.lnroot_ready, 1)
                    for k in range(CT):
                        TT_(cacc[:, k, :], cacc[:, k, :], rstd[:, :], mult).then_inc(s.ln_mul, 1)
                if 0 <= i - 1 < 4 * NH2:
                    k = i - 1
                    w = P * (k % 4 + 1)
                    dve.wait_ge(s.sp_ln, k + 1)
                    if k >= 2:
                        dve.wait_ge(s.sp_lo, k - 1)
                    STT(spF[:, k % 2, 0:w], bank[Z_BANKS[k % 6]][:, 0:w], 0.0, sptmp[:, k % 2, 0:w], ALU.max, add)\
                        .then_inc(s.sp_sum, 1)
                    at = SP_AT[k % 4]
                    dve.wait_ge(s.sp_sum, k + 1)
                    slot = k // 4 % 2
                    if k >= 8:
                        dve.wait_ge(s.arg_done, k - k % 4 - 4)
                    V.tensor_copy(spH[slot][:, at:at + w], spF[:, k % 2, 0:w]).then_inc(s.sp_hi, 1)
                    dve.wait_ge(s.sp_hi, k + 1)
                    TT_(spL[slot][:, at:at + w], spF[:, k % 2, 0:w], spH[slot][:, at:at + w], sub)\
                        .then_inc(s.sp_lo, 1)
                if i >= 9 and i % 4 == 1:
                    h = (i - 9) // 4
                    r = 64 * (h % 2)
                    dve.wait_ge(s.pv2_done, 4 * h + 4)
                    V.tensor_copy(q2H[r:r + 64, h // 2, :], bank[4 + h % 2][r:r + 64, :]).then_inc(s.o2_hi, 1)
                    dve.wait_ge(s.o2_hi, h + 1)
                    TT_(q2L[r:r + 64, h // 2, :], bank[4 + h % 2][r:r + 64, :], q2H[r:r + 64, h // 2, :], sub)\
                        .then_inc(s.o2_lo, 1)
            for k in range(CT):
                dve.wait_ge(s.c_hi, k + 1)
                TT_(cL[:, k, :], cacc[:, k, :], cH[:, k, :], sub).then_inc(s.c_lo, 1)
            for p in range(4):
                split_lo(C_MERGE + p + 1, (p + 1) % 2)
                for x in range(2):
                    n = 2 * p + x
                    dve.wait_ge(s.mm_done, done(C_MERGE + p, x, 2))
                    if n:
                        dve.wait_ge(s.mg_lo, n)
                    TT_(scratch[:, 0, :], gates[:, n, :], bank[2 * x][:, :], mult)
                    TT_(scratch[:, 1, :], gates[:, 8 + n, :], bank[2 * x + 1][:, :], mult).then_inc(s.bank_free, 2)
                    dve.wait_ge(s.bank_free, B_MERGE + 2 * (n + 1))
                    TT_(scratch[:, 0, :], scratch[:, 0, :], scratch[:, 1, :], add).then_inc(s.mg_sum, 1)
                    dve.wait_ge(s.mg_hi, n + 1)
                    TT_(mgL[:, n, :], scratch[:, 0, :], mgH[:, n, :], sub).then_inc(s.mg_lo, 1)
            out_phase(2, C_O, B_O)
            with dve.Fori(0, FT // 2) as i:
                for j in range(2):
                    split_lo(2 * i + (C_UP2 + j + 1), 1 - j)
                    dve.wait_ge(s.ffn2_silu, 2 * i + (j + 1))
                    dve.wait_ge(s.mm_done, 32 * i + done(C_UP2 + j, 1, 2))
                    TT_(tB[:, j, :], tA[:, j, :], bank[2 * j + 1][:, :], mult).then_inc(s.bank_free, 2)
                    dve.wait_ge(s.ffn2_hi, 2 * i + (j + 1))
                    TT_(GL[:, bass.ds(2 * i + j, 1), :], tB[:, j:j + 1, :], GH[:, bass.ds(2 * i + j, 1), :], sub)\
                        .then_inc(s.ffn2_lo, 1)
            down_phase(3, C_DOWN2, B_DOWN2, 11)

        @block.tensor
        def _(pe):
            mm = nc.tensor.matmul

            def mm3(o, lh, ll, rh, rl, start, stop, skip=False):
                mm(o, lh, rh, start=start, stop=False, skip_group_check=skip)
                mm(o, lh, rl, start=False, stop=False, skip_group_check=skip)
                return mm(o, ll, rh, start=False, stop=stop, skip_group_check=skip)

            def have(c):
                pe.wait_ge(s.lo_done, c + 1)

            def wblock(slot, k, a, b):
                return WH[:, slot, 256 * k + a:256 * k + b], WL[:, slot, 256 * k + a:256 * k + b]

            def project(o, slot, n, src_h, src_l, ks, start=True, stop=True, ready=None):
                for x, (kb, k) in enumerate(ks):
                    if ready is not None:
                        pe.wait_ge(ready[0], ready[1] + x + 1)
                    wh, wl = wblock(slot, kb, P * n, P * n + P)
                    ins = mm3(o, wh, wl, src_h[:, k, :], src_l[:, k, :], start and x == 0, stop and x == len(ks) - 1)
                return ins

            def project_pair(slot, src_h, src_l, ks, ready, of):
                for x, (kb, k) in enumerate(ks):
                    pe.wait_ge(ready[0], ready[1] + x + 1)
                    for n in range(2):
                        wh, wl = wblock(slot, kb, P * n, P * n + P)
                        ins = mm3(bank[n][:, :], wh, wl, src_h[:, k, :], src_l[:, k, :], x == 0, x == len(ks) - 1)
                        if x == len(ks) - 1:
                            ins.then_inc(s.mm_done, step(n, of))

            ALL = [(k, k) for k in range(KT)]
            ada_next = [0]

            def ada_sum(a, slot, col):
                pe.wait_ge(s.ada_read, 2 * a + 2)
                for j in range(2):
                    ins = mm(bank[7][:, col(j)], ada_acc[:, slot, P * j:P * j + P], ones[:, 0:1], start=True, stop=True,
                             skip_group_check=True)
                ins.then_inc(s.ada_summed, 1)

            def ada_now():
                a = ada_next[0] - 1
                ada_next[0] += 1
                if a < 0:
                    return
                if a == 9:
                    pe.wait_ge(s.mod_read, 1)
                ada_sum(a, a % 2, lambda j: slice(2 * a + j, 2 * a + j + 1))

            pe.wait_ge(s.ones_ready, 1)
            pe.wait_ge(s.csil_ready, 2)

            def mod0_turn(q):
                pe.wait_ge(s.mod0_row, q + 1)
                if q == 0:
                    pe.wait_ge(s.ident2_in, 16)
                for j in range(4):
                    t = 4 * q + j
                    ins = mm(bank[4][:, 2 * t:2 * t + 2], m0row[:, P * t:P * t + P], ident2[:, :], start=True,
                             stop=True, skip_group_check=True)
                ins.then_inc(s.mod0_done, 1)

            for c in range(ADA_FIRST):
                pe.wait_ge(adaf_in[c], 16)
                for k in range(KT):
                    ins = mm(bank[c // 2][0:2, 256 * (c % 2):256 * (c % 2) + 256], csil[:, k, :],
                             adaf[:, c, 256 * k:256 * k + 256], start=(k == 0), stop=(k == KT - 1))
                ins.then_inc(s.mod0_sum, 1)
                if c == 0:
                    pe.wait_ge(s.csq_used, KT - 1)
                    mm(bank[6][:, 0:LC], ones[:, :], csqacc[:, :], start=True, stop=True).then_inc(s.cstat_done, 1)
                if c == 2:
                    pe.wait_ge(s.xsq0_used, KT - 1)
                    mm(bank[5][:, :], ones[:, :], sqacc[:, :], start=True, stop=True).then_inc(s.xstat_done, 1)
                if c >= 3 and c % 2:
                    mod0_turn(c // 2 - 1)
            mod0_turn(3)

            have(0)
            for p in range(2):
                slot, c = 0, 2 * p
                have(c)
                if p == 0:
                    project_pair(slot, hH, hL, ALL, (s.h_lo, 0), 4)
                else:
                    for n in range(2):
                        pe.wait_ge(s.v_read, n + 1)
                        project(bank[n][:, :], slot, n, hH, hL, ALL).then_inc(s.mm_done, step(n, 4))

                def states(q):
                    pe.wait_ge(s.kc_lo, 2 * q + 2)
                    pe.wait_ge(s.vc_lo, q + 1)
                    for d in range(2):
                        for h in range(2):
                            at = slice(P * (2 * d + h), P * (2 * d + h) + P)
                            hs = slice(P * h, P * h + P)
                            for tt in range(TC):
                                ins = mm3(bank[3][:, at], kcH[:, tt, d, hs], kcL[:, tt, d, hs], vcH[:, tt, hs],
                                          vcL[:, tt, hs], tt == 0, tt == TC - 1, True)
                    ins.then_inc(s.state_done, 1)

                if p:
                    states(0)
                for tt in range(TC):
                    if p and tt == 0:
                        pe.wait_ge(s.vc_lo, 1)
                    if p and tt == 1:
                        pe.wait_ge(s.state_lo, 1)
                    if p == 0 and tt == 1:
                        pe.wait_ge(s.mod0_ready, 2)
                    for k in range(KT):
                        pe.wait_ge(s.hc_lo, k + 1)
                        wh, wl = wblock(slot, k, 0, 256)
                        ts = slice(P * tt, P * tt + P)
                        ins = mm3(bank[2 + tt][:, 0:256], hcH[:, k, ts], hcL[:, k, ts], wh, wl, k == 0, k == KT - 1)
                    ins.then_inc(s.mm_done, step(2 + tt, 4))
                ada_now()
                slot, c = 1, 2 * p + 1
                have(c)
                for b in range(3):
                    if b < 2:
                        pe.wait_ge(s.k_sum, 2 * p + b + 1)
                    else:
                        pe.wait_ge(s.kc_lo, 2 * p + 1)
                    for half in range(2):
                        hh, hl = (hH, hL) if b < 2 else (hcH, hcL)
                        tt = 2 * b + half if b < 2 else half
                        for k in range(KT):
                            wh, wl = wblock(slot, k, 0, 256)
                            ts = slice(P * tt, P * tt + P)
                            ins = mm3(bank[b][:, 256 * half:256 * half + 256], hh[:, k, ts], hl[:, k, ts], wh, wl,
                                      k == 0, k == KT - 1)
                    ins.then_inc(s.mm_done, step(b, 3))
                ada_now()
            for p in range(2):
                have(C_Q + p)
                for n in range(2):
                    if p:
                        pe.wait_ge(s.q_sum, n + 1)
                    else:
                        pe.wait_ge(s.v_read, 3 + n)
                    project(bank[n][:, :], p, n, hH, hL, ALL).then_inc(s.mm_done, step(n, 2))
                if p == 0:
                    pe.wait_ge(s.kc_lo, 4)
                    states(1)
                ada_now()
            def o_stat(h):
                pe.wait_ge(s.osq_ready, h + 1)
                if h:
                    pe.wait_ge(s.oroot_ready, h)
                mm(bank[1][:, :], ones[:, :], scratch[:, 1, :], start=True, stop=True).then_inc(s.ostat_done, 1)

            pe.wait_ge(s.state_lo, 2)
            for i in range(TT * HEADS + 2):
                if i < TT * HEADS:
                    h, j = divmod(i, TT)
                    if j == 0:
                        pe.wait_ge(s.q_lo, h + 1)
                    if i >= 2:
                        pe.wait_ge(s.a_mul, i - 1)
                    ks = slice(P * j, P * j + P)
                    mm3(bank[4 + i % 2][:, :], kH[:, h, ks], kL[:, h, ks], qH[:, h, :], qL[:, h, :], True, True)\
                        .then_inc(s.s_done, 1)
                if i >= 2:
                    h, j = divmod(i - 2, TT)
                    pe.wait_ge(s.a_mul, i - 1)
                    if j == 0 and h >= 2:
                        pe.wait_ge(s.o_sum, h - 1)
                    hs = slice(P * h, P * h + P)
                    mm(bank[6 if h % 2 == 0 else 0][:, :], vF[:, j, hs], aF[:, (i - 2) % 4, :], start=(j == 0),
                       stop=(j == TT - 1)).then_inc(s.pv_done, 1)
                if i < TT * HEADS and i % TT == 0:
                    h = i // TT
                    if h:
                        pe.wait_ge(s.cross_read, h)
                    for d in range(2):
                        ins = mm3(bank[2 + d][:, :], sH[:, d, h, :], sL[:, d, h, :], qH[:, h, :], qL[:, h, :],
                                  True, True)
                    ins.then_inc(s.cross_done, 1)
                if TT <= i < TT * HEADS and i % TT == 3:
                    o_stat(i // TT - 1)
            for p in range(2):
                have(C_F + p)
                for n in range(2):
                    if p:
                        pe.wait_ge(s.f_lo, n + 1)
                    else:
                        pe.wait_ge(s.cross_read, HEADS)
                    project(bank[2 + n][:, :], p, n, hH, hL, ALL).then_inc(s.mm_done, step(n, 2))
                    if p == n == 0:
                        o_stat(HEADS - 1)
                ada_now()
            have(C_DFT)
            pe.wait_ge(s.csd_lo, 1)
            pe.wait_ge(s.oroot_ready, HEADS)
            for g in range(GROUPS + 1):
                if g < GROUPS:
                    pe.wait_ge(s.f_lo, g + 1)
                    for n in range(2):
                        if g:
                            pe.wait_ge(s.fc_lo, 2 * (g - 1) + n + 1)
                        for half in range(2):
                            ts = slice(P * (2 * n + half), P * (2 * n + half) + P)
                            ins = mm3(bank[n][:, 256 * half:256 * half + 256], fH[:, g, ts], fL[:, g, ts],
                                      csdH[:, :], csdL[:, :], True, True)
                        ins.then_inc(s.fc_done, 1)
                if g:
                    pe.wait_ge(s.fc_lo, 2 * g)
                    for q, part in ((), ((0, 0), (0, 1)), ((1, 0), (1, 1)), ((2, 0),),
                                    ((3, 0), (2, 1), (3, 1)))[g]:
                        if part == 0 and q >= 2:
                            pe.wait_ge(s.mix_lo, q - 1)
                        if part:
                            have(C_DFT + 1)
                        for st in range(TT):
                            es = slice(P * part, P * part + P)
                            ss = slice(L * st, L * st + L)
                            ins = mm3(bank[4 + q % 2][:, :], fcH[:, q % 2, st, es], fcL[:, q % 2, st, es],
                                      WH[:, part, ss], WL[:, part, ss], part == st == 0,
                                      part == 1 and st == TT - 1)
                        if (q, part) == (3, 0):
                            ins.then_inc(s.mm_done, 14)
                        elif (q, part) == (3, 1):
                            ins.then_inc(s.mm_done, 15)
                        elif part:
                            ins.then_inc(s.mm_done, 1)
            for p in range(2):
                have(C_G + p)
                for n in range(2):
                    if p:
                        pe.wait_ge(s.g_silu, n + 1)
                    else:
                        pe.wait_ge(s.fc_lo, 2 * GROUPS)
                    project(bank[n][:, :], p, n, hH, hL, ALL).then_inc(s.mm_done, step(n, 2))
                ada_now()

            def out_stat(m):
                pe.wait_ge(s.ysq_used, 6 * m + 6)
                mm(bank[4][:, :], ones[:, :], sqacc[:, :], start=True, stop=False)
                pe.wait_ge(s.ysq_ready, (m + 1) * KT)
                mm(bank[4][:, :], ones[:, :], scratch[:, 1, :], start=False, stop=True).then_inc(s.ystat_done, 1)

            def x_stats(m):
                for k in range(KT):
                    pe.wait_ge(s.xsq_ready, (m - 1) * KT + k + 1)
                    mm(bank[5][:, :], ones[:, :], squares[k % 4], start=(k == 0), stop=(k == KT - 1))\
                        .then_inc(s.xsq_used, 1)

            def free(t):
                pe.wait_ge(s.bank_free, t - 3)

            def out_phase(m, c0, free0, src_h, src_l, ready, jobs=0, order=ALL):
                for p in range(4):
                    have(c0 + p)
                    for n in range(2):
                        t = 2 * p + n
                        if free0 + t >= 4:
                            free(free0 + t)
                        else:
                            pe.wait_ge(s.g_silu, 4)
                        if p:
                            project(bank[t % 4][:, :], p % 2, n, src_h, src_l, order).then_inc(s.mm_done, step(n, 2))
                    if p == 0:
                        project_pair(0, src_h, src_l, order, ready, 2)
                    for _ in range(jobs if p < 3 else 0):
                        ada_now()
                out_stat(m)
                for _ in range(jobs):
                    ada_now()
                if m < 3:
                    x_stats(m + 1)

            def down_phase(m, c0, free0, ready):
                for p in range(4):
                    for j in range(3):
                        c = c0 + 3 * p + j
                        have(c)
                        ks = [(k, 8 * j + k) for k in range(min(8, FT - 8 * j))]
                        for n in range(2):
                            t = 2 * p + n
                            if j == 0:
                                free(free0 + t)
                            ins = project(bank[t % 4][:, :], c % 2, n, GH, GL, ks, j == 0, j == 2,
                                          ready=(ready, 8 * j) if p == 0 and n == 0 else None)
                            if j == 2:
                                ins.then_inc(s.mm_done, step(n, 2))
                            elif n == 1:
                                ins.then_inc(s.mm_done, 16)
                        if m == 1:
                            a = JOBS_DOWN - 1 + 3 * p + j
                            pe.wait_ge(s.mod_read, 4)
                            ada_sum(a, (a + 1) % 2, lambda jj: slice(2 * a + jj, 2 * a + jj + 1))
                out_stat(m)
                if m < 3:
                    x_stats(m + 1)

            out_phase(0, C_OUT, B_OUT, mixH, mixL, (s.mix_lo, 0), 1, ALL[4:] + ALL[:4])
            with pe.Fori(0, FT // 2) as i:
                for j in range(2):
                    have(2 * i + (C_UP + j))
                    for x in range(2):
                        pe.wait_ge(s.bank_free, 4 * i + (B_UP + 2 * j + x - 3))
                        if j:
                            project(bank[2 + x][:, :], 1, x, hH, hL, ALL).then_inc(s.mm_done, step(x, 2))
                    if j == 0:
                        project_pair(0, hH, hL, ALL, (s.h_lo, KT), 2)
                    if j == 0:
                        pe.wait_ge(s.mod_read, 2)
                        ada_sum(i + (JOBS_UP - 1), 1, lambda jj: bass.ds(2 * i + (2 * JOBS_UP - 2 + jj), 1))
            down_phase(1, C_DOWN, B_DOWN, s.ffn_lo)
            for i in range(4):
                have(C_U + i)
                for x in range(2):
                    free(B_U + 2 * i + x)
                    if i:
                        project(bank[2 * (i % 2) + x][:, :], i % 2, x, hH, hL, ALL).then_inc(s.mm_done, step(x, 2))
                if i == 0:
                    project_pair(0, hH, hL, ALL, (s.h_lo, 2 * KT), 2)
                a = JOBS_DOWN + 11 + i
                ada_sum(a, (a + 1) % 2, lambda jj: slice(2 * a + jj, 2 * a + jj + 1))
            for c0, free0 in ((C_K2, B_K2), (C_V2, B_V2), (C_Q2, B_Q2)):
                for i in range(4):
                    c, n = c0 + i // 2, i % 2
                    if n == 0:
                        have(c)
                    free(free0 + i)
                    if c0 == C_V2:
                        for half in range(2):
                            for k in range(KT):
                                wh, wl = wblock(c % 2, k, 0, 256)
                                ts = slice(P * (2 * n + half), P * (2 * n + half) + P)
                                ins = mm3(bank[i][:, 256 * half:256 * half + 256], hH[:, k, ts], hL[:, k, ts], wh,
                                          wl, k == 0, k == KT - 1)
                    else:
                        ins = project(bank[i][:, :], c % 2, n, hH, hL, ALL)
                    ins.then_inc(s.mm_done, step(n, 2))
            for i in range(16):
                if i % 2 == 0:
                    have(C_GATES + i // 2)
                if i < 4:
                    free(B_MERGE + i)
                else:
                    pe.wait_ge(s.gate_sig, i - 3)
                project(bank[i % 4][:, :], (i // 2) % 2, i % 2, hH, hL, ALL).then_inc(s.mm_done, step(i % 2, 2))
                if i == 12:
                    pe.wait_ge(s.conv_tap, TAPS * CT)
                    for k in range(CT):
                        ins = mm(bank[6][:, :], ones[:, :], cacc[:, k, :], start=(k == 0), stop=(k == CT - 1))
                    ins.then_inc(s.lnsum_done, 1)
                if i == 14:
                    for k in range(CT):
                        pe.wait_ge(s.lnsq_ready, k + 1)
                        ins = mm(bank[5][:, :], ones[:, :], lnsq[:, k, :], start=(k == 0), stop=(k == CT - 1))
                    ins.then_inc(s.lnvar_done, 1)
            pe.wait_ge(s.mask_ready, 1)
            pe.wait_ge(s.bank_free, B_MERGE)
            pe.wait_ge(s.ln_center, 1)
            for i in range(-1, 4 * NH2 + 5):
                if i + 1 < 4 * NH2:
                    k = i + 1
                    h, x = divmod(k, 4)
                    j, w = 3 - x, P * (x + 1)
                    r = slice(64 * (h % 2), 64 * (h % 2) + 64)
                    if k < 4:
                        pe.wait_ge(s.gate_sig, 13 + k)
                    if k >= 6:
                        pe.wait_ge(s.at_exp, k - 5)
                    z = bank[Z_BANKS[k % 6]]
                    ks, qs = slice(P * j, P * j + P), slice(P * j, L)
                    mm3(z[:, 0:w], k2H[r, h // 2, ks], k2L[r, h // 2, ks], q2H[r, h // 2, qs], q2L[r, h // 2, qs],
                        True, False, True)
                    mm(z[:, 0:P], maskR[:, 0, :], maskR[:, 1, :], start=False, stop=True,
                       skip_group_check=True).then_inc(s.z_done, 1)
                if 0 <= i - 3 < 4 * NH2:
                    k = i - 3
                    x, slot = k % 4, k // 4 % 2
                    pe.wait_ge(s.sp_lo, k + 1)
                    for y in range(x + 1):
                        at, wy = SP_AT[y], P * (y + 1)
                        o = bank[Z_BANKS[k % 6]][:, P * (x - y):P * (x + 1)]
                        lhs = maskR[:, 2 if y == x else 3, :]
                        mm(o, lhs, spH[slot][:, at:at + wy], start=False, stop=False, skip_group_check=True)
                        ins = mm(o, lhs, spL[slot][:, at:at + wy], start=False, stop=(y == x), skip_group_check=True)
                    ins.then_inc(s.arg_done, 1)
                if i >= 5:
                    k = i - 5
                    h, x = divmod(k, 4)
                    pe.wait_ge(s.at_exp, k + 1)
                    if x == 0 and h >= 2:
                        pe.wait_ge(s.o2_lo, h - 1)
                    if x == 0 and h == 1:
                        pe.wait_ge(s.lnroot_ready, 1)
                    hs = slice(P * (h // 2), P * (h // 2) + P)
                    w = P * (x + 1)
                    mm(bank[4 + h % 2][:, L - w:L], v2F[:, 3 - x, hs], atF[:, k % 4, 0:w], start=(x == 0),
                       stop=(x == 3), skip_group_check=True).then_inc(s.pv2_done, 1)
            pe.wait_ge(s.at_exp, 4 * NH2)
            for p in range(4):
                have(C_MERGE + p)
                for x, y in ((0, 1), (1, 1), (0, 0), (1, 0)) if p == 0 else ((0, 1), (0, 0), (1, 1), (1, 0)):
                    if 2 * p + x >= 2:
                        free(B_MERGE + 4 * p + 2 * x + 1)
                    src = (cH, cL) if y == 0 else (q2H, q2L)
                    if p == 0 and x == 0:
                        pe.wait_ge(s.o2_lo, NH2) if y else pe.wait_ge(s.c_lo, CT)
                    ins = project(bank[2 * x + y][:, :], p % 2, x, *src, [(4 * y + k, k) for k in range(4)])
                    if y == 0:
                        ins.then_inc(s.mm_done, step(x, 2))
            out_phase(2, C_O, B_O, mgH, mgL, (s.mg_lo, 0))
            with pe.Fori(0, FT // 2) as i:
                for j in range(2):
                    have(2 * i + (C_UP2 + j))
                    for x in range(2):
                        pe.wait_ge(s.bank_free, 4 * i + (B_UP2 + 2 * j + x - 3))
                        if j:
                            project(bank[2 + x][:, :], 1, x, hH, hL, ALL).then_inc(s.mm_done, step(x, 2))
                    if j == 0:
                        project_pair(0, hH, hL, ALL, (s.h_lo, 3 * KT), 2)
            down_phase(3, C_DOWN2, B_DOWN2, s.ffn2_lo)


def tiles(w, cols):
    k = w.shape[0] // P
    return np.concatenate([w[:, c].reshape(k, P, -1) for c in cols], axis=2).transpose(1, 0, 2)


def col(i, width=P):
    return slice(i * width, (i + 1) * width)


def weight_stream(w_in, w_out, w_up, w_down, w_in2, w_conv, w_att, w_o, w_ffn_in, w_ffn_out, dft):
    out = np.zeros((N_CHUNKS, P, CH), np.float32)

    def put(c, w, cols, at=0):
        t = tiles(w, cols)
        out[c, :, at:at + t.shape[1] * 256] = t.reshape(P, -1)

    for p in range(2):
        put(2 * p, w_in, [col(2 + p, 256)])
        put(2 * p + 1, w_in, [col(4 + p, 256)])
        put(C_Q + p, w_in, [col(p, 256)])
        put(C_F + p, w_in, [col(8 + p, 256)])
        out[C_DFT + p] = dft[p].reshape(TT, P, L).transpose(1, 0, 2).reshape(P, -1)
        put(C_G + p, w_in, [col(6 + p, 256)])
    for p in range(4):
        put(C_OUT + p, w_out, [col(p, 256)])
        put(C_MERGE + p, w_conv, [col(p, 256)])
        put(C_MERGE + p, w_att, [col(p, 256)], CH // 2)
        put(C_O + p, w_o, [col(p, 256)])
        put(C_U + p, w_in2, [col(p), col(4 + p)])
        for j in range(3):
            rows = slice(8 * j * P, min(8 * j + 8, FT) * P)
            put(C_DOWN + 3 * p + j, w_down[rows], [col(p, 256)])
            put(C_DOWN2 + 3 * p + j, w_ffn_out[rows], [col(p, 256)])
    for t in range(FT):
        put(C_UP + t, w_up, [col(t), col(FT + t)])
        put(C_UP2 + t, w_ffn_in, [col(t), col(FT + t)])
    for p in range(2):
        put(C_Q2 + p, w_in2, [col(4 + p, 256)])
        put(C_K2 + p, w_in2, [col(6 + p, 256)])
        put(C_V2 + p, w_in2, [col(8 + p, 256)])
    for p in range(8):
        put(C_GATES + p, w_in2, [col(10 + p, 256)])
    return out


def tables():
    f32 = np.float32
    n_freq = HD // 4
    freqs = (f32(10000.0) ** (-np.arange(n_freq, dtype=f32) / f32(n_freq))).astype(f32)
    t = np.arange(L)
    ang = np.concatenate([(t // ROW).astype(f32)[:, None] * freqs, (t % ROW).astype(f32)[:, None] * freqs], 1)
    cos, sin = np.cos(ang).T, np.sin(ang).T
    rope = np.stack([np.concatenate([cos, cos]), np.concatenate([-sin, sin])], 1).astype(f32)
    band = (np.arange(BAND)[None, :] - np.arange(P)[:, None] - (TT - 1) * P).astype(f32)
    pos = np.broadcast_to(np.arange(1, L + 1, dtype=f32), (P, L)).copy()
    e = np.outer(np.arange(P), np.arange(P)) % P * (2 * np.pi / P)
    csd = (np.concatenate([np.cos(e), np.sin(e)], 1) / 256.0).astype(f32)
    a = np.outer(np.arange(L), np.arange(L)) % L * (2 * np.pi / L)
    dft = np.stack([np.cos(a), -np.sin(a)]).astype(f32)
    key, query = np.arange(P)[:, None], np.arange(P)[None, :]
    masks = np.stack([np.eye(P), np.where(key >= query, NEG, 0.0), np.where(key >= query, -1.0, 0.0),
                      -np.ones((P, P))], 1).astype(f32)
    return rope, band, pos, csd, dft, masks


def kernel(x, c, ctx, c_ctx, w_ada, b_ada, g_mix_pre, g_mix_post, g_ffn_pre, g_ffn_post, w_in,
           ret_decay_fwd, ret_decay_bwd, w_out, w_up, conv_w, conv_b, w_down, c_2, ada_w_2, ada_b_2,
           pre_mix_g_2, post_mix_g_2, pre_ffn_g_2, post_ffn_g_2, w_in_2, conv_w_2, conv_b_2,
           conv_ln_g_2, conv_ln_b_2, w_conv_out_2, w_att_out_2, w_o_2, w_ffn_in_2, w_ffn_out_2):
    import concourse.bacc as bacc
    from concourse.bass_utils import run_bass_kernel_spmd

    def vt(a):
        return np.asarray(a).reshape(-1, P).T

    def feature_major(a, n):
        return np.ascontiguousarray(np.asarray(a).reshape(n, KT, P).transpose(2, 1, 0))

    rope, band, pos, csd, dft, masks = tables()
    decays = np.concatenate([np.asarray(ret_decay_fwd)[0], np.asarray(ret_decay_bwd)[0]])
    m = np.arange(LC, dtype=np.float32).reshape(TC, P).T
    vecs = np.concatenate(
        [vt(c), vt(c_ctx), vt(c_2), vt(b_ada), vt(ada_b_2), vt(g_mix_pre), vt(g_mix_post), vt(g_ffn_pre),
         vt(g_ffn_post), vt(pre_mix_g_2), vt(post_mix_g_2), vt(pre_ffn_g_2), vt(post_ffn_g_2), vt(conv_w),
         vt(conv_b), vt(conv_w_2), vt(conv_b_2), vt(conv_ln_g_2), vt(conv_ln_b_2),
         np.broadcast_to(decays, (P, 2 * HEADS)), LC - 1 - m, m], axis=1)
    stream = weight_stream(*(np.asarray(w)[0] for w in (w_in, w_out, w_up, w_down, w_in_2, w_conv_out_2,
                                                        w_att_out_2, w_o_2, w_ffn_in_2, w_ffn_out_2)), dft)
    ada = np.stack([tiles(np.asarray(w)[0], [col(i, 256)]).reshape(P, CH) for w in (w_ada, ada_w_2)
                    for i in range(24)])
    arrays = {"weights": stream, "ada": ada, "x_t": feature_major(x, L), "ctx_t": feature_major(ctx, LC),
              "vecs": vecs, "rope": rope, "band": band, "pos": pos, "csd": csd, "masks": masks}
    arrays = {k: np.ascontiguousarray(a) for k, a in arrays.items()}
    nc = bacc.Bacc("TRN2", target_bir_lowering=False, num_devices=1, dynamic_dma_scratch_size=1024)
    args = {k: nc.dram_tensor(k, a.shape, mybir.dt.float32, kind="ExternalInput").ap() for k, a in arrays.items()}
    out = nc.dram_tensor("out_t", (P, KT, L), mybir.dt.float32, kind="ExternalOutput").ap()
    build(nc, out=out, **args)
    r = run_bass_kernel_spmd(nc, [arrays], core_ids=[0])
    return r.results[0]["out_t"].transpose(2, 1, 0).reshape(1, L, D)
```
